# Optimizing a Trainium2 kernel written in Bass

```python
import math
import jax
import jax.numpy as jnp
from jax import lax
import numpy as np
import jax, jax.numpy as jnp

D_MODEL = 1024
BATCH = 1
SEQ = 512
DEPTH = 1

GROUP_HEADS = 4
HEAD_DIM = 64
GROUP_WIDTH = GROUP_HEADS * HEAD_DIM
N_GROUPS = 4
D_MIX = N_GROUPS * GROUP_WIDTH
IN_SIZES = (GROUP_WIDTH, GROUP_WIDTH, GROUP_WIDTH, GROUP_WIDTH, GROUP_HEADS, GROUP_HEADS, GROUP_WIDTH, GROUP_WIDTH, GROUP_WIDTH, GROUP_WIDTH, GROUP_WIDTH, GROUP_WIDTH, GROUP_WIDTH, GROUP_WIDTH, GROUP_WIDTH, GROUP_WIDTH)
N_IN = sum(IN_SIZES)
MLSTM_F_OFFSET = 4 * GROUP_WIDTH + GROUP_HEADS
MLSTM_CHUNK = 64
HGRN_CHUNK = 64
SCONV_WIDTH = 3
MOBA_BLOCK = 256
MOBA_TOPK = 3
MOBA_QCHUNK = 32
REL_BUCKETS = 32
REL_MAX_DIST = 128
N_MEM = 256
CROSS_HEADS = 4
CROSS_HEAD_DIM = 128
CROSS_WIDTH = CROSS_HEADS * CROSS_HEAD_DIM
D_FF = 2816
FFN_CONV_WIDTH = 3
RMS_EPS = 1e-6
NEG_BIG = -1e30


def rmsnorm(x, gain):
    x32 = x.astype(jnp.float32)
    y = x32 * lax.rsqrt(jnp.mean(x32 * x32, axis=-1, keepdims=True) + RMS_EPS)
    return (y * gain.astype(jnp.float32)).astype(x.dtype)

def head_rmsnorm(h, gain):
    b, nh, s, d = h.shape
    h32 = h.astype(jnp.float32).transpose(0, 2, 1, 3)
    h32 = h32 * lax.rsqrt(jnp.mean(h32 * h32, axis=-1, keepdims=True) + RMS_EPS)
    return h32.reshape(b, s, nh * d) * gain.astype(jnp.float32)

def causal_dwconv(x, w):
    width, ch = w.shape
    return lax.conv_general_dilated(x, w.astype(x.dtype)[:, None, :], window_strides=(1,), padding=[(width - 1, 0)], dimension_numbers=('NWC', 'WIO', 'NWC'), feature_group_count=ch)

def to_heads(a, n_heads):
    b, s, _ = a.shape
    return a.reshape(b, s, n_heads, -1).transpose(0, 2, 1, 3)

def _chunks(a, size):
    b, h, s = a.shape[:3]
    return jnp.moveaxis(a.reshape(b, h, s // size, size, *a.shape[3:]), 2, 0)

def _unchunk(a):
    nc, b, h, l, d = a.shape
    return jnp.moveaxis(a, 0, 2).reshape(b, h, nc * l, d)

def rel_bucket(dist):
    n = jnp.maximum(dist, 0)
    exact = REL_BUCKETS // 2
    nf = jnp.maximum(n, 1).astype(jnp.float32)
    large = exact + (jnp.log(nf / exact) / math.log(REL_MAX_DIST / exact) * (REL_BUCKETS - exact)).astype(jnp.int32)
    large = jnp.minimum(large, REL_BUCKETS - 1)
    return jnp.where(n < exact, n, large)

def mlstm_chunkwise(q, k, v, i_pre, f_pre):
    b, nh, s, d = q.shape
    f32 = jnp.float32
    q = q.astype(f32)
    k = k.astype(f32) * (d ** -0.5)
    v = v.astype(f32)
    log_i = i_pre.astype(f32)
    log_f = jax.nn.log_sigmoid(f_pre.astype(f32))
    causal = jnp.tril(jnp.ones((MLSTM_CHUNK, MLSTM_CHUNK), dtype=bool))

    def step(carry, xs):
        c_mat, n_vec, m_prev = carry
        qc, kc, vc, lic, lfc = xs
        g = jnp.cumsum(lfc, axis=-1)
        dlog = jnp.where(causal, g[..., :, None] - g[..., None, :] + lic[..., None, :], NEG_BIG)
        a = g + m_prev[..., None]
        m_t = jnp.maximum(a, jnp.max(dlog, axis=-1))
        w = jnp.exp(dlog - m_t[..., None]) * jnp.einsum('bhtd,bhsd->bhts', qc, kc)
        inter = jnp.exp(a - m_t)
        num = jnp.einsum('bhts,bhsd->bhtd', w, vc) + inter[..., None] * jnp.einsum('bhvk,bhtk->bhtv', c_mat, qc)
        den = jnp.sum(w, axis=-1) + inter * jnp.einsum('bhk,bhtk->bht', n_vec, qc)
        h = num / jnp.maximum(jnp.abs(den), jnp.exp(-m_t))[..., None]
        g_last = g[..., -1]
        u = g_last[..., None] - g + lic
        m_new = jnp.maximum(g_last + m_prev, jnp.max(u, axis=-1))
        ws = jnp.exp(u - m_new[..., None])
        decay = jnp.exp(g_last + m_prev - m_new)
        c_new = decay[..., None, None] * c_mat + jnp.einsum('bhs,bhsv,bhsk->bhvk', ws, vc, kc)
        n_new = decay[..., None] * n_vec + jnp.einsum('bhs,bhsk->bhk', ws, kc)
        return (c_new, n_new, m_new), h

    init = (jnp.zeros((b, nh, d, d), f32), jnp.zeros((b, nh, d), f32), jnp.zeros((b, nh), f32))
    _, hs = lax.scan(step, init, tuple(_chunks(a, MLSTM_CHUNK) for a in (q, k, v, log_i, log_f)))
    return _unchunk(hs)

def hgrn2_chunkwise(q, k, log_f, v):
    b, nh, s, dk = q.shape
    dv = v.shape[-1]
    causal = jnp.tril(jnp.ones((HGRN_CHUNK, HGRN_CHUNK), dtype=bool))[:, :, None]

    def step(state, xs):
        qc, kc, lfc, vc = xs
        g = jnp.cumsum(lfc, axis=2)
        rel = jnp.exp(jnp.where(causal, g[:, :, :, None, :] - g[:, :, None, :, :], NEG_BIG))
        attn = jnp.einsum('bhtk,bhtsk,bhsk->bhts', qc, rel, kc)
        out = jnp.einsum('bhts,bhsv->bhtv', attn, vc) + jnp.einsum('bhtk,bhkv->bhtv', qc * jnp.exp(g), state)
        g_last = g[:, :, -1:, :]
        new_state = jnp.exp(g_last[:, :, 0, :])[..., None] * state + jnp.einsum('bhsk,bhsv->bhkv', kc * jnp.exp(g_last - g), vc)
        return new_state, out

    init = jnp.zeros((b, nh, dk, dv), jnp.float32)
    _, outs = lax.scan(step, init, tuple(_chunks(a, HGRN_CHUNK) for a in (q, k, log_f, v)))
    return _unchunk(outs)

def moba_attention(q, k, v, rel_bias):
    b, nh, s, d = q.shape
    f32 = jnp.float32
    nb = -(-s // MOBA_BLOCK)
    s_pad = nb * MOBA_BLOCK
    padw = ((0, 0), (0, 0), (0, s_pad - s), (0, 0))
    q, k, v = jnp.pad(q, padw), jnp.pad(k, padw), jnp.pad(v, padw)
    kb = k.reshape(b, nh, nb, MOBA_BLOCK, d)
    vb = v.reshape(b, nh, nb, MOBA_BLOCK, d)
    n_sel = min(MOBA_TOPK, nb - 1)
    scale = d ** -0.5
    bias_t = rel_bias.astype(f32).T
    blk_of = jnp.arange(s_pad, dtype=jnp.int32) // MOBA_BLOCK
    if n_sel > 0:
        kmean = jnp.mean(kb.astype(f32), axis=3)
        gate = jnp.einsum('bhsd,bhnd->bhsn', q.astype(f32), kmean)
        past = jnp.arange(nb, dtype=jnp.int32)[None, :] < blk_of[:, None]
        gate = jnp.where(past, gate, NEG_BIG)
        _, sel = lax.top_k(gate, n_sel)
        sel = sel.astype(jnp.int32)
        sel_valid = sel < blk_of[:, None]
    b_ix = jnp.arange(b)[:, None, None, None]
    h_ix = jnp.arange(nh)[None, :, None, None]
    key_off = jnp.arange(MOBA_BLOCK, dtype=jnp.int32)

    def attend_chunk(c):
        start = c * MOBA_QCHUNK
        qc = lax.dynamic_slice_in_dim(q, start, MOBA_QCHUNK, axis=2)
        t = start + jnp.arange(MOBA_QCHUNK, dtype=jnp.int32)
        j = start // MOBA_BLOCK
        k_own = lax.dynamic_index_in_dim(kb, j, axis=2, keepdims=False)
        v_own = lax.dynamic_index_in_dim(vb, j, axis=2, keepdims=False)
        dist_own = t[:, None] - (j * MOBA_BLOCK + key_off)[None, :]
        s_own = jnp.einsum('bhqd,bhkd->bhqk', qc, k_own).astype(f32) * scale + bias_t[:, rel_bucket(dist_own)][None]
        s_own = jnp.where(dist_own >= 0, s_own, NEG_BIG)
        if n_sel == 0:
            p = jax.nn.softmax(s_own, axis=-1)
            out = jnp.einsum('bhqk,bhkd->bhqd', p, v_own.astype(f32))
        else:
            sel_c = lax.dynamic_slice_in_dim(sel, start, MOBA_QCHUNK, axis=2)
            valid_c = lax.dynamic_slice_in_dim(sel_valid, start, MOBA_QCHUNK, axis=2)
            k_sel = kb[b_ix, h_ix, sel_c]
            v_sel = vb[b_ix, h_ix, sel_c]
            dist = t[None, None, :, None, None] - (sel_c[..., None] * MOBA_BLOCK + key_off)
            bias = bias_t[h_ix[..., None], rel_bucket(dist)]
            s_past = jnp.einsum('bhqd,bhqnkd->bhqnk', qc, k_sel).astype(f32) * scale + bias
            s_past = jnp.where(valid_c[..., None], s_past, NEG_BIG)
            n_past = n_sel * MOBA_BLOCK
            p = jax.nn.softmax(jnp.concatenate([s_past.reshape(b, nh, MOBA_QCHUNK, n_past), s_own], axis=-1), axis=-1)
            p_past = p[..., :n_past].reshape(b, nh, MOBA_QCHUNK, n_sel, MOBA_BLOCK)
            out = jnp.einsum('bhqnk,bhqnkd->bhqd', p_past, v_sel.astype(f32)) + jnp.einsum('bhqk,bhkd->bhqd', p[..., n_past:], v_own.astype(f32))
        return out.astype(q.dtype)

    outs = lax.map(attend_chunk, jnp.arange(s_pad // MOBA_QCHUNK, dtype=jnp.int32))
    return _unchunk(outs)[:, :, :s]

def token_mixer(xn, w_in, b_in, mlstm_norm, sconv_w, rel_bias, hgrn_lb, hgrn_norm, w_out):
    b, s, _ = xn.shape
    f32 = jnp.float32
    dt = xn.dtype
    proj = xn @ w_in + b_in
    splits = np.cumsum(IN_SIZES)[:-1].tolist()
    (m_q, m_k, m_v, m_o, m_i, m_f, c_b, c_c, c_h, a_q, a_k, a_v, h_q, h_f, h_i, h_g) = jnp.split(proj, splits, axis=-1)
    h_m = mlstm_chunkwise(to_heads(m_q, GROUP_HEADS), to_heads(m_k, GROUP_HEADS), to_heads(m_v, GROUP_HEADS), m_i.transpose(0, 2, 1), m_f.transpose(0, 2, 1))
    y_m = head_rmsnorm(h_m, mlstm_norm) * jax.nn.sigmoid(m_o.astype(f32))
    y_c = c_b * causal_dwconv(c_c * c_h, sconv_w)
    y_a = moba_attention(to_heads(a_q, GROUP_HEADS), to_heads(a_k, GROUP_HEADS), to_heads(a_v, GROUP_HEADS), rel_bias)
    y_a = y_a.transpose(0, 2, 1, 3).reshape(b, s, GROUP_WIDTH)
    lb = hgrn_lb.astype(f32).reshape(1, GROUP_HEADS, 1, HEAD_DIM)
    z = to_heads(h_f, GROUP_HEADS).astype(f32)
    f_gate = lb + (1.0 - lb) * jax.nn.sigmoid(z)
    log_f = jnp.log(f_gate)
    k_h = 1.0 - f_gate
    q_h = jax.nn.silu(to_heads(h_q, GROUP_HEADS).astype(f32))
    o_h = hgrn2_chunkwise(q_h, k_h, log_f, to_heads(h_i, GROUP_HEADS).astype(f32))
    y_h = head_rmsnorm(o_h, hgrn_norm) * jax.nn.silu(h_g.astype(f32))
    y = jnp.concatenate([y_m.astype(dt), y_c.astype(dt), y_a.astype(dt), y_h.astype(dt)], axis=-1)
    return y @ w_out

def memory_cross_attention(xn, memn, wq, wk, wv, wo):
    b, s, _ = xn.shape
    m = memn.shape[1]
    q = (xn @ wq).reshape(b, s, CROSS_HEADS, CROSS_HEAD_DIM)
    k = (memn @ wk).reshape(b, m, CROSS_HEADS, CROSS_HEAD_DIM)
    v = (memn @ wv).reshape(b, m, CROSS_HEADS, CROSS_HEAD_DIM)
    logits = jnp.einsum('bshd,bmhd->bhsm', q, k).astype(jnp.float32) * (CROSS_HEAD_DIM ** -0.5)
    p = jax.nn.softmax(logits, axis=-1)
    o = jnp.einsum('bhsm,bmhd->bshd', p, v.astype(jnp.float32)).astype(xn.dtype).reshape(b, s, CROSS_WIDTH)
    return o @ wo

def conv_glu_ffn(xn, w_up, conv_w, conv_b, w_down):
    gu = xn @ w_up
    gate, up = jnp.split(gu, 2, axis=-1)
    gate = causal_dwconv(gate, conv_w) + conv_b.astype(gate.dtype)
    return (jax.nn.silu(gate) * up) @ w_down

def first_inputs(seed: int = 0) -> dict:
    key = jax.random.key(seed)
    ks = jax.random.split(key, 26)
    f32 = jnp.float32

    def nrm(k, shape, scale):
        return scale * jax.random.normal(k, shape, f32)

    def gain(k, shape):
        return 1.0 + 0.05 * jax.random.normal(k, shape, f32)

    b_in = nrm(ks[3], (DEPTH, N_IN), 0.01)
    b_in = b_in.at[:, MLSTM_F_OFFSET:MLSTM_F_OFFSET + GROUP_HEADS].add(jnp.linspace(3.0, 6.0, GROUP_HEADS))
    return {
        'x': nrm(ks[0], (BATCH, SEQ, D_MODEL), 1.0),
        'mem': nrm(ks[1], (BATCH, N_MEM, D_MODEL), 1.0),
        'w_in': nrm(ks[2], (DEPTH, D_MODEL, N_IN), D_MODEL ** -0.5),
        'b_in': b_in,
        'mlstm_norm': gain(ks[4], (DEPTH, GROUP_WIDTH)),
        'sconv_w': nrm(ks[5], (DEPTH, SCONV_WIDTH, GROUP_WIDTH), SCONV_WIDTH ** -0.5),
        'rel_bias': nrm(ks[6], (REL_BUCKETS, GROUP_HEADS), 0.5),
        'hgrn_lb_logits': nrm(ks[7], (DEPTH, GROUP_WIDTH), 0.5),
        'hgrn_norm': gain(ks[8], (DEPTH, GROUP_WIDTH)),
        'w_mix_out': nrm(ks[9], (DEPTH, D_MIX, D_MODEL), D_MIX ** -0.5),
        'norm_mix_pre': gain(ks[10], (DEPTH, D_MODEL)),
        'norm_mix_post': gain(ks[11], (DEPTH, D_MODEL)),
        'mem_norm': gain(ks[12], (DEPTH, D_MODEL)),
        'w_cq': nrm(ks[13], (DEPTH, D_MODEL, CROSS_WIDTH), D_MODEL ** -0.5),
        'w_ck': nrm(ks[14], (DEPTH, D_MODEL, CROSS_WIDTH), D_MODEL ** -0.5),
        'w_cv': nrm(ks[15], (DEPTH, D_MODEL, CROSS_WIDTH), D_MODEL ** -0.5),
        'w_co': nrm(ks[16], (DEPTH, CROSS_WIDTH, D_MODEL), CROSS_WIDTH ** -0.5),
        'norm_cross_pre': gain(ks[17], (DEPTH, D_MODEL)),
        'norm_cross_post': gain(ks[18], (DEPTH, D_MODEL)),
        'w_ffn_in': nrm(ks[19], (DEPTH, D_MODEL, 2 * D_FF), D_MODEL ** -0.5),
        'ffn_conv_w': nrm(ks[20], (DEPTH, FFN_CONV_WIDTH, D_FF), FFN_CONV_WIDTH ** -0.5),
        'ffn_conv_b': nrm(ks[21], (DEPTH, D_FF), 0.01),
        'w_ffn_out': nrm(ks[22], (DEPTH, D_FF, D_MODEL), D_FF ** -0.5),
        'norm_ffn_pre': gain(ks[23], (DEPTH, D_MODEL)),
        'norm_ffn_post': gain(ks[24], (DEPTH, D_MODEL)),
    }

def first_block(x, mem, w_in, b_in, mlstm_norm, sconv_w, rel_bias, hgrn_lb_logits, hgrn_norm, w_mix_out, norm_mix_pre, norm_mix_post, mem_norm, w_cq, w_ck, w_cv, w_co, norm_cross_pre, norm_cross_post, w_ffn_in, ffn_conv_w, ffn_conv_b, w_ffn_out, norm_ffn_pre, norm_ffn_post):
    lb_soft = jax.nn.softmax(hgrn_lb_logits.astype(jnp.float32), axis=0)
    lb_all = jnp.cumsum(lb_soft, axis=0) - lb_soft[0]
    for l in range(DEPTH):
        h = token_mixer(rmsnorm(x, norm_mix_pre[l]), w_in[l], b_in[l], mlstm_norm[l], sconv_w[l], rel_bias, lb_all[l], hgrn_norm[l], w_mix_out[l])
        x = x + rmsnorm(h, norm_mix_post[l])
        h = memory_cross_attention(rmsnorm(x, norm_cross_pre[l]), rmsnorm(mem, mem_norm[l]), w_cq[l], w_ck[l], w_cv[l], w_co[l])
        x = x + rmsnorm(h, norm_cross_post[l])
        h = conv_glu_ffn(rmsnorm(x, norm_ffn_pre[l]), w_ffn_in[l], ffn_conv_w[l], ffn_conv_b[l], w_ffn_out[l])
        x = x + rmsnorm(h, norm_ffn_post[l])
    return x


DEPTH_2 = 2

A_Q_HEADS = 8
A_KV_HEADS = 2
A_GROUP = A_Q_HEADS // A_KV_HEADS
A_WINDOW = 128
A_BLOCK = 128
B_HEADS = 8
GRID_W = 64
NA_KH = 8
NA_KW = 16
RET_HEADS = 8
RET_DK = D_MODEL // RET_HEADS
RET_DV = 2 * D_MODEL // RET_HEADS
RET_CHUNK = 128
D_FF_2 = 4 * D_MODEL
N_EVEN = (DEPTH_2 + 1) // 2
N_ODD = DEPTH_2 // 2
EVEN_SPLITS = (A_Q_HEADS * HEAD_DIM, A_KV_HEADS * HEAD_DIM, A_KV_HEADS * HEAD_DIM,
               B_HEADS * HEAD_DIM, B_HEADS * HEAD_DIM, B_HEADS * HEAD_DIM)
EVEN_IN = sum(EVEN_SPLITS)
EVEN_MIX = (A_Q_HEADS + B_HEADS) * HEAD_DIM
ODD_SPLITS = (RET_HEADS * RET_DK, RET_HEADS * RET_DK, RET_HEADS * RET_DV, RET_HEADS * RET_DV)
ODD_IN = sum(ODD_SPLITS)
ODD_MIX = RET_HEADS * RET_DV
GN_EPS = 1e-5


def _split(t, sizes):
    idx = np.cumsum(sizes)[:-1].tolist()
    return jnp.split(t, idx, axis=-1)

def _rmsnorm(x, g):
    xf = x.astype(jnp.float32)
    y = xf * lax.rsqrt(jnp.mean(xf * xf, axis=-1, keepdims=True) + RMS_EPS)
    return (y * g.astype(jnp.float32)).astype(x.dtype)

def _alibi_slopes(n):
    return 2.0 ** (-(8.0 / n) * (jnp.arange(n, dtype=jnp.float32) + 1.0))

def _window_gqa(q, k, v, sink):
    B, S = q.shape[0], q.shape[1]
    nb = S // A_BLOCK
    qb = q.reshape(B, nb, A_BLOCK, A_KV_HEADS, A_GROUP, HEAD_DIM)
    pad = ((0, 0), (A_BLOCK, A_BLOCK), (0, 0), (0, 0))
    kp = jnp.pad(k, pad).reshape(B, nb + 2, A_BLOCK, A_KV_HEADS, HEAD_DIM)
    vp = jnp.pad(v, pad).reshape(B, nb + 2, A_BLOCK, A_KV_HEADS, HEAD_DIM)
    kb = jnp.concatenate([kp[:, :-2], kp[:, 1:-1], kp[:, 2:]], axis=2)
    vb = jnp.concatenate([vp[:, :-2], vp[:, 1:-1], vp[:, 2:]], axis=2)
    s = jnp.einsum('bnqhgd,bnkhd->bnhgqk', qb, kb).astype(jnp.float32) * (HEAD_DIM ** -0.5)
    qi = jnp.arange(A_BLOCK)[:, None]
    kj = jnp.arange(3 * A_BLOCK)[None, :]
    rel = kj - A_BLOCK - qi
    kpos = jnp.arange(nb)[:, None, None] * A_BLOCK + kj[None] - A_BLOCK
    valid = (jnp.abs(rel) <= A_WINDOW)[None] & (kpos >= 0) & (kpos < S)
    slopes = _alibi_slopes(A_Q_HEADS).reshape(A_KV_HEADS, A_GROUP, 1, 1)
    s = s - slopes * jnp.abs(rel).astype(jnp.float32)
    s = jnp.where(valid[None, :, None, None], s, -jnp.inf)
    sk = sink.astype(jnp.float32).reshape(A_KV_HEADS, A_GROUP)[None, None, :, :, None, None]
    m = jnp.maximum(jnp.max(s, axis=-1, keepdims=True), sk)
    p = jnp.exp(s - m)
    p = p / (jnp.sum(p, axis=-1, keepdims=True) + jnp.exp(sk - m))
    o = jnp.einsum('bnhgqk,bnkhd->bnqhgd', p.astype(v.dtype), vb)
    return o.reshape(B, S, A_Q_HEADS * HEAD_DIM)

def _neighbourhood_attn(q, k, v, rpb):
    B, S = q.shape[0], q.shape[1]
    rows = S // GRID_W
    kh = min(NA_KH, rows)
    kw = NA_KW
    qg = q.reshape(B, rows, GRID_W, B_HEADS, HEAD_DIM)
    kg = k.reshape(B, rows, GRID_W, B_HEADS, HEAD_DIM)
    vg = v.reshape(B, rows, GRID_W, B_HEADS, HEAD_DIM)
    qc = jnp.arange(GRID_W)
    cstart = jnp.clip(qc - kw // 2, 0, GRID_W - kw)
    kc = jnp.arange(GRID_W)
    col_valid = (kc[None, :] >= cstart[:, None]) & (kc[None, :] < cstart[:, None] + kw)
    col_idx = jnp.clip(kc[None, :] - qc[:, None] + NA_KW - 1, 0, 2 * NA_KW - 2)
    rpb_f = rpb.astype(jnp.float32)
    scale = HEAD_DIM ** -0.5

    def row_fn(r):
        rstart = jnp.clip(r - kh // 2, 0, rows - kh)
        qr = lax.dynamic_index_in_dim(qg, r, axis=1, keepdims=False)
        kr = lax.dynamic_slice_in_dim(kg, rstart, kh, axis=1)
        vr = lax.dynamic_slice_in_dim(vg, rstart, kh, axis=1)
        s = jnp.einsum('bqhd,brkhd->bhqrk', qr, kr).astype(jnp.float32) * scale
        row_idx = rstart + jnp.arange(kh) - r + NA_KH - 1
        bias = rpb_f[:, row_idx[None, :, None], col_idx[:, None, :]]
        s = jnp.where(col_valid[:, None, :], s + bias, -jnp.inf)
        p = jax.nn.softmax(s.reshape(B, B_HEADS, GRID_W, kh * GRID_W), axis=-1)
        p = p.reshape(B, B_HEADS, GRID_W, kh, GRID_W).astype(v.dtype)
        return jnp.einsum('bhqrk,brkhd->bqhd', p, vr)

    out = lax.map(row_fn, jnp.arange(rows))
    return out.transpose(1, 0, 2, 3, 4).reshape(B, S, B_HEADS * HEAD_DIM)

def _retention_dir(q, k, v, log_gamma, strict):
    B, S, H, dk = q.shape
    dv = v.shape[-1]
    nc = S // RET_CHUNK
    dt = q.dtype

    def chunks(t):
        return t.reshape(B, nc, RET_CHUNK, H, t.shape[-1]).transpose(1, 0, 3, 2, 4)

    lg = log_gamma[:, None]
    pos = jnp.arange(RET_CHUNK, dtype=jnp.float32)
    diff = pos[:, None] - pos[None, :]
    allowed = (diff > 0) if strict else (diff >= 0)
    dmask = jnp.where(allowed[None], jnp.exp(lg[:, :, None] * jnp.maximum(diff, 0.0)[None]), 0.0).astype(dt)
    cross = jnp.exp(lg * (pos + 1.0)).astype(dt)
    zeta = jnp.exp(lg * (RET_CHUNK - 1.0 - pos)).astype(dt)
    chunk_decay = jnp.exp(log_gamma * RET_CHUNK).astype(dt)

    def step(R, inp):
        qc, kc, vc = inp
        a = jnp.einsum('bhid,bhjd->bhij', qc, kc) * dmask
        o = jnp.einsum('bhij,bhjv->bhiv', a, vc) + jnp.einsum('bhid,bhdv->bhiv', qc, R) * cross[:, :, None]
        R = R * chunk_decay[:, None, None] + jnp.einsum('bhjd,bhjv->bhdv', kc * zeta[:, :, None], vc)
        return R, o

    R0 = jnp.zeros((B, H, dk, dv), dt)
    _, o = lax.scan(step, R0, (chunks(q), chunks(k), chunks(v)))
    return o.transpose(1, 0, 3, 2, 4).reshape(B, S, H, dv)

def _even_mixer(x, norm_g, w_in, qn_a, kn_a, sink_a, qn_b, kn_b, rpb_b, w_out):
    B, S, _ = x.shape
    h = _rmsnorm(x, norm_g)
    qa, ka, va, qb, kb, vb = _split(h @ w_in, EVEN_SPLITS)
    qa = _rmsnorm(qa.reshape(B, S, A_KV_HEADS, A_GROUP, HEAD_DIM), qn_a)
    ka = _rmsnorm(ka.reshape(B, S, A_KV_HEADS, HEAD_DIM), kn_a)
    va = va.reshape(B, S, A_KV_HEADS, HEAD_DIM)
    oa = _window_gqa(qa, ka, va, sink_a)
    qb = _rmsnorm(qb.reshape(B, S, B_HEADS, HEAD_DIM), qn_b)
    kb = _rmsnorm(kb.reshape(B, S, B_HEADS, HEAD_DIM), kn_b)
    vb = vb.reshape(B, S, B_HEADS, HEAD_DIM)
    ob = _neighbourhood_attn(qb, kb, vb, rpb_b)
    return jnp.concatenate([oa, ob], axis=-1) @ w_out

def _odd_mixer(x, norm_g, w_in, dec_f, dec_b, gn_g, w_out):
    B, S, _ = x.shape
    h = _rmsnorm(x, norm_g)
    q, k, v, g = _split(h @ w_in, ODD_SPLITS)
    q = q.reshape(B, S, RET_HEADS, RET_DK)
    k = k.reshape(B, S, RET_HEADS, RET_DK) * (RET_DK ** -0.5)
    v = v.reshape(B, S, RET_HEADS, RET_DV)
    lgf = jax.nn.log_sigmoid(dec_f.astype(jnp.float32))
    lgb = jax.nn.log_sigmoid(dec_b.astype(jnp.float32))
    y_f = _retention_dir(q, k, v, lgf, False)
    y_b = jnp.flip(_retention_dir(jnp.flip(q, 1), jnp.flip(k, 1), jnp.flip(v, 1), lgb, True), 1)
    yf = (y_f + y_b).astype(jnp.float32)
    mu = jnp.mean(yf, axis=-1, keepdims=True)
    var = jnp.mean(jnp.square(yf - mu), axis=-1, keepdims=True)
    yn = (yf - mu) * lax.rsqrt(var + GN_EPS) * gn_g.astype(jnp.float32).reshape(RET_HEADS, RET_DV)
    yn = yn.astype(x.dtype).reshape(B, S, ODD_MIX)
    return (jax.nn.silu(g) * yn) @ w_out

def _mlp(x, norm_g, w1, w2):
    h = _rmsnorm(x, norm_g)
    return jnp.square(jax.nn.relu(h @ w1)) @ w2

def second_inputs(seed: int = 0) -> dict:
    key = jax.random.key(seed)
    ks = jax.random.split(key, 20)
    f32 = jnp.float32

    def nrm(k, shape, scale):
        return jax.random.normal(k, shape, f32) * scale

    def gain(k, shape):
        return 1.0 + 0.02 * jax.random.normal(k, shape, f32)

    hr = jnp.arange(RET_HEADS, dtype=f32)
    gamma = 1.0 - 2.0 ** (-5.0 - hr)
    base_logit = jnp.log(gamma) - jnp.log1p(-gamma)
    return {
        'x': nrm(ks[0], (BATCH, SEQ, D_MODEL), 1.0),
        'attn_norm_e': gain(ks[1], (N_EVEN, D_MODEL)),
        'w_in_e': nrm(ks[2], (N_EVEN, D_MODEL, EVEN_IN), D_MODEL ** -0.5),
        'q_norm_a': gain(ks[3], (N_EVEN, HEAD_DIM)),
        'k_norm_a': gain(ks[4], (N_EVEN, HEAD_DIM)),
        'sink_a': nrm(ks[5], (N_EVEN, A_Q_HEADS), 0.5),
        'q_norm_b': gain(ks[6], (N_EVEN, HEAD_DIM)),
        'k_norm_b': gain(ks[7], (N_EVEN, HEAD_DIM)),
        'rpb_b': nrm(ks[8], (N_EVEN, B_HEADS, 2 * NA_KH - 1, 2 * NA_KW - 1), 0.02),
        'w_out_e': nrm(ks[9], (N_EVEN, EVEN_MIX, D_MODEL), EVEN_MIX ** -0.5),
        'ret_norm_o': gain(ks[10], (N_ODD, D_MODEL)),
        'w_in_o': nrm(ks[11], (N_ODD, D_MODEL, ODD_IN), D_MODEL ** -0.5),
        'decay_fwd_o': base_logit[None] + nrm(ks[12], (N_ODD, RET_HEADS), 0.05),
        'decay_bwd_o': base_logit[None] + nrm(ks[13], (N_ODD, RET_HEADS), 0.05),
        'ret_gn_o': gain(ks[14], (N_ODD, ODD_MIX)),
        'w_out_o': nrm(ks[15], (N_ODD, ODD_MIX, D_MODEL), ODD_MIX ** -0.5),
        'mlp_norm': gain(ks[16], (DEPTH_2, D_MODEL)),
        'w_mlp_in': nrm(ks[17], (DEPTH_2, D_MODEL, D_FF_2), D_MODEL ** -0.5),
        'w_mlp_out': nrm(ks[18], (DEPTH_2, D_FF_2, D_MODEL), D_FF_2 ** -0.5),
    }

def second_block(x, attn_norm_e, w_in_e, q_norm_a, k_norm_a, sink_a, q_norm_b, k_norm_b, rpb_b, w_out_e,
              ret_norm_o, w_in_o, decay_fwd_o, decay_bwd_o, ret_gn_o, w_out_o,
              mlp_norm, w_mlp_in, w_mlp_out):
    for layer in range(DEPTH_2):
        i = layer // 2
        if layer % 2 == 0:
            x = x + _even_mixer(x, attn_norm_e[i], w_in_e[i], q_norm_a[i], k_norm_a[i], sink_a[i],
                                q_norm_b[i], k_norm_b[i], rpb_b[i], w_out_e[i])
        else:
            x = x + _odd_mixer(x, ret_norm_o[i], w_in_o[i], decay_fwd_o[i], decay_bwd_o[i],
                               ret_gn_o[i], w_out_o[i])
        x = x + _mlp(x, mlp_norm[layer], w_mlp_in[layer], w_mlp_out[layer])
    return x


def setup_inputs(seed=0):
    out = dict(first_inputs(seed))
    for name, value in second_inputs(seed + 1).items():
        if name != "x":
            out[name + "_2"] = value
    return out


def reference(
    x, mem, w_in, b_in, mlstm_norm, sconv_w, rel_bias, hgrn_lb_logits, hgrn_norm, w_mix_out,
    norm_mix_pre, norm_mix_post, mem_norm, w_cq, w_ck, w_cv, w_co, norm_cross_pre,
    norm_cross_post, w_ffn_in, ffn_conv_w, ffn_conv_b, w_ffn_out, norm_ffn_pre, norm_ffn_post,
    attn_norm_e_2, w_in_e_2, q_norm_a_2, k_norm_a_2, sink_a_2, q_norm_b_2, k_norm_b_2, rpb_b_2,
    w_out_e_2, ret_norm_o_2, w_in_o_2, decay_fwd_o_2, decay_bwd_o_2, ret_gn_o_2, w_out_o_2,
    mlp_norm_2, w_mlp_in_2, w_mlp_out_2,
):
    x = first_block(
        x, mem, w_in, b_in, mlstm_norm, sconv_w, rel_bias, hgrn_lb_logits, hgrn_norm, w_mix_out,
        norm_mix_pre, norm_mix_post, mem_norm, w_cq, w_ck, w_cv, w_co, norm_cross_pre,
        norm_cross_post, w_ffn_in, ffn_conv_w, ffn_conv_b, w_ffn_out, norm_ffn_pre,
        norm_ffn_post,
    )
    return second_block(
        x, attn_norm_e_2, w_in_e_2, q_norm_a_2, k_norm_a_2, sink_a_2, q_norm_b_2, k_norm_b_2,
        rpb_b_2, w_out_e_2, ret_norm_o_2, w_in_o_2, decay_fwd_o_2, decay_bwd_o_2, ret_gn_o_2,
        w_out_o_2, mlp_norm_2, w_mlp_in_2, w_mlp_out_2,
    )


_drawn_inputs = setup_inputs


def setup_inputs(seed=0):
    import zlib

    import numpy as np

    out = dict(_drawn_inputs(seed))
    spreads = {}
    factors = {'mlstm_norm': 3.037,
     'hgrn_norm': 2.92,
     'ffn_conv_b': 8.0,
     'attn_norm_e_2': 8.0,
     'q_norm_a_2': 8.0,
     'k_norm_a_2': 8.0,
     'sink_a_2': 6.083,
     'q_norm_b_2': 8.0,
     'k_norm_b_2': 8.0,
     'rpb_b_2': 8.0,
     'ret_norm_o_2': 4.645,
     'ret_gn_o_2': 8.0,
     'mlp_norm_2': 3.254}
    for name, (base, spread) in spreads.items():
        noise = np.random.default_rng([zlib.crc32(name.encode()), seed]).standard_normal(out[name].shape)
        drawn = base * np.exp(spread * noise) if base else spread * noise
        out[name] = jnp.asarray(drawn.astype(out[name].dtype))
    for name, factor in factors.items():
        out[name] = (out[name] * factor).astype(out[name].dtype)
    return out
```

```python
from contextlib import ExitStack

import numpy as np
import concourse.bass as bass
from concourse import mybir

F32 = mybir.dt.float32
F32R = mybir.dt.float32r
U32 = mybir.dt.uint32
ALU = mybir.AluOpType
ACT = mybir.ActivationFunctionType
AX_X = mybir.AxisListType.X

P = 128
D = 1024
KT = D // P
N = 512
T = N // P
M = 256
HD = 64
G = 256
FF1 = 2816
FF2 = 4096
NEG = -1.0e30
LEAST = -3.0e38
RMS_EPS = 1e-6
GN_EPS = 1e-5

U_IN = 1 + 14 * 2
U_MIX = KT
U_CROSS = 12
U_CO = KT
FF1_PARTS = (8, 8, 6)
FF2_PARTS = (8, 8, 8, 8)
U_EVEN_IN = 18
U_EVEN_OUT = KT
U_HEAD = 6
RH = 8

ORDER = []
ORDER.append(("in", U_IN))
ORDER.append(("mix", U_MIX))
ORDER.append(("cross", U_CROSS))
ORDER.append(("co", U_CO))


def _parts(name, parts, up):
    out = [(f"{name}up0", up * parts[0])]
    for p in range(len(parts)):
        if p + 1 < len(parts):
            out.append((f"{name}up{p + 1}", up * parts[p + 1]))
        out.append((f"{name}down{p}", KT))
    return out


ORDER += _parts("f", FF1_PARTS, 2)
ORDER += [("even_in", U_EVEN_IN), ("even_out", U_EVEN_OUT)]
ORDER += _parts("m", FF2_PARTS, 1)
ORDER += [("odd_in0", 4 * U_HEAD), ("odd_out0", KT), ("odd_in1", 4 * U_HEAD), ("odd_out1", KT)]
ORDER += _parts("n", FF2_PARTS, 1)
FIRST = {}
_n = 0
for _name, _count in ORDER:
    FIRST[_name] = _n
    _n += _count
UNITS = _n
COUNT = dict(ORDER)

RING = 4
W_IN_P = 28

EMPTIED_BY = []
for _name, _count in ORDER:
    if _name in ("in", "cross", "even_in", "odd_in0", "odd_in1") or _name[1:3] == "up" and _name[0] in "mn":
        EMPTIED_BY += ["a"] * _count
    elif _name[1:3] == "up":
        EMPTIED_BY += ["a", "v"] * (_count // 2)
    else:
        EMPTIED_BY += ["v"] * _count
EMPTIED_BY_ACT = np.cumsum([e == "a" for e in EMPTIED_BY]).tolist()
EMPTIED_BY_DVE = np.cumsum([e == "v" for e in EMPTIED_BY]).tolist()

PCOL = {}
_c = 0
for _name, _w in (("norm_mix_pre", 8), ("norm_mix_post", 8), ("mem_norm", 8), ("norm_cross_pre", 8),
                  ("norm_cross_post", 8), ("norm_ffn_pre", 8), ("norm_ffn_post", 8), ("attn_norm_e_2", 8),
                  ("mlp0", 8), ("ret_norm_o_2", 8), ("mlp1", 8), ("b_in", 28), ("b_gates", 1),
                  ("mlstm_norm", 2), ("hgrn_norm", 2), ("hgrn_lb", 2), ("sconv_w", 6),
                  ("ffn_conv_w", 66), ("ffn_conv_b", 22), ("qa", 1), ("ka", 1), ("qb", 1), ("kb", 1),
                  ("sink", 8), ("dec_f", 8), ("dec_b", 8), ("gn", 16)):
    PCOL[_name] = _c
    _c += _w
PARAMS = _c

NSTAT = 16
LEVELS = (64, 32, 16, 8, 4, 2, 1)
CCOL = {}
_c = 0
for _name, _w in (("ident", P), ("ones", P), ("stat", 2 * NSTAT), ("pair", 8 * P), ("row", 4 * P),
                  ("col", 8), ("tri", P), ("level", 8 * P), ("half", 2)):
    CCOL[_name] = _c
    _c += _w
CONSTS = _c


def _constants():
    c = np.zeros((P, CONSTS), np.float32)
    i = np.arange(P)

    def at(name, w):
        return c[:, CCOL[name]:CCOL[name] + w]

    at("ident", P)[:] = np.eye(P)
    at("ones", P)[:] = 1.0
    at("stat", 2 * NSTAT)[:HD, NSTAT] = 1.0
    at("stat", 2 * NSTAT)[HD:, NSTAT + 1] = 1.0
    for b in range(8):
        at("pair", 8 * P)[2 * b, b * P:b * P + HD] = 1.0
        at("pair", 8 * P)[2 * b + 1, b * P + HD:(b + 1) * P] = 1.0
    for h in range(4):
        at("row", 4 * P)[h, h * P:(h + 1) * P] = 1.0
    at("col", 8)[:, 4] = 1.0
    at("tri", P)[:] = i[None, :] >= i[:, None]
    for n, half in enumerate(LEVELS):
        seg = i // (2 * half)
        right = (i % (2 * half)) >= half
        at("level", 8 * P)[:, n * P:(n + 1) * P] = (
            (seg[:, None] == seg[None, :]) & ~right[:, None] & right[None, :])
    at("level", 8 * P)[:, 7 * P:] = np.eye(P)
    at("half", 2)[:HD, 0] = at("half", 2)[HD:, 1] = HD ** -0.5
    return c


def _alibi():
    q, k = np.arange(P)[:, None], np.arange(3 * P)[None, :]
    rel = k - P - q
    out = np.zeros((P, 8, 3 * P), np.float32)
    for b in range(4):
        for s in range(2):
            slope = 2.0 ** -(4 * s + b + 1.0)
            out[:, 2 * b + s] = np.where(np.abs(rel) <= P, -slope * np.abs(rel), NEG)
    return out.reshape(P, -1)


def _distances():
    d = np.arange(7 * P)[None, :] - 3 * P - np.arange(P)[:, None]
    return np.concatenate([np.maximum(d, 0), np.maximum(-d, 0)], 1).astype(np.float32)


def build(nc, x_in, mem_in, w_in, par_in, con_in, moba_in, alibi_in, na_in, dist_in, out):
    with ExitStack() as ctx:
        def sb(name, shape, dt=F32):
            return ctx.enter_context(nc.sbuf_tensor(name, shape, dt))

        def sem(name):
            return ctx.enter_context(nc.semaphore(name))

        gemm_ps = ctx.enter_context(nc.psum_tensor("gemm_ps", [P, 2, N], F32))
        score_ps = ctx.enter_context(nc.psum_tensor("score_ps", [P, 2, N], F32))
        turn_ps = ctx.enter_context(nc.psum_tensor("turn_ps", [P, 2, N], F32))
        out_ps = ctx.enter_context(nc.psum_tensor("out_ps", [P, 2, N], F32))

        x = sb("x", [P, KT, N])
        xh = sb("xh", [P, KT, N], F32R)
        xl = sb("xl", [P, KT, N], F32R)
        raw = sb("raw", [P, RING, KT * P])
        wh = sb("wh", [P, 2, KT * P], F32R)
        wl = sb("wl", [P, 2, KT * P], F32R)
        y_all = sb("y_all", [P, (KT + 1) * N])
        y = y_all[:, 0:KT * N].rearrange("p (b n) -> p b n", n=N)
        par = sb("par", [P, PARAMS])
        con = sb("con", [P, CONSTS])
        eps = sb("eps", [P, 2])
        unity = sb("unity", [P, 2])
        small = sb("small", [P, 64])
        sq = sb("sq", [P, 2, N])
        rstd = sb("rstd", [P, N])
        tmp = sb("tmp", [P, 2, N])
        ARENA = 43 * N
        arena_at = nc.sbuf_base
        arena = sb("arena", [P, ARENA])
        arena_r = nc.alloc_sbuf_tensor_at("arena_r", [P, ARENA], F32R, offset=arena_at)

        def region(first, blocks, dt=F32):
            a = (arena if dt is F32 else arena_r)[:, first * N:(first + blocks) * N]
            return a.rearrange("p (b n) -> p b n", n=N)

        def c_(name, w, p0=0, p1=P):
            return con[p0:p1, CCOL[name]:CCOL[name] + w]

        ident = c_("ident", P)
        ones = c_("ones", P)

        def p_(name, i, p0=0, p1=P):
            return par[p0:p1, PCOL[name] + i:PCOL[name] + i + 1]

        proj1 = region(0, W_IN_P)
        M_Q, M_K, M_V, M_O, C_B, C_C, C_H, A_Q, A_K, A_V, H_Q, H_F, H_I, H_G = range(0, W_IN_P, 2)
        edge = region(28, 4)
        edge_all = arena[:, 28 * N:32 * N]
        values1 = arena[:, 32 * N:34 * N].rearrange("p (t c) -> p t c", c=G)
        mixed = region(34, 2)
        gates = arena[:, 36 * N:37 * N]
        gate_a, gate_b, gate_g = (arena[:, (37 + k) * N:(38 + k) * N] for k in range(3))
        moba_bias = region(8, 4)
        decay_q = (region(36, 2), region(38, 2))
        weights = (y_all[:, 0:4 * N], y_all[:, 4 * N:8 * N])

        def diagonal(w):
            return y_all[:, w * 4 * N:w * 4 * N + 5 * N].rearrange("p (j c) -> p j c", c=N + P)[:, :, 0:P]

        E_AQ, E_AK, E_AV, E_BQ, E_BK, E_BV = 0, 4, 5, 6, 10, 14
        proj2 = region(0, U_EVEN_IN)
        values_a = arena[:, 18 * N:19 * N].rearrange("p (t c) -> p t c", c=P)
        values_b = arena[:, 19 * N:23 * N].rearrange("p (t c) -> p t c", c=4 * P)
        alibi = arena[:, 23 * N:29 * N].rearrange("p (h k) -> p h k", h=8)
        na_all = arena[:, 29 * N:43 * N]
        na_bias = [na_all[:, 0:8 * 256].rearrange("p (h k) -> p h k", h=8),
                   na_all[:, 8 * 256:8 * 640].rearrange("p (h k) -> p h k", h=8),
                   na_all[:, 8 * 640:8 * 896].rearrange("p (h k) -> p h k", h=8)]
        na_bias = [na_bias[0], na_bias[1], na_bias[1], na_bias[2]]

        head_in = [region(6 * s, 6) for s in range(2)]
        values_r = arena[:, 12 * N:14 * N].rearrange("p (t c) -> p t c", c=G)
        decay = arena[:, 14 * N:14 * N + 7 * P]
        ret_w = region(16, 4)
        dist = arena[:, 20 * N:20 * N + 14 * P]
        ret_o = region(24, 2)
        ret_h, ret_l = region(26, 8, F32R), region(34, 8, F32R)

        hidden = [(region(16 * s, 8, F32R), region(16 * s + 8, 8, F32R)) for s in range(2)]
        padded = [arena[:, 32 * N + s * (N + 4):32 * N + (s + 1) * (N + 4)] for s in range(2)]

        def ret_unit(h):
            return FIRST[f"odd_in{h // 4}"] + U_HEAD * (h % 4)

        def attention_items(kind):
            items = []
            if kind == "moba":
                for b in range(2):
                    for t in range(T):
                        for s in range(2):
                            nk = (t + 1) * P
                            r = slice(s * HD, (s + 1) * HD)
                            items.append(dict(
                                q=proj1[:, A_Q + b, t * P:(t + 1) * P], k=proj1[:, (A_V if s == 0 else A_K) + b, 0:nk], nk=nk,
                                bias=moba_bias[:, 2 * b + s, (3 - t) * P:4 * P], sink=None,
                                v=[values1[:, c, (2 * b + s) * HD:(2 * b + s + 1) * HD] for c in range(t + 1)],
                                rows=r, tile=t, group=b, last=t == T - 1 and s == 1, first=t == 0 and s == 0,
                                to=4 + b, turned=False))
            elif kind == "cross":
                for b in range(4):
                    for t in range(T):
                        items.append(dict(
                            q=cross_q[:, b, t * P:(t + 1) * P], k=cross_k[:, b, :], nk=M, bias=None,
                            sink=None, v=[cross_v[:, c, b * P:(b + 1) * P] for c in range(2)],
                            rows=slice(0, P), tile=t, group=b, last=t == T - 1, first=t == 0, to=b, turned=False))
            elif kind == "window":
                for b in range(4):
                    for t in range(T):
                        lo, hi = max(t - 1, 0), min(t + 2, T)
                        for s in range(2):
                            r = slice(s * HD, (s + 1) * HD)
                            items.append(dict(
                                q=proj2[:, E_AQ + b, t * P:(t + 1) * P], k=proj2[:, E_AV if s == 0 else E_AK, lo * P:hi * P],
                                nk=(hi - lo) * P, bias=alibi[:, 2 * b + s, (lo - t + 1) * P:(hi - t + 1) * P],
                                sink=p_("sink", 2 * b + s),
                                v=[values_a[:, c, s * HD:(s + 1) * HD] for c in range(lo, hi)],
                                rows=r, tile=t, group=b, last=t == T - 1 and s == 1, first=t == 0 and s == 0,
                                to=b, turned=False))
            else:
                for b in range(4):
                    for t in range(T):
                        lo, hi = max(t - 1, 0), min(t + 2, T)
                        for s in range(2):
                            r = slice(s * HD, (s + 1) * HD)
                            items.append(dict(
                                q=proj2[:, E_BQ + b, t * P:(t + 1) * P],
                                k=proj2[:, (E_BV if s == 0 else E_BK) + b, lo * P:hi * P],
                                nk=(hi - lo) * P, bias=na_bias[t][:, 2 * b + s, :],
                                sink=None,
                                v=[values_b[:, c, (2 * b + s) * HD:(2 * b + s + 1) * HD] for c in range(lo, hi)],
                                rows=r, tile=t, group=b, last=t == T - 1 and s == 1, first=t == 0 and s == 0,
                                to=4 + b, turned=True))
            return items

        cross_q = region(0, 4)
        cross_k = arena[:, 4 * N:6 * N].rearrange("p (b m) -> p b m", m=M)
        cross_vf = arena[:, 6 * N:8 * N].rearrange("p (b m) -> p b m", m=M)
        cross_v = arena[:, 8 * N:10 * N].rearrange("p (t c) -> p t c", c=N)
        mem_raw = arena[:, 10 * N:14 * N].rearrange("p (b m) -> p b m", m=M)
        mem_h = arena_r[:, 14 * N:18 * N].rearrange("p (b m) -> p b m", m=M)
        mem_l = arena_r[:, 18 * N:22 * N].rearrange("p (b m) -> p b m", m=M)

        inputs_in = sem("inputs_in")
        tables_in = sem("tables_in")
        unit_in = [sem(f"unit_in{k}") for k in range(RING)]
        unity_set = sem("unity_set")
        high_split = sem("high_split")
        unit_split = sem("unit_split")
        unit_done = sem("unit_done")
        emptied_act = sem("emptied_act")
        emptied_dve = sem("emptied_dve")
        act_step = sem("act_step")
        dve_step = sem("dve_step")
        at_pe, at_act, at_dve = sem("at_pe"), sem("at_act"), sem("at_dve")
        rhs_ready = sem("rhs_ready")
        square_ready = sem("square_ready")
        square_used = sem("square_used")
        std_ready = sem("std_ready")
        rows_ready = sem("rows_ready")
        spread_ready = sem("spread_ready")
        spread_used = sem("spread_used")
        turned_v = sem("turned_v")
        copied_v = sem("copied_v")
        values_free = sem("values_free")
        scores_ready = sem("scores_ready")
        scores_used = sem("scores_used")
        logits_ready = sem("logits_ready")
        exp_ready = sem("exp_ready")
        probs_ready = sem("probs_ready")
        probs_turned = sem("probs_turned")
        probs_copied = sem("probs_copied")
        keys_ready = sem("keys_ready")
        item_done = sem("item_done")
        high_ready = sem("high_ready")
        group_used = sem("group_used")
        gate_arg = sem("gate_arg")
        gate_fun = sem("gate_fun")
        gate_rows = sem("gate_rows")
        bound_ready = sem("bound_ready")
        bound_used = sem("bound_used")
        weights_ready = sem("weights_ready")
        weights_used = sem("weights_used")
        cols_turned = sem("cols_turned")
        cols_ready = sem("cols_ready")
        level_ready = sem("level_ready")
        far_ready = sem("far_ready")
        far_copied = sem("far_copied")
        ret_std = sem("ret_std")
        value_copied = sem("value_copied")
        sum_ready = sem("sum_ready")
        hidden_raw = sem("hidden_raw")
        hidden_used = sem("hidden_used")
        conv_ready = sem("conv_ready")
        out_done = sem("out_done")

        block = ctx.enter_context(nc.Block())

        def counter(eng):
            taken = {}

            def take(s, by=1):
                taken[s] = taken.get(s, 0) + by
                eng.wait_ge(s, taken[s])
            return take, taken

        @block.sync
        def _(sp):
            sp.dma_start(x[:], x_in).then_inc(inputs_in, 16)
            sp.dma_start(par[:], par_in).then_inc(inputs_in, 16)
            sp.dma_start(con[:], con_in).then_inc(inputs_in, 16)
            for k in range(RING):
                sp.dma_start(raw[:, k, :], w_in[k * P:(k + 1) * P, :]).then_inc(unit_in[k], 16)
            with sp.Fori(1, UNITS // RING) as i:
                for k in range(RING):
                    sp.wait_ge(unit_split, RING * i + (k + 1 - RING))
                    sp.dma_start(raw[:, k, :], w_in[bass.ds((RING * i + k) * P, P), :]).then_inc(unit_in[k], 16)
            for n in range(UNITS // RING * RING, UNITS):
                sp.wait_ge(unit_split, n + 1 - RING)
                sp.dma_start(raw[:, n % RING, :], w_in[n * P:(n + 1) * P, :]).then_inc(unit_in[n % RING], 16)

        @block.gpsimd
        def _(pool):
            def split(k, landed, done, high):
                pool.wait_ge(unit_in[k], landed)
                if done is not None:
                    pool.wait_ge(unit_done, done)
                pool.tensor_tensor(wh[:, k % 2, :], raw[:, k, :], unity[:, 0:1].broadcast_to([P, KT * P]),
                                   ALU.mult).then_inc(high_split, 1)
                pool.wait_ge(high_split, high)
                pool.tensor_tensor(wl[:, k % 2, :], raw[:, k, :], wh[:, k % 2, :].bitcast(F32),
                                   ALU.subtract).then_inc(unit_split, 1)

            pool.memset(unity[:, :], 1.0).then_inc(unity_set, 1)
            pool.wait_ge(unity_set, 1)
            for n in range(RING):
                split(n, 16, None if n < 2 else n - 1, n + 1)
            with pool.Fori(1, UNITS // RING) as i:
                for k in range(RING):
                    split(k, 16 * i + 16, RING * i + k - 1, RING * i + k + 1)
            for n in range(UNITS // RING * RING, UNITS):
                split(n % RING, 16 * (n // RING + 1), n - 1, n + 1)

        @block.tensor
        def _(pe):
            take, taken = counter(pe)
            meetings, blocks_split = [0], [0]

            def meet():
                meetings[0] += 1
                pe.drain().then_inc(at_pe, 1)
                pe.wait_ge(at_act, meetings[0])
                pe.wait_ge(at_dve, meetings[0])

            def products(n, nkt, h, l, width, fresh=None):
                o = gemm_ps[:, n % 2, 0:width]
                for kt in range(nkt):
                    if fresh is not None:
                        pe.wait_ge(rhs_ready, fresh + kt + 1)
                    w = slice(kt * P, (kt + 1) * P)
                    pe.matmul(o, wh[:, n % 2, w], h[:, kt, 0:width], start=(kt == 0), stop=False)
                    pe.matmul(o, wh[:, n % 2, w], l[:, kt, 0:width], start=False, stop=False)
                    last = pe.matmul(o, wl[:, n % 2, w], h[:, kt, 0:width], start=False, stop=(kt == nkt - 1))
                last.then_inc(unit_done, 1)

            def bank_empty(n, ahead=0):
                if n < 2:
                    return
                if EMPTIED_BY[n - 2] == "a":
                    pe.wait_ge(emptied_act, ahead + EMPTIED_BY_ACT[n - 2])
                else:
                    pe.wait_ge(emptied_dve, ahead + EMPTIED_BY_DVE[n - 2])

            def units(n0, count, h, l, nkt=KT, width=N, fresh=True):
                head = min(2, count)
                for n in range(n0, n0 + head):
                    pe.wait_ge(unit_split, n + 1)
                    bank_empty(n)
                    products(n, nkt, h, l, width, blocks_split[0] if fresh and n == n0 else None)
                if fresh:
                    blocks_split[0] += nkt
                first, pairs = n0 + head, (count - head) // 2
                if pairs:
                    per = 2 if EMPTIED_BY[first] == EMPTIED_BY[first + 1] else 1
                    with pe.Fori(0, pairs) as i:
                        for n in (first, first + 1):
                            pe.wait_ge(unit_split, 2 * i + (n + 1))
                            bank_empty(n, per * i)
                            products(n, nkt, h, l, width)
                for n in range(first + 2 * pairs, n0 + count):
                    pe.wait_ge(unit_split, n + 1)
                    bank_empty(n)
                    products(n, nkt, h, l, width)

            def norm_sums(width=N, kts=KT):
                for kt in range(kts):
                    take(square_ready)
                    pe.matmul(turn_ps[:, 0, 0:width], ones, sq[:, kt % 2, 0:width], start=(kt == 0),
                              stop=(kt == kts - 1)).then_inc(square_used, 1)

            def head_norm(nb):
                heads = 2 * nb
                for b in range(nb):
                    take(square_ready)
                    w = CCOL["stat"] + NSTAT - 2 * b
                    pe.matmul(turn_ps[0:heads, 0, :], con[:, w:w + heads], sq[:, b % 2, :], start=(b == 0),
                              stop=(b == nb - 1)).then_inc(square_used, 1)
                spread(nb, heads)

            def spread(nb, heads):
                take(rows_ready)
                for b in range(nb):
                    if b >= 2:
                        take(spread_used)
                    w = CCOL["pair"] + b * P
                    pe.matmul(score_ps[:, b % 2, :], con[0:heads, w:w + P], rstd[0:heads, :], start=True,
                              stop=True).then_inc(spread_ready, 1)
                take(spread_used, min(2, nb))

            def turn_values(blocks):
                for i, a in enumerate(blocks):
                    if i >= 2:
                        take(copied_v)
                    for t in range(a.shape[1] // P):
                        m = pe.transpose(turn_ps[:, i % 2, t * P:(t + 1) * P], a[:, t * P:(t + 1) * P], ident)
                    m.then_inc(turned_v, 1)
                take(copied_v, min(2, len(blocks)))

            def attention(items):
                groups0 = taken.get(group_used, 0)

                def scores(i, it):
                    if i >= 2:
                        take(exp_ready if it["bias"] is None else scores_used)
                    pe.matmul(score_ps[:, i % 2, 0:it["nk"]], it["q"], it["k"], start=True,
                              stop=True).then_inc(scores_ready, 1)

                def turned(i, it):
                    take(probs_ready)
                    for c in range(it["nk"] // P):
                        m = pe.transpose(turn_ps[:, i % 2, c * P:(c + 1) * P], y[:, i % 3, c * P:(c + 1) * P],
                                         ident)
                    m.then_inc(probs_turned, 1)

                def values(i, it):
                    take(probs_copied)
                    if it["first"] and it["group"] >= 2:
                        pe.wait_ge(group_used, groups0 + it["group"] - 1)
                    o = out_ps[it["rows"], it["group"] % 2, it["tile"] * P:(it["tile"] + 1) * P]
                    chunks = it["nk"] // P
                    for c in range(chunks):
                        m = pe.matmul(o, it["v"][c], y[:, 3 + i % 2, c * P:(c + 1) * P], start=(c == 0),
                                      stop=(c == chunks - 1))
                    m.then_inc(item_done, 1)

                n = len(items)
                for i in range(n + 3):
                    if i < n:
                        scores(i, items[i])
                    if 2 <= i < n + 2:
                        turned(i - 2, items[i - 2])
                    if i >= 3:
                        values(i - 3, items[i - 3])
                take(exp_ready if items[0]["bias"] is None else scores_used, 2)
                if items[0]["bias"] is not None:
                    taken[exp_ready] = taken.get(exp_ready, 0) + n
                taken[group_used] = groups0 + items[-1]["group"] + 1

            def weighted(h, w, j, **flags):
                return pe.matmul(out_ps[(h % 2) * HD:(h % 2 + 1) * HD, h // 2, j * P:N],
                                 values1[:, j, h * HD:(h + 1) * HD], w[:, j * N + j * P:(j + 1) * N], **flags)

            def mlstm():
                turn_values([proj1[:, M_V, :], proj1[:, M_V + 1, :]])
                take(gate_rows)
                for t in range(T):
                    m = pe.transpose(turn_ps[:, 0, 4 * t:4 * t + 4], gate_b[0:4, t * P:(t + 1) * P], ident[0:4, 0:4])
                m.then_inc(cols_turned, 1)
                take(cols_ready)
                take(gate_rows)
                for h in range(4):
                    w = weights[h % 2]
                    r = slice((h % 2) * HD, (h % 2 + 1) * HD)
                    if h >= 1:
                        take(bound_used)
                    pe.matmul(turn_ps[:, 0, :], con[0:4, CCOL["row"] + h * P:CCOL["row"] + (h + 1) * P],
                              gate_a[0:4, :], start=True, stop=True).then_inc(bound_ready, 1)
                    for j in range(T + 2):
                        if j < T:
                            if h > 0 or j >= 2:
                                take(scores_used)
                            pe.matmul(score_ps[:, j % 2, j * P:N], proj1[r, M_K + h // 2, j * P:(j + 1) * P],
                                      proj1[r, M_Q + h // 2, j * P:N], start=True, stop=True).then_inc(scores_ready, 1)
                        if j >= 2:
                            k = j - 2
                            take(weights_ready)
                            weighted(h, w, k, start=(k == 0), stop=(k == T - 1))
                            m = pe.matmul(turn_ps[0:4, 1, k * P:N], con[:, CCOL["col"] + 4 - h:CCOL["col"] + 8 - h],
                                          w[:, k * N + k * P:(k + 1) * N], start=(h == 0 and k == 0),
                                          stop=(h == 3 and k == T - 1), skip_group_check=True)
                    m.then_inc(weights_used, 1)
                take(scores_used, 2)
                take(bound_used)
                spread(2, 4)

            def hgrn():
                turn_values([proj1[:, H_I, :], proj1[:, H_I + 1, :]])
                for b in range(2):
                    take(level_ready)
                    kk, q1, q2, q3 = proj1[:, 6, :], proj1[:, 7, :], edge[:, 0, :], edge[:, 1, :]
                    for s in range(2):
                        r = slice(s * HD, (s + 1) * HD)
                        for j, i, q in ((0, 1, q1), (1, 2, q1), (2, 3, q1), (0, 2, q2), (1, 3, q2), (0, 3, q3)):
                            bank, col = (0, i * P) if j == 0 else (1, (i if j == 1 else 0) * P)
                            m = pe.matmul(turn_ps[:, bank, col:col + P], kk[r, j * P:(j + 1) * P],
                                          q[r, i * P:(i + 1) * P], start=True, stop=True)
                        m.then_inc(far_ready, 1)
                        take(far_copied)
                    for lev in range(len(LEVELS) + 1):
                        take(level_ready)
                        kk, qq = decay_q[lev % 2][:, 0, :], decay_q[lev % 2][:, 1, :]
                        for s in range(2):
                            r = slice(s * HD, (s + 1) * HD)
                            if lev:
                                take(scores_used)
                            for j in range(T):
                                t = slice(j * P, (j + 1) * P)
                                m = pe.matmul(score_ps[:, s, t], kk[r, t], qq[r, t], start=True, stop=True)
                            m.then_inc(scores_ready, 1)
                    take(scores_used, 2)
                    for s in range(2):
                        for j in range(T):
                            m = weighted(2 * b + s, weights[s], j, start=(j == 0), stop=(j == T - 1))
                    m.then_inc(weights_used, 1)

            def retention(h):
                q, k, v0, v1 = (head_in[h % 2][:, b, :] for b in range(4))
                pe.wait_ge(emptied_act, EMPTIED_BY_ACT[ret_unit(h) + 5])
                turn_values([v0, v1])
                for j in range(T + 2):
                    if j >= 2:
                        take(scores_used)
                    if j < T:
                        pe.matmul(score_ps[:, j % 2, :], k[:, j * P:(j + 1) * P], q, start=True,
                                  stop=True).then_inc(scores_ready, 1)
                    if j >= 2:
                        i = j - 2
                        for c in range(2):
                            m = pe.matmul(out_ps[:, c, :], values_r[:, i, c * P:(c + 1) * P], ret_w[:, i, :],
                                          start=(i == 0), stop=(i == T - 1))
                m.then_inc(weights_used, 1)
                take(value_copied)
                for c in range(2):
                    m = pe.matmul(turn_ps[:, 0, :], ones, ret_o[:, c, :], start=(c == 0), stop=(c == 1))
                m.then_inc(sum_ready, 1)
                for c in range(2):
                    take(square_ready)
                    pe.matmul(turn_ps[:, 1, :], ones, sq[:, c, :], start=(c == 0),
                              stop=(c == 1)).then_inc(square_used, 1)
                take(ret_std)

            def mlp(name, parts, up):
                def down(p):
                    units(FIRST[f"{name}down{p}"], KT, *hidden[p % 2], nkt=parts[p])
                for p in range(len(parts)):
                    units(FIRST[f"{name}up{p}"], up * parts[p], xh, xl, fresh=p == 0)
                    if p:
                        down(p - 1)
                down(len(parts) - 1)

            pe.wait_ge(inputs_in, 48)
            meet()
            norm_sums()
            units(FIRST["in"], U_IN, xh, xl)
            meet()
            mlstm()
            meet()
            head_norm(2)
            meet()
            hgrn()
            meet()
            head_norm(2)
            meet()
            turn_values([proj1[:, A_V, :], proj1[:, A_V + 1, :]])
            take(keys_ready, 2)
            attention(attention_items("moba"))
            meet()
            units(FIRST["mix"], U_MIX, xh, xl, fresh=False)
            meet()
            norm_sums()
            meet()
            norm_sums(M)
            meet()
            norm_sums()
            units(FIRST["cross"], 4, xh, xl)
            units(FIRST["cross"] + 4, 8, mem_h, mem_l, width=M, fresh=False)
            meet()
            turn_values([cross_vf[:, b, :] for b in range(4)])
            attention(attention_items("cross"))
            meet()
            units(FIRST["co"], U_CO, xh, xl, nkt=4, fresh=False)
            meet()
            norm_sums()
            meet()
            norm_sums()
            mlp("f", FF1_PARTS, 2)
            meet()
            norm_sums()
            meet()
            norm_sums()
            units(FIRST["even_in"], U_EVEN_IN, xh, xl)
            meet()
            turn_values([proj2[:, E_AV, :]])
            turn_values([proj2[:, E_BV + b, :] for b in range(4)])
            head_norm(5)
            head_norm(8)
            take(keys_ready, 5)
            meet()
            attention(attention_items("window"))
            attention(attention_items("neighbour"))
            meet()
            units(FIRST["even_out"], U_EVEN_OUT, xh, xl, fresh=False)
            meet()
            norm_sums()
            mlp("m", FF2_PARTS, 1)
            meet()
            norm_sums()
            for half in range(2):
                for h in range(4 * half, 4 * half + 4):
                    units(ret_unit(h), U_HEAD, xh, xl, fresh=h == 0)
                    if h % 4:
                        retention(h - 1)
                retention(4 * half + 3)
                units(FIRST[f"odd_out{half}"], KT, ret_h, ret_l)
            meet()
            norm_sums()
            mlp("n", FF2_PARTS, 1)
            meet()

        @block.scalar
        def _(act):
            take, taken = counter(act)
            meetings, steps = [0], [0]

            def meet():
                meetings[0] += 1
                act.drain().then_inc(at_act, 1)
                act.wait_ge(at_pe, meetings[0])
                act.wait_ge(at_dve, meetings[0])

            def step(ins):
                steps[0] += 1
                ins.then_inc(act_step, 1)
                act.wait_ge(act_step, steps[0])

            def squares(src, nb, width=N):
                for b in range(nb):
                    if b >= 2:
                        take(square_used)
                    act.activation(sq[:, b % 2, 0:width], src[b], ACT.Square).then_inc(square_ready, 1)
                take(square_used, min(2, nb))

            def norm(src, width=N):
                squares([src[:, kt, :] for kt in range(KT)], KT, width)
                act.activation(rstd[:, 0:width], turn_ps[:, 0, 0:width], ACT.Sqrt, bias=eps[:, 0:1],
                               scale=1.0 / D).then_inc(std_ready, 1)

            def head_norm(src):
                squares(src, len(src))
                r = slice(0, 2 * len(src))
                act.activation(rstd[r, :], turn_ps[r, 0, :], ACT.Sqrt, bias=eps[r, 0:1],
                               scale=1.0 / HD).then_inc(std_ready, 1)

            def copy_values(dst):
                for i, o in enumerate(dst):
                    take(turned_v)
                    w = o.shape[1] * P
                    act.activation(o, turn_ps[:, i % 2, 0:w].rearrange("p (t c) -> p t c", c=P),
                                   ACT.Identity).then_inc(copied_v, 1)

            def empty(n, dst, func=ACT.Identity, bias=0.0, width=N, rows=P, src=None, scale=1.0):
                act.wait_ge(unit_done, n + 1)
                a = gemm_ps[0:rows, n % 2, 0:width] if src is None else src(gemm_ps[:, n % 2, :])
                return act.activation(dst, a, func, bias=bias, scale=scale).then_inc(emptied_act, 1)

            def attention(items):
                items0 = taken.get(item_done, 0)

                def exps(i, it):
                    take(logits_ready)
                    s, a = 8 * (i % 3), y[:, i % 3, 0:it["nk"]]
                    if it["sink"] is not None:
                        act.activation(small[:, s + 2:s + 3], it["sink"], ACT.Exp, bias=small[:, s:s + 1], scale=-1.0)
                    act.activation(a, score_ps[:, i % 2, 0:it["nk"]] if it["bias"] is None else a, ACT.Exp,
                                   bias=small[:, s:s + 1], accum_out=small[:, s + 1:s + 2]).then_inc(exp_ready, 1)

                def copies(i, it):
                    take(probs_turned)
                    if i >= 2:
                        act.wait_ge(item_done, items0 + i - 1)
                    act.activation(y[:, 3 + i % 2, 0:it["nk"]], turn_ps[:, i % 2, 0:it["nk"]],
                                   ACT.Identity).then_inc(probs_copied, 1)

                def outputs(i, it):
                    act.wait_ge(item_done, items0 + i + 1)
                    o, a = xh[:, it["to"], :], out_ps[:, it["group"] % 2, :]
                    if it["turned"]:
                        o = o.rearrange("p (r c) -> p c r", r=8)
                        a = a.rearrange("p (c r) -> p c r", r=8)
                    act.activation(o, a, ACT.Identity).then_inc(high_ready, 1)

                n = len(items)
                for i in range(n + 4):
                    if i < n:
                        exps(i, items[i])
                    if 2 <= i < n + 2:
                        copies(i - 2, items[i - 2])
                    if i >= 4 and items[i - 4]["last"]:
                        outputs(i - 4, items[i - 4])
                taken[item_done] = items0 + n

            def mlstm():
                f = slice(32, 36)
                step(act.activation(gate_a[f, :], gates[f, :], ACT.Abs))
                step(act.activation(gate_a[f, :], gate_a[f, :], ACT.Exp, scale=-1.0))
                act.activation(gate_b[f, :], gate_a[f, :], ACT.Ln, bias=1.0).then_inc(gate_fun, 1)
                copy_values([values1[:, :, b * P:(b + 1) * P] for b in range(2)])
                take(cols_turned)
                act.activation(small[:, 32:48], turn_ps[:, 0, 0:16], ACT.Identity).then_inc(cols_ready, 1)
                take(gate_arg)
                step(act.activation(gates[0:4, :], gates[0:4, :], ACT.Exp, scale=-1.0))
                for h in range(4):
                    take(bound_used)
                    for j in range(T):
                        m = act.activation(edge[:, j, j * P:N], edge[:, j, j * P:N], ACT.Exp)
                    m.then_inc(gate_fun, 1)
                take(weights_used, 4)
                act.activation(gate_g[0:4, :], turn_ps[0:4, 1, :], ACT.Abs).then_inc(gate_fun, 1)
                for b in range(2):
                    step(act.activation(proj1[:, M_O + b, :], proj1[:, M_O + b, :], ACT.Sigmoid))

            def hgrn():
                take(gate_arg)
                act.activation(small[:, 18:20], small[:, 16:18], ACT.Exp).then_inc(gate_fun, 1)
                for b in range(2):
                    act.activation(proj1[:, H_F + b, :], proj1[:, H_F + b, :], ACT.Sigmoid)
                    act.activation(proj1[:, H_Q + b, :], proj1[:, H_Q + b, :], ACT.Silu)
                    m = act.activation(proj1[:, H_G + b, :], proj1[:, H_G + b, :], ACT.Silu)
                m.then_inc(gate_fun, 1)
                copy_values([values1[:, :, b * P:(b + 1) * P] for b in range(2)])
                take(gate_arg)
                for b in range(2):
                    m = act.activation(proj1[:, 2 + b, :], proj1[:, H_F + b, :], ACT.Ln)
                m.then_inc(gate_fun, 1)
                take(gate_arg)
                for b in range(2):
                    g = proj1[:, 4 + b, :]
                    if b:
                        take(weights_used)
                    for j in range(T):
                        t = slice(j * P, (j + 1) * P)
                        act.activation(proj1[:, 6, t], g[:, t], ACT.Exp, bias=g[:, (j + 1) * P - 1:(j + 1) * P],
                                       scale=-1.0)
                    act.activation(proj1[:, 7, :], g, ACT.Exp)
                    act.activation(small[:, 24:28], g[:, P - 1:N:P], ACT.Exp).then_inc(gate_fun, 1)
                    for s in range(2):
                        take(far_ready)
                        w = weights[s]
                        act.activation(w[:, P:N], turn_ps[:, 0, P:N], ACT.Identity)
                        act.activation(w[:, N + 2 * P:2 * N], turn_ps[:, 1, 2 * P:N], ACT.Identity)
                        act.activation(w[:, 2 * N + 3 * P:3 * N], turn_ps[:, 1, 0:P],
                                       ACT.Identity).then_inc(far_copied, 1)
                    for lev in range(len(LEVELS)):
                        take(gate_arg)
                        act.activation(edge[:, 2, :], edge[:, 3, :], ACT.Exp).then_inc(gate_fun, 1)
                take(weights_used)
                for b in range(2):
                    step(act.activation(mixed[:, b, :], out_ps[:, b, :], ACT.Identity))

            def retention(h):
                copy_values([values_r[:, :, c * P:(c + 1) * P] for c in range(2)])
                take(gate_arg)
                act.activation(decay, decay, ACT.Exp).then_inc(gate_fun, 1)
                take(weights_used)
                if h:
                    act.wait_ge(hidden_used, heads0[0] + h)
                for c in range(2):
                    m = act.activation(ret_o[:, c, :], out_ps[:, c, :], ACT.Identity)
                m.then_inc(value_copied, 1)
                for c in range(2):
                    take(gate_arg)
                    act.activation(sq[:, c, :], ret_o[:, c, :], ACT.Square).then_inc(square_ready, 1)
                take(square_used, 2)
                act.activation(rstd[:, :], turn_ps[:, 1, :], ACT.Sqrt, bias=eps[:, 1:2],
                               scale=1.0 / G).then_inc(ret_std, 1)

            def mlp(name, parts):
                blocks = 0
                for p in range(len(parts)):
                    n0 = FIRST[f"{name}up{p}"]
                    for b in range(parts[p]):
                        if blocks >= 2:
                            take(hidden_used)
                        blocks += 1
                        empty(n0 + b, tmp[:, blocks % 2, :], ACT.Relu)
                take(hidden_used, 2)

            def gated(parts):
                def silu(b):
                    take(conv_ready)
                    act.activation(sq[:, b % 2, :], tmp[:, b % 2, :], ACT.Silu,
                                   bias=p_("ffn_conv_b", b)).then_inc(hidden_raw, 1)
                b = 0
                for p in range(len(parts)):
                    for i in range(parts[p]):
                        empty(FIRST[f"fup{p}"] + 2 * i, padded[b % 2][:, 2:N + 2])
                        silu(b)
                        b += 1

            heads0 = [0]
            act.wait_ge(inputs_in, 48)
            meet()
            norm(x)
            empty(FIRST["in"], gates[0:HD, :], bias=p_("b_gates", 0, 0, HD), rows=HD)
            for b in range(W_IN_P):
                empty(FIRST["in"] + 1 + b, proj1[:, b, :], bias=p_("b_in", b))
            meet()
            mlstm()
            meet()
            head_norm([mixed[:, b, :] for b in range(2)])
            meet()
            act.dma_start(arena[:, 8 * N:12 * N], moba_in).then_inc(tables_in, 16)
            hgrn()
            meet()
            head_norm([mixed[:, b, :] for b in range(2)])
            meet()
            act.wait_ge(tables_in, 16)
            copy_values([values1[:, :, b * P:(b + 1) * P] for b in range(2)])
            act.drain().then_inc(values_free, 1)
            attention(attention_items("moba"))
            meet()
            act.dma_start(arena[:, 10 * N:14 * N], mem_in).then_inc(tables_in, 16)
            meet()
            norm(y)
            meet()
            act.wait_ge(tables_in, 32)
            norm(mem_raw, M)
            meet()
            norm(x)
            for b in range(4):
                empty(FIRST["cross"] + b, cross_q[:, b, :], scale=P ** -0.5)
            for b in range(4):
                empty(FIRST["cross"] + 4 + b, cross_k[:, b, :], width=M)
            for b in range(4):
                empty(FIRST["cross"] + 8 + b, cross_vf[:, b, :], width=M)
            meet()
            copy_values([cross_v[:, :, b * P:(b + 1) * P] for b in range(4)])
            attention(attention_items("cross"))
            meet()
            meet()
            norm(y)
            meet()
            norm(x)
            gated(FF1_PARTS)
            meet()
            act.dma_start(arena[:, 23 * N:29 * N], alibi_in).then_inc(tables_in, 16)
            act.dma_start(na_all, na_in).then_inc(tables_in, 16)
            norm(y)
            meet()
            norm(x)
            for b in range(U_EVEN_IN):
                o, src = proj2[:, b, :], None
                if b >= E_BQ:
                    o = o.rearrange("p (c r) -> p r c", r=8)
                    src = lambda a: a.rearrange("p (r c) -> p r c", r=8)
                empty(FIRST["even_in"] + b, o, src=src)
            meet()
            copy_values([values_a])
            copy_values([values_b[:, :, b * P:(b + 1) * P] for b in range(4)])
            head_norm([proj2[:, E_AQ + b, :] for b in range(5)])
            head_norm([proj2[:, E_BQ + b, :] for b in range(8)])
            meet()
            attention(attention_items("window"))
            attention(attention_items("neighbour"))
            meet()
            meet()
            norm(x)
            mlp("m", FF2_PARTS)
            meet()
            act.dma_start(dist, dist_in).then_inc(tables_in, 16)
            norm(x)
            step(act.activation(small[:, 16:32], par[:, PCOL["dec_f"]:PCOL["dec_f"] + 16], ACT.Abs))
            step(act.activation(small[:, 16:32], small[:, 16:32], ACT.Exp, scale=-1.0))
            act.activation(small[:, 32:48], small[:, 16:32], ACT.Ln, bias=1.0).then_inc(gate_fun, 1)
            heads0[0] = taken[hidden_used]
            for half in range(2):
                for h in range(4 * half, 4 * half + 4):
                    if h >= 2:
                        act.wait_ge(hidden_used, heads0[0] + h - 1)
                    for b in range(U_HEAD):
                        empty(ret_unit(h) + b, head_in[h % 2][:, b, :], ACT.Silu if b >= 4 else ACT.Identity)
                    if h % 4:
                        retention(h - 1)
                retention(4 * half + 3)
            taken[hidden_used] += RH
            meet()
            norm(x)
            mlp("n", FF2_PARTS)
            meet()
            act.dma_start(out, x[:]).then_inc(out_done, 16)
            act.wait_ge(out_done, 16)

        @block.vector
        def _(dve):
            take, taken = counter(dve)
            meetings = [0]

            def meet():
                meetings[0] += 1
                dve.drain().then_inc(at_dve, 1)
                dve.wait_ge(at_pe, meetings[0])
                dve.wait_ge(at_act, meetings[0])

            def done(ins, s=dve_step):
                ins.then_inc(s, 1)
                take(s)

            def stt(o, a, scalar, b, op0, op1, s=dve_step):
                done(dve.scalar_tensor_tensor(out=o, in0=a, scalar=scalar, in1=b, op0=op0, op1=op1), s)

            def split(a, h, l, s=dve_step):
                done(dve.tensor_copy(h, a))
                done(dve.tensor_tensor(l, a, h.bitcast(F32), ALU.subtract), s)

            def norm_split(src, gain, h, l, width=N, s=rhs_ready):
                r = rstd[:, 0:width]
                take(std_ready)
                done(dve.reciprocal(r, r))
                for kt in range(KT):
                    t = tmp[:, kt % 2, 0:width]
                    stt(t, src[:, kt, :], p_(gain, kt), r, ALU.mult, ALU.mult)
                    split(t, h[:, kt, :], l[:, kt, :], s)

            def norm_add(gain):
                take(std_ready)
                done(dve.reciprocal(rstd[:, :], rstd[:, :]))
                for kt in range(KT):
                    t = tmp[:, kt % 2, :]
                    stt(t, y[:, kt, :], p_(gain, kt), rstd[:, :], ALU.mult, ALU.mult)
                    done(dve.tensor_tensor(x[:, kt, :], x[:, kt, :], t, ALU.add))

            def head_rows(nb):
                take(std_ready)
                done(dve.reciprocal(rstd[0:2 * nb, :], rstd[0:2 * nb, :]), rows_ready)

            def head_norm(blocks, gains):
                head_rows(len(blocks))
                for b, a in enumerate(blocks):
                    take(spread_ready)
                    stt(a, a, gains[b], score_ps[:, b % 2, :], ALU.mult, ALU.mult, spread_used)

            def mixer_out(gain, gate, to):
                head_rows(2)
                for b in range(2):
                    take(spread_ready)
                    stt(tmp[:, b, :], mixed[:, b, :], p_(gain, b), score_ps[:, b, :], ALU.mult, ALU.mult,
                        spread_used)
                    done(dve.tensor_tensor(tmp[:, b, :], tmp[:, b, :], proj1[:, gate + b, :], ALU.mult))
                    split(tmp[:, b, :], xh[:, to + b, :], xl[:, to + b, :])

            def store(n0, first):
                for b in range(KT):
                    dve.wait_ge(unit_done, n0 + b + 1)
                    ps = gemm_ps[:, (n0 + b) % 2, :]
                    if first:
                        done(dve.tensor_copy(y[:, b, :], ps), emptied_dve)
                    else:
                        done(dve.tensor_tensor(y[:, b, :], y[:, b, :], ps, ALU.add), emptied_dve)

            def add(n0):
                for b in range(KT):
                    dve.wait_ge(unit_done, n0 + b + 1)
                    done(dve.tensor_tensor(x[:, b, :], x[:, b, :], gemm_ps[:, (n0 + b) % 2, :], ALU.add),
                         emptied_dve)

            def part_heads(k, other):
                done(dve.tensor_scalar(other, k, c_("half", 2)[:, 0:1], None, ALU.mult))
                done(dve.tensor_scalar(k, k, c_("half", 2)[:, 1:2], None, ALU.mult), keys_ready)

            def attention(items):
                def logits(i, it):
                    take(scores_ready)
                    s = 8 * (i % 3)
                    ps, top = score_ps[:, i % 2, 0:it["nk"]], small[:, s:s + 1]
                    if i >= 3:
                        take(probs_turned)
                    if it["bias"] is None:
                        done(dve.tensor_reduce(top, ps, AX_X, ALU.max, negate=True), logits_ready)
                        return
                    done(dve.tensor_tensor_reduce(y[:, i % 3, 0:it["nk"]], ps, it["bias"], 1.0, LEAST, ALU.add,
                                                  ALU.max, small[:, s + 4:s + 5]), scores_used)
                    if it["sink"] is None:
                        done(dve.tensor_scalar(top, small[:, s + 4:s + 5], -1.0, None, ALU.mult), logits_ready)
                    else:
                        stt(top, small[:, s + 4:s + 5], -1.0, it["sink"], ALU.mult, ALU.min, logits_ready)

                def divide(i, it):
                    take(exp_ready)
                    s = 8 * (i % 3)
                    total, a = small[:, s + 1:s + 2], y[:, i % 3, 0:it["nk"]]
                    if it["sink"] is not None:
                        done(dve.tensor_tensor(total, total, small[:, s + 2:s + 3], ALU.add))
                    done(dve.reciprocal(small[:, s + 3:s + 4], total))
                    done(dve.tensor_scalar(a, a, small[:, s + 3:s + 4], None, ALU.mult), probs_ready)

                def outputs(it):
                    take(high_ready)
                    h, l, a = xh[:, it["to"], :], xl[:, it["to"], :], out_ps[:, it["group"] % 2, :]
                    if it["turned"]:
                        h, l = (v.rearrange("p (r c) -> p c r", r=8) for v in (h, l))
                        a = a.rearrange("p (c r) -> p c r", r=8)
                    done(dve.tensor_tensor(l, a, h.bitcast(F32), ALU.subtract), group_used)

                n = len(items)
                for i in range(n + 4):
                    if i < n:
                        logits(i, items[i])
                    if 1 <= i <= n:
                        divide(i - 1, items[i - 1])
                    if i >= 4 and items[i - 4]["last"]:
                        outputs(items[i - 4])
                take(probs_turned, 3)

            def mlstm():
                f, r = slice(32, 36), slice(0, 4)
                one = edge[:, 0, :]
                done(dve.memset(one, 1.0))
                done(dve.tensor_scalar(gate_g[f, :], gates[f, :], 0.0, None, ALU.min))
                take(gate_fun)
                done(dve.tensor_tensor(gate_g[f, :], gate_g[f, :], gate_b[f, :], ALU.subtract))
                done(dve.tensor_tensor_scan(gate_a[f, :], one[f, :], gate_g[f, :], 0.0,
                                            ALU.mult, ALU.add))
                done(dve.tensor_copy(gate_g[r, :], gate_a[f, :]))
                done(dve.tensor_tensor(gate_b[r, :], gates[r, :], gate_g[r, :], ALU.subtract), gate_rows)
                done(dve.tensor_tensor_scan(gate_a[r, :], one[r, :], gate_b[r, :], 0.0,
                                            ALU.mult, ALU.max))
                done(dve.tensor_tensor(gates[r, :], gate_g[r, :], gate_a[r, :], ALU.add), gate_arg)
                done(dve.tensor_scalar(gate_a[r, :], gate_a[r, :], -1.0, None, ALU.mult), gate_rows)
                take(cols_ready)
                for h in range(4):
                    take(bound_ready)
                    for j in range(T):
                        m = dve.tensor_scalar(edge[:, j, j * P:N], turn_ps[:, 0, j * P:N],
                                              small[:, 32 + 4 * j + h:33 + 4 * j + h], 0.0, ALU.add, ALU.min)
                    done(m, bound_used)
                    take(gate_fun)
                    if h >= 2:
                        take(weights_used)
                    w = weights[h % 2]
                    for j in range(T):
                        take(scores_ready)
                        stt(w[:, j * N + j * P:(j + 1) * N], score_ps[:, j % 2, j * P:N], HD ** -0.5,
                            edge[:, j, j * P:N], ALU.mult, ALU.mult, scores_used)
                        d = w[:, j * N + j * P:j * N + (j + 1) * P]
                        done(dve.tensor_tensor(d, d, c_("tri", P), ALU.mult), weights_ready)
                take(weights_used, 2)
                take(gate_fun)
                done(dve.tensor_tensor(gate_g[r, :], gate_g[r, :], gates[r, :], ALU.max))
                done(dve.reciprocal(rstd[r, :], gate_g[r, :]), rows_ready)
                for b in range(2):
                    take(spread_ready)
                    done(dve.tensor_copy(tmp[:, b, :], score_ps[:, b, :]), spread_used)
                    done(dve.tensor_tensor(mixed[:, b, :], out_ps[:, b, :], tmp[:, b, :], ALU.mult))

            def short_conv():
                for b in range(2):
                    u = edge_all[:, b * (N + 4):(b + 1) * (N + 4)]
                    t = tmp[:, b, :]
                    done(dve.memset(u[:, 0:2], 0.0))
                    done(dve.tensor_tensor(u[:, 2:N + 2], proj1[:, C_C + b, :], proj1[:, C_H + b, :], ALU.mult))
                    convolve(t, u, [p_("sconv_w", 2 * k + b) for k in range(3)])
                    done(dve.tensor_tensor(t, t, proj1[:, C_B + b, :], ALU.mult))
                    split(t, xh[:, 2 + b, :], xl[:, 2 + b, :])

            def convolve(o, u, w, s=dve_step):
                done(dve.tensor_scalar(o, u[:, 0:N], w[0], None, ALU.mult))
                stt(o, u[:, 1:N + 1], w[1], o, ALU.mult, ALU.add)
                stt(o, u[:, 2:N + 2], w[2], o, ALU.mult, ALU.add, s)

            def hgrn():
                lb = par[:, PCOL["hgrn_lb"]:PCOL["hgrn_lb"] + 2]
                a, e, r = small[:, 16:18], small[:, 18:20], small[:, 20:22]
                done(dve.tensor_tensor(a, lb, lb, ALU.subtract), gate_arg)
                take(gate_fun)
                done(dve.reciprocal(r, e))
                done(dve.tensor_tensor(a, e, r, ALU.mult))
                done(dve.tensor_tensor(e, a, a, ALU.subtract))
                done(dve.tensor_scalar(r, e, -1.0, 1.0, ALU.mult, ALU.add))
                take(gate_fun)
                for b in range(2):
                    f = proj1[:, H_F + b, :]
                    done(dve.tensor_scalar(f, f, r[:, b:b + 1], e[:, b:b + 1], ALU.mult, ALU.add),
                         gate_arg if b else dve_step)
                for b in range(2):
                    done(dve.tensor_scalar(proj1[:, b, :], proj1[:, H_F + b, :], -1.0, 1.0, ALU.mult, ALU.add))
                for w in weights:
                    done(dve.memset(w, 0.0))
                reset = edge[:, 3, :]
                done(dve.memset(reset, 1.0))
                done(dve.memset(reset.rearrange("p (t c) -> p t c", c=P)[:, :, 0:1], 0.0))
                take(gate_fun)
                for b in range(2):
                    done(dve.tensor_tensor_scan(proj1[:, 4 + b, :], reset, proj1[:, 2 + b, :], 0.0,
                                                ALU.mult, ALU.add), gate_arg if b else dve_step)
                for b in range(2):
                    k, q, g = proj1[:, b, :], proj1[:, H_Q + b, :], proj1[:, 4 + b, :]
                    kk, q1, q2, q3 = proj1[:, 6, :], proj1[:, 7, :], edge[:, 0, :], edge[:, 1, :]
                    take(gate_fun)
                    done(dve.tensor_tensor(kk, kk, k, ALU.mult))
                    done(dve.tensor_tensor(q1, q1, q, ALU.mult))
                    for o, src, i, over in ((q2, q1, 2, 1), (q2, q1, 3, 2), (q3, q2, 3, 1)):
                        t = slice(i * P, (i + 1) * P)
                        done(dve.tensor_scalar(o[:, t], src[:, t], small[:, 24 + over:25 + over], None, ALU.mult),
                             level_ready if o is q3 else dve_step)
                    if b:
                        take(weights_used)

                    def scores(lev):
                        mask = con[:, CCOL["level"] + lev * P:CCOL["level"] + (lev + 1) * P].bitcast(U32)
                        for s in range(2):
                            take(scores_ready)
                            done(dve.copy_predicated(
                                diagonal(s), mask.unsqueeze(1).broadcast_to([P, T, P]),
                                score_ps[:, s, :].rearrange("p (j c) -> p j c", c=P)), scores_used)

                    for lev, half in enumerate(LEVELS):
                        gs = g.rearrange("p (s c) -> p s c", c=2 * half)
                        ds = edge[:, 3, :].rearrange("p (s c) -> p s c", c=2 * half)
                        ref = gs[:, :, half - 1:half].broadcast_to([P, N // (2 * half), half])
                        done(dve.tensor_tensor(ds[:, :, 0:half], ref, gs[:, :, 0:half], ALU.subtract))
                        done(dve.tensor_tensor(ds[:, :, half:], gs[:, :, half:], ref, ALU.subtract), gate_arg)
                        if lev:
                            scores(lev - 1)
                        take(gate_fun)
                        done(dve.tensor_tensor(decay_q[lev % 2][:, 0, :], k, edge[:, 2, :], ALU.mult))
                        done(dve.tensor_tensor(decay_q[lev % 2][:, 1, :], q, edge[:, 2, :], ALU.mult), level_ready)
                    done(dve.tensor_copy(decay_q[1][:, 0, :], k))
                    done(dve.tensor_copy(decay_q[1][:, 1, :], q), level_ready)
                    scores(6)
                    scores(7)
                take(weights_used)

            def retention(h):
                done(dve.tensor_scalar(decay, dist[:, 0:7 * P], small[:, 48 + h:49 + h], None, ALU.mult))
                stt(decay, dist[:, 7 * P:14 * P], small[:, 56 + h:57 + h], decay, ALU.mult, ALU.add, gate_arg)
                take(gate_fun)
                for j in range(T):
                    take(scores_ready)
                    stt(ret_w[:, j, :], score_ps[:, j % 2, :], P ** -0.5, decay[:, (3 - j) * P:(7 - j) * P],
                        ALU.mult, ALU.mult, scores_used)
                take(weights_used)
                take(sum_ready)
                for c in range(2):
                    stt(ret_o[:, c, :], turn_ps[:, 0, :], -1.0 / G, ret_o[:, c, :], ALU.mult, ALU.add, gate_arg)
                take(ret_std)
                done(dve.reciprocal(rstd[:, :], rstd[:, :]))
                dve.wait_ge(emptied_act, EMPTIED_BY_ACT[ret_unit(h) + 5])
                for c in range(2):
                    t, b = tmp[:, c, :], 2 * (h % 4) + c
                    stt(t, ret_o[:, c, :], p_("gn", 2 * h + c), rstd[:, :], ALU.mult, ALU.mult)
                    done(dve.tensor_tensor(t, t, head_in[h % 2][:, 4 + c, :], ALU.mult),
                         hidden_used if c else dve_step)
                    split(t, ret_h[:, b, :], ret_l[:, b, :], rhs_ready)

            def mlp(name, parts):
                blocks = 0
                for p in range(len(parts)):
                    h, l = hidden[p % 2]
                    for b in range(parts[p]):
                        n = FIRST[f"{name}up{p}"] + b
                        blocks += 1
                        dve.wait_ge(emptied_act, EMPTIED_BY_ACT[n])
                        r = tmp[:, blocks % 2, :]
                        done(dve.tensor_tensor(rstd[:, :], r, r, ALU.mult), hidden_used)
                        split(rstd[:, :], h[:, b, :], l[:, b, :], rhs_ready)
                    if p:
                        add(FIRST[f"{name}down{p - 1}"])
                add(FIRST[f"{name}down{len(parts) - 1}"])

            def gated(parts):
                for u in padded:
                    done(dve.memset(u[:, 0:2], 0.0))

                def finish(b, p, i):
                    n = FIRST[f"fup{p}"] + 2 * i + 1
                    take(hidden_raw)
                    dve.wait_ge(unit_done, n + 1)
                    done(dve.tensor_tensor(rstd[:, :], sq[:, b % 2, :], gemm_ps[:, n % 2, :], ALU.mult), emptied_dve)
                    split(rstd[:, :], hidden[p % 2][0][:, i, :], hidden[p % 2][1][:, i, :], rhs_ready)

                b = 0
                for p in range(len(parts)):
                    for i in range(parts[p]):
                        dve.wait_ge(emptied_act, EMPTIED_BY_ACT[FIRST[f"fup{p}"] + 2 * i])
                        convolve(tmp[:, b % 2, :], padded[b % 2], [p_("ffn_conv_w", 22 * k + b) for k in range(3)],
                                 conv_ready)
                        finish(b, p, i)
                        b += 1
                    if p:
                        store(FIRST[f"fdown{p - 1}"], p == 1)
                store(FIRST[f"fdown{len(parts) - 1}"], False)

            dve.memset(eps[:, 0:1], RMS_EPS)
            dve.memset(eps[:, 1:2], GN_EPS)
            dve.wait_ge(inputs_in, 48)
            meet()
            norm_split(x, "norm_mix_pre", xh, xl)
            meet()
            mlstm()
            meet()
            mixer_out("mlstm_norm", M_O, 0)
            short_conv()
            meet()
            hgrn()
            meet()
            mixer_out("hgrn_norm", H_G, 6)
            meet()
            dve.wait_ge(tables_in, 16)
            take(values_free, 1)
            for b in range(2):
                part_heads(proj1[:, A_K + b, :], proj1[:, A_V + b, :])
            attention(attention_items("moba"))
            meet()
            store(FIRST["mix"], True)
            meet()
            norm_add("norm_mix_post")
            meet()
            norm_split(mem_raw, "mem_norm", mem_h, mem_l, M, dve_step)
            meet()
            norm_split(x, "norm_cross_pre", xh, xl)
            meet()
            attention(attention_items("cross"))
            meet()
            store(FIRST["co"], True)
            meet()
            norm_add("norm_cross_post")
            meet()
            norm_split(x, "norm_ffn_pre", xh, xl)
            gated(FF1_PARTS)
            meet()
            norm_add("norm_ffn_post")
            meet()
            norm_split(x, "attn_norm_e_2", xh, xl)
            meet()
            head_norm([proj2[:, E_AQ + b, :] for b in range(5)], [p_("qa", 0)] * 4 + [p_("ka", 0)])
            head_norm([proj2[:, E_BQ + b, :] for b in range(8)], [p_("qb", 0)] * 4 + [p_("kb", 0)] * 4)
            dve.wait_ge(tables_in, 64)
            part_heads(proj2[:, E_AK, :], proj2[:, E_AV, :])
            for b in range(4):
                part_heads(proj2[:, E_BK + b, :], proj2[:, E_BV + b, :])
            sinks = par[:, PCOL["sink"]:PCOL["sink"] + 8]
            done(dve.tensor_scalar(sinks, sinks, -1.0, None, ALU.mult))
            meet()
            attention(attention_items("window"))
            attention(attention_items("neighbour"))
            meet()
            add(FIRST["even_out"])
            meet()
            norm_split(x, "mlp0", xh, xl)
            mlp("m", FF2_PARTS)
            meet()
            norm_split(x, "ret_norm_o_2", xh, xl)
            take(gate_fun)
            dec = par[:, PCOL["dec_f"]:PCOL["dec_f"] + 16]
            done(dve.tensor_scalar(small[:, 16:32], dec, 0.0, None, ALU.min))
            done(dve.tensor_tensor(small[:, 48:64], small[:, 16:32], small[:, 32:48], ALU.subtract))
            dve.wait_ge(tables_in, 80)
            for half in range(2):
                for h in range(4 * half, 4 * half + 4):
                    if h % 4:
                        retention(h - 1)
                retention(4 * half + 3)
                add(FIRST[f"odd_out{half}"])
            meet()
            norm_split(x, "mlp1", xh, xl)
            mlp("n", FF2_PARTS)
            meet()


def _blocks(w, nkt=KT, start=0):
    k, m = w.shape
    a = w[start * P:(start + nkt) * P].reshape(nkt, P, m // P, P).transpose(2, 1, 0, 3).reshape(m // P, P, nkt * P)
    return np.pad(a, ((0, 0), (0, 0), (0, KT * P - nkt * P)))


def _stream(inp):
    units = []
    w = inp["w_in"][0]
    cuts = np.cumsum([G] * 4 + [4, 4] + [G] * 10)
    cols = np.split(w, cuts[:-1], axis=1)
    gates = np.zeros((D, P), w.dtype)
    gates[:, 0:4], gates[:, 32:36] = cols[4], cols[5]
    units.append(_blocks(gates))
    units.append(_blocks(np.concatenate(cols[0:4] + cols[6:16], axis=1)))
    units.append(_blocks(inp["w_mix_out"][0]))
    for name in ("w_cq", "w_ck", "w_cv"):
        units.append(_blocks(inp[name][0]))
    units.append(_blocks(inp["w_co"][0], 4))

    def parts(sizes, ups, down):
        at = np.concatenate([[0], np.cumsum(sizes)])

        def up(p):
            u = [_blocks(a[:, at[p] * P:at[p + 1] * P]) for a in ups]
            units.append(np.stack(u, 1).reshape(-1, P, KT * P))

        up(0)
        for p in range(len(sizes)):
            if p + 1 < len(sizes):
                up(p + 1)
            units.append(_blocks(down, sizes[p], at[p]))

    f = inp["w_ffn_in"][0]
    parts(FF1_PARTS, [f[:, :FF1], f[:, FF1:]], inp["w_ffn_out"][0])
    pair = np.array([0, 4, 1, 5, 2, 6, 3, 7])
    e = inp["w_in_e_2"][0]
    units.append(_blocks(np.concatenate([e[:, :512].reshape(D, 8, HD)[:, pair].reshape(D, 512), e[:, 512:]], 1)))
    e = inp["w_out_e_2"][0]
    units.append(_blocks(np.concatenate([e[:512].reshape(8, HD, D)[pair].reshape(512, D), e[512:]], 0)))
    parts(FF2_PARTS, [inp["w_mlp_in_2"][0]], inp["w_mlp_out_2"][0])
    o = inp["w_in_o_2"][0]
    q, k, v, g = np.split(o, [D, 2 * D, 4 * D], axis=1)
    for half in range(2):
        heads = []
        for h in range(4 * half, 4 * half + 4):
            heads += [q[:, h * P:(h + 1) * P], k[:, h * P:(h + 1) * P], v[:, h * G:(h + 1) * G],
                      g[:, h * G:(h + 1) * G]]
        units.append(_blocks(np.concatenate(heads, 1)))
        units.append(_blocks(inp["w_out_o_2"][0], KT, half * KT))
    parts(FF2_PARTS, [inp["w_mlp_in_2"][1]], inp["w_mlp_out_2"][1])
    out = np.concatenate(units)
    assert out.shape == (UNITS, P, KT * P), out.shape
    return out.reshape(UNITS * P, KT * P)


def _parameters(inp):
    par = np.zeros((P, PARAMS), np.float32)

    def put(name, a):
        par[:, PCOL[name]:PCOL[name] + a.shape[0]] = a.T

    for name in ("norm_mix_pre", "norm_mix_post", "mem_norm", "norm_cross_pre", "norm_cross_post", "norm_ffn_pre",
                 "norm_ffn_post", "attn_norm_e_2", "ret_norm_o_2", "mlstm_norm", "hgrn_norm"):
        put(name, inp[name][0].reshape(-1, P))
    put("mlp0", inp["mlp_norm_2"][0].reshape(-1, P))
    put("mlp1", inp["mlp_norm_2"][1].reshape(-1, P))
    b = inp["b_in"][0]
    put("b_in", np.concatenate([b[:4 * G], b[4 * G + 8:]]).reshape(-1, P))
    par[0:4, PCOL["b_gates"]] = b[4 * G:4 * G + 4]
    par[32:36, PCOL["b_gates"]] = b[4 * G + 4:4 * G + 8]
    put("hgrn_lb", inp["hgrn_lb_logits"][0].reshape(-1, P))
    put("sconv_w", inp["sconv_w"][0].reshape(-1, P))
    put("ffn_conv_w", inp["ffn_conv_w"][0].reshape(-1, P))
    put("ffn_conv_b", inp["ffn_conv_b"][0].reshape(-1, P))
    for name, src in (("qa", "q_norm_a_2"), ("ka", "k_norm_a_2"), ("qb", "q_norm_b_2"), ("kb", "k_norm_b_2")):
        put(name, np.tile(inp[src][0], 2).reshape(1, P))
    sink = inp["sink_a_2"][0][[0, 4, 1, 5, 2, 6, 3, 7]]
    put("sink", np.broadcast_to(sink[:, None], (8, P)))
    put("dec_f", np.broadcast_to(inp["decay_fwd_o_2"][0][:, None], (8, P)))
    put("dec_b", np.broadcast_to(inp["decay_bwd_o_2"][0][:, None], (8, P)))
    put("gn", inp["ret_gn_o_2"][0].reshape(-1, P))
    return par


def _moba_bias(rel_bias):
    dist = np.arange(P)[:, None] + 3 * P - np.arange(N)[None, :]
    n = np.maximum(dist, 0)
    large = 16 + (np.log(np.maximum(n, 1).astype(np.float32) / np.float32(16)) / np.float32(np.log(8.0))
                  * np.float32(16)).astype(np.int32)
    bucket = np.where(n < 16, n, np.minimum(large, 31))
    out = np.where((dist >= 0)[:, :, None], rel_bias[bucket], np.float32(NEG))
    return np.ascontiguousarray(out.transpose(0, 2, 1)).reshape(P, 4 * N)


def _na_bias(rpb):
    q = np.arange(P)
    out = []
    for t, lo, hi in ((0, 0, 2), (1, 0, 3), (3, 2, 4)):
        k = np.arange(lo * P, hi * P)
        qc, qr, kc, kr = 16 * t + q // 8, q % 8, k // 8, k % 8
        start = np.clip(qc - 8, 0, 48)
        valid = (kc[None] >= start[:, None]) & (kc[None] < start[:, None] + 16)
        col = np.clip(kc[None] - qc[:, None] + 15, 0, 30)
        row = kr[None] - qr[:, None] + 7
        out.append(np.where(valid[None], rpb[:, row, col], np.float32(NEG)).transpose(1, 0, 2).reshape(P, -1))
    return np.concatenate(out, 1)


def _feature_major(a):
    return np.ascontiguousarray(a.T.reshape(KT, P, -1).transpose(1, 0, 2)).reshape(P, -1)


def kernel(**inputs):
    import concourse.bacc as bacc
    from concourse.bass_utils import run_bass_kernel_spmd

    inp = {k: np.asarray(v) for k, v in inputs.items()}
    arrays = {
        "x_in": _feature_major(inp["x"][0]),
        "mem_in": _feature_major(inp["mem"][0]),
        "w_in": _stream(inp),
        "par_in": _parameters(inp),
        "con_in": _constants(),
        "moba_in": _moba_bias(inp["rel_bias"]),
        "alibi_in": _alibi(),
        "na_in": _na_bias(inp["rpb_b_2"][0]),
        "dist_in": _distances(),
    }
    nc = bacc.Bacc("TRN2", target_bir_lowering=False, num_devices=1)
    args = [nc.dram_tensor(k, a.shape, F32, kind="ExternalInput").ap() for k, a in arrays.items()]
    out = nc.dram_tensor("out", (P, KT * N), F32, kind="ExternalOutput").ap()
    args[0] = args[0].rearrange("p (b n) -> p b n", n=N)
    build(nc, *args, out.rearrange("p (b n) -> p b n", n=N))
    got = run_bass_kernel_spmd(nc, [arrays], core_ids=[0]).results[0]["out"]
    return np.ascontiguousarray(got.reshape(P, KT, N).transpose(2, 1, 0)).reshape(1, N, D)
```

```python
from contextlib import ExitStack

import numpy as np
import concourse.bass as bass
from concourse import mybir

F32 = mybir.dt.float32
F32R = mybir.dt.float32r
U32 = mybir.dt.uint32
ALU = mybir.AluOpType
ACT = mybir.ActivationFunctionType
AX_X = mybir.AxisListType.X
AX_XY = mybir.AxisListType.XY

P = 128
D = 1024
KT = D // P
N = 512
T = N // P
M = 256
HD = 64
G = 256
FF1 = 2816
FF2 = 4096
NEG = -1.0e30
LEAST = -3.0e38
RMS_EPS = 1e-6
GN_EPS = 1e-5

U_IN = 1 + 14 * 2
U_MIX = KT
U_CO = KT
FF1_PARTS = (8, 8, 6)
FF2_PARTS = (8, 8, 8, 8)
U_EVEN_IN = 18
U_EVEN_OUT = KT
U_HEAD = 6
RH = 8

ORDER = []
ORDER.append(("in", U_IN))
ORDER.append(("mix", U_MIX))
ORDER.append(("cross_kv", 8))
ORDER.append(("cross_q", 4))
ORDER.append(("co", U_CO))


def _parts(name, parts, up):
    out = [(f"{name}up0", up * parts[0])]
    for p in range(len(parts)):
        if p + 1 < len(parts):
            out.append((f"{name}up{p + 1}", up * parts[p + 1]))
        out.append((f"{name}down{p}", KT))
    return out


ORDER += _parts("f", FF1_PARTS, 2)
ORDER += [("even_in", U_EVEN_IN), ("even_out", U_EVEN_OUT)]
ORDER += _parts("m", FF2_PARTS, 1)
ORDER += [("odd_in0", 4 * U_HEAD), ("odd_out0", KT), ("odd_in1", 4 * U_HEAD), ("odd_out1", KT)]
ORDER += _parts("n", FF2_PARTS, 1)
FIRST = {}
_n = 0
for _name, _count in ORDER:
    FIRST[_name] = _n
    _n += _count
UNITS = _n
COUNT = dict(ORDER)

KV_BLOCKS = ((), (), (0,), (1, 2), (3,), (4, 5), (6,), (7,))

RING = 4
FILL_START, FILL_LEVELS, FILL_NORM, FILL_MLSTM = 3, (0, 1, 2, 3, 4, 5, 6), 0, 3
W_IN_P = 28
FIRST_BLOCKS = tuple(range(20, 28))
LATER_BLOCKS = tuple(range(0, 20))
assert FILL_START + 2 * len(FILL_LEVELS) + 2 * FILL_NORM + FILL_MLSTM == len(LATER_BLOCKS)

PCOL = {}
_c = 0
for _name, _w in (("norm_mix_pre", 8), ("norm_mix_post", 8), ("mem_norm", 8), ("norm_cross_pre", 8),
                  ("norm_cross_post", 8), ("norm_ffn_pre", 8), ("norm_ffn_post", 8), ("attn_norm_e_2", 8),
                  ("mlp0", 8), ("ret_norm_o_2", 8), ("mlp1", 8), ("b_in", 28), ("b_gates", 1),
                  ("mlstm_norm", 2), ("hgrn_norm", 2), ("hgrn_lb", 2), ("sconv_w", 6),
                  ("ffn_conv_w", 66), ("ffn_conv_b", 22), ("qa", 1), ("ka", 1), ("qb", 1), ("kb", 1),
                  ("sink", 8), ("dec_f", 8), ("dec_b", 8), ("gn", 16)):
    PCOL[_name] = _c
    _c += _w
PARAMS = _c

NSTAT = 16
LEVELS = (64, 32, 16, 8, 4, 2, 1)
CCOL = {}
_c = 0
for _name, _w in (("ident", P), ("ones", P), ("stat", 2 * NSTAT), ("pair", 8 * P), ("row", 4 * P),
                  ("col", 8), ("tri", P), ("level", 8 * P), ("half", 2)):
    CCOL[_name] = _c
    _c += _w
CONSTS = _c


def _constants():
    c = np.zeros((P, CONSTS), np.float32)
    i = np.arange(P)

    def at(name, w):
        return c[:, CCOL[name]:CCOL[name] + w]

    at("ident", P)[:] = np.eye(P)
    at("ones", P)[:] = 1.0
    at("stat", 2 * NSTAT)[:HD, NSTAT] = 1.0
    at("stat", 2 * NSTAT)[HD:, NSTAT + 1] = 1.0
    for b in range(8):
        at("pair", 8 * P)[2 * b, b * P:b * P + HD] = 1.0
        at("pair", 8 * P)[2 * b + 1, b * P + HD:(b + 1) * P] = 1.0
    for h in range(4):
        at("row", 4 * P)[h, h * P:(h + 1) * P] = 1.0
    at("col", 8)[:, 4] = 1.0
    at("tri", P)[:] = i[None, :] >= i[:, None]
    for n, half in enumerate(LEVELS):
        seg = i // (2 * half)
        right = (i % (2 * half)) >= half
        at("level", 8 * P)[:, n * P:(n + 1) * P] = (
            (seg[:, None] == seg[None, :]) & ~right[:, None] & right[None, :])
    at("level", 8 * P)[:, 7 * P:] = np.eye(P)
    at("half", 2)[:HD, 0] = at("half", 2)[HD:, 1] = HD ** -0.5
    return c


def _alibi():
    q, k = np.arange(P)[:, None], np.arange(3 * P)[None, :]
    rel = k - P - q
    out = np.zeros((P, 8, 3 * P), np.float32)
    for b in range(4):
        for s in range(2):
            slope = 2.0 ** -(4 * s + b + 1.0)
            out[:, 2 * b + s] = np.where(np.abs(rel) <= P, -slope * np.abs(rel), NEG)
    return out.reshape(P, -1)


def _distances():
    d = np.arange(7 * P)[None, :] - 3 * P - np.arange(P)[:, None]
    return np.concatenate([np.maximum(d, 0), np.maximum(-d, 0)], 1).astype(np.float32)


def build(nc, x_in, mem_in, w_in, par_in, con_in, moba_in, alibi_in, na_in, dist_in, out):
    with ExitStack() as ctx:
        def sb(name, shape, dt=F32):
            return ctx.enter_context(nc.sbuf_tensor(name, shape, dt))

        def sem(name):
            return ctx.enter_context(nc.semaphore(name))

        gemm_ps = ctx.enter_context(nc.psum_tensor("gemm_ps", [P, 2, N], F32))
        score_ps = ctx.enter_context(nc.psum_tensor("score_ps", [P, 2, N], F32))
        turn_ps = ctx.enter_context(nc.psum_tensor("turn_ps", [P, 2, N], F32))
        out_ps = ctx.enter_context(nc.psum_tensor("out_ps", [P, 2, N], F32))

        x = sb("x", [P, KT, N])
        xh = sb("xh", [P, KT, N], F32R)
        xl = sb("xl", [P, KT, N], F32R)
        raw = sb("raw", [P, RING, KT * P])
        wh = sb("wh", [P, 2, KT * P], F32R)
        wl = sb("wl", [P, 2, KT * P], F32R)
        y_at = nc.sbuf_base
        y_all = sb("y_all", [P, (KT + 1) * N])
        y = y_all[:, :].rearrange("p (b n) -> p b n", n=N)
        y_r = nc.alloc_sbuf_tensor_at("y_r", [P, KT * N], F32R, offset=y_at)
        par = sb("par", [P, PARAMS])
        con = sb("con", [P, CONSTS])
        eps = sb("eps", [P, 4])
        unity = sb("unity", [P, 2])
        small = sb("small", [P, 64])
        sq = sb("sq", [P, 2, N])
        rstd = sb("rstd", [P, N])
        tmp = sb("tmp", [P, 2, N])
        ARENA = 43 * N
        arena_at = nc.sbuf_base
        arena = sb("arena", [P, ARENA])
        arena_r = nc.alloc_sbuf_tensor_at("arena_r", [P, ARENA], F32R, offset=arena_at)

        def region(first, blocks, dt=F32):
            a = (arena if dt is F32 else arena_r)[:, first * N:(first + blocks) * N]
            return a.rearrange("p (b n) -> p b n", n=N)

        def c_(name, w, p0=0, p1=P):
            return con[p0:p1, CCOL[name]:CCOL[name] + w]

        ident = c_("ident", P)
        ones = c_("ones", P)

        def p_(name, i, p0=0, p1=P):
            return par[p0:p1, PCOL[name] + i:PCOL[name] + i + 1]

        proj1 = region(0, W_IN_P)
        M_Q, M_K, M_V, M_O, C_B, C_C, C_H, A_Q, A_K, A_V, H_Q, H_F, H_I, H_G = range(0, W_IN_P, 2)
        edge = region(28, 4)
        edge_all = arena[:, 28 * N:32 * N]
        values1 = arena[:, 32 * N:34 * N].rearrange("p (t c) -> p t c", c=G)
        mixed = region(34, 2)
        gates = arena[:, 36 * N:37 * N]
        gate_a, gate_b, gate_g = (arena[:, (37 + k) * N:(38 + k) * N] for k in range(3))
        moba_bias = region(8, 4)
        level_kq = ((tmp[:, 0, :], tmp[:, 1, :], y[:, 8, :]), (sq[:, 0, :], sq[:, 1, :], arena[:, 42 * N:43 * N]))
        log_decay = region(40, 2)
        weights = (y_all[:, 0:4 * N], y_all[:, 4 * N:8 * N])

        def diagonal(w):
            return y_all[:, w * 4 * N:w * 4 * N + 5 * N].rearrange("p (j c) -> p j c", c=N + P)[:, :, 0:P]

        E_AQ, E_AK, E_AV, E_BQ, E_BK, E_BV = 0, 4, 5, 6, 10, 14
        proj2 = region(0, U_EVEN_IN)
        values_a = arena[:, 18 * N:19 * N].rearrange("p (t c) -> p t c", c=P)
        values_b = arena[:, 19 * N:23 * N].rearrange("p (t c) -> p t c", c=4 * P)
        alibi = arena[:, 23 * N:29 * N].rearrange("p (h k) -> p h k", h=8)
        na_all = arena[:, 29 * N:43 * N]
        na_bias = [na_all[:, 0:8 * 256].rearrange("p (h k) -> p h k", h=8),
                   na_all[:, 8 * 256:8 * 640].rearrange("p (h k) -> p h k", h=8),
                   na_all[:, 8 * 640:8 * 896].rearrange("p (h k) -> p h k", h=8)]
        na_bias = [na_bias[0], na_bias[1], na_bias[1], na_bias[2]]

        head_in = [region(6 * s, 6) for s in range(2)]
        values_r = arena[:, 12 * N:14 * N].rearrange("p (t c) -> p t c", c=G)
        decay = arena[:, 14 * N:14 * N + 7 * P]
        ret_w = region(16, 4)
        rstd_r = arena[:, 24 * N:25 * N]
        dist = arena[:, 20 * N:20 * N + 14 * P]
        ret_h, ret_l = region(26, 8, F32R), region(34, 8, F32R)
        mh, ml = y_r[:, :].rearrange("p (b n) -> p b n", n=N), region(32, 8, F32R)

        hidden = [(region(16 * s, 8, F32R), region(16 * s + 8, 8, F32R)) for s in range(2)]
        padded = [arena[:, 32 * N + s * (N + 4):32 * N + (s + 1) * (N + 4)] for s in range(2)]

        def later_unit(i):
            return FIRST["in"] + 1 + len(FIRST_BLOCKS) + i

        def ret_unit(h):
            return FIRST[f"odd_in{h // 4}"] + U_HEAD * (h % 4)

        def attention_items(kind):
            items = []
            if kind == "moba":
                for b in range(2):
                    for t in range(T):
                        for s in range(2):
                            nk = (t + 1) * P
                            r = slice(s * HD, (s + 1) * HD)
                            items.append(dict(
                                q=proj1[:, A_Q + b, t * P:(t + 1) * P], k=proj1[:, (A_V if s == 0 else A_K) + b, 0:nk], nk=nk,
                                bias=moba_bias[:, 2 * b + s, (3 - t) * P:4 * P], sink=None,
                                v=[values1[:, c, (2 * b + s) * HD:(2 * b + s + 1) * HD] for c in range(t + 1)],
                                rows=r, tile=t, group=b, last=t == T - 1 and s == 1, first=t == 0 and s == 0,
                                to=4 + b, turned=False))
            elif kind == "cross":
                for b in range(4):
                    for t in range(T):
                        items.append(dict(
                            q=cross_q[:, b, t * P:(t + 1) * P], k=cross_k[:, b, :], nk=M, bias=None,
                            sink=None, v=[cross_v[:, c, b * P:(b + 1) * P] for c in range(2)],
                            rows=slice(0, P), tile=t, group=b, last=t == T - 1, first=t == 0, to=b, turned=False))
            elif kind == "window":
                for b in range(4):
                    for t in range(T):
                        lo, hi = max(t - 1, 0), min(t + 2, T)
                        for s in range(2):
                            r = slice(s * HD, (s + 1) * HD)
                            items.append(dict(
                                q=proj2[:, E_AQ + b, t * P:(t + 1) * P], k=proj2[:, E_AV if s == 0 else E_AK, lo * P:hi * P],
                                nk=(hi - lo) * P, bias=alibi[:, 2 * b + s, (lo - t + 1) * P:(hi - t + 1) * P],
                                sink=p_("sink", 2 * b + s),
                                v=[values_a[:, c, s * HD:(s + 1) * HD] for c in range(lo, hi)],
                                rows=r, tile=t, group=b, last=t == T - 1 and s == 1, first=t == 0 and s == 0,
                                to=b, turned=False))
            else:
                for b in range(4):
                    for t in range(T):
                        lo, hi = max(t - 1, 0), min(t + 2, T)
                        for s in range(2):
                            r = slice(s * HD, (s + 1) * HD)
                            items.append(dict(
                                q=proj2[:, E_BQ + b, t * P:(t + 1) * P],
                                k=proj2[:, (E_BV if s == 0 else E_BK) + b, lo * P:hi * P],
                                nk=(hi - lo) * P, bias=na_bias[t][:, 2 * b + s, :],
                                sink=None,
                                v=[values_b[:, c, (2 * b + s) * HD:(2 * b + s + 1) * HD] for c in range(lo, hi)],
                                rows=r, tile=t, group=b, last=t == T - 1 and s == 1, first=t == 0 and s == 0,
                                to=4 + b, turned=True))
            return items

        cross_q = region(4, 4)
        cross_k = arena[:, 8 * N:10 * N].rearrange("p (b m) -> p b m", m=M)
        cross_vf = arena[:, 10 * N:12 * N].rearrange("p (b m) -> p b m", m=M)
        cross_v = arena[:, 13 * N:15 * N].rearrange("p (t c) -> p t c", c=N)
        mem_raw = arena[:, 0:4 * N].rearrange("p (b m) -> p b m", m=M)
        mem_h = arena_r[:, 24 * N:28 * N].rearrange("p (b m) -> p b m", m=M)
        mem_l = arena_r[:, 20 * N:24 * N].rearrange("p (b m) -> p b m", m=M)
        mem_rstd = arena[:, 12 * N:12 * N + M]

        roots = y[:, 4, :]

        inputs_in = sem("inputs_in")
        x_in_sem = [sem(f"x_in_{b}") for b in range(KT)]
        moba_table_in = sem("moba_table_in")
        memory_in = sem("memory_in")
        layer_tables_in = sem("layer_tables_in")
        distances_in = sem("distances_in")
        unit_in = [sem(f"unit_in{k}") for k in range(RING)]
        unity_set = sem("unity_set")
        high_split = sem("high_split")
        unit_split = sem("unit_split")
        unit_done = sem("unit_done")
        emptied = sem("emptied")
        block_ready = sem("block_ready")
        high_made = sem("high_made")
        proj_raw = sem("proj_raw")
        proj_ready = sem("proj_ready")
        act_step = sem("act_step")
        dve_step = sem("dve_step")
        at_pe, at_act, at_dve = sem("at_pe"), sem("at_act"), sem("at_dve")
        rhs_ready = sem("rhs_ready")
        square_ready = sem("square_ready")
        square_used = sem("square_used")
        std_ready = sem("std_ready")
        rows_ready = sem("rows_ready")
        spread_ready = sem("spread_ready")
        spread_used = sem("spread_used")
        turned_v = sem("turned_v")
        bias_added = sem("bias_added")
        conv_done = sem("conv_done")
        copied_v = sem("copied_v")
        values_free = sem("values_free")
        scores_ready = sem("scores_ready")
        scores_used = sem("scores_used")
        logits_ready = sem("logits_ready")
        exp_ready = sem("exp_ready")
        probs_ready = sem("probs_ready")
        probs_turned = sem("probs_turned")
        probs_copied = sem("probs_copied")
        keys_ready = sem("keys_ready")
        item_done = sem("item_done")
        high_ready = sem("high_ready")
        group_used = sem("group_used")
        gate_arg = sem("gate_arg")
        gate_fun = sem("gate_fun")
        gate_rows = sem("gate_rows")
        bound_ready = sem("bound_ready")
        bound_used = sem("bound_used")
        weights_ready = sem("weights_ready")
        weights_used = sem("weights_used")
        cols_turned = sem("cols_turned")
        cols_ready = sem("cols_ready")
        level_ready = sem("level_ready")
        far_ready = sem("far_ready")
        far_copied = sem("far_copied")
        ret_std = sem("ret_std")
        head_turned = sem("head_turned")
        mean_ready = sem("mean_ready")
        hidden_raw = sem("hidden_raw")
        head_done = sem("head_done")
        conv_ready = sem("conv_ready")
        out_done = sem("out_done")

        block = ctx.enter_context(nc.Block())

        def counter(eng):
            taken = {}

            def take(s, by=1):
                taken[s] = taken.get(s, 0) + by
                eng.wait_ge(s, taken[s])
            return take, taken

        @block.sync
        def _(sp):
            sp.dma_start(par[:], par_in).then_inc(inputs_in, 16)
            sp.dma_start(x[:, 0, :], x_in[:, 0, :]).then_inc(x_in_sem[0], 16)
            sp.dma_start(x[:, 1, :], x_in[:, 1, :]).then_inc(x_in_sem[1], 16)
            sp.dma_start(con[:], con_in).then_inc(inputs_in, 16)
            for b in range(2, KT):
                sp.dma_start(x[:, b, :], x_in[:, b, :]).then_inc(x_in_sem[b], 16)
            for k in range(RING):
                sp.dma_start(raw[:, k, :], w_in[k * P:(k + 1) * P, :]).then_inc(unit_in[k], 16)
            with sp.Fori(1, UNITS // RING) as i:
                for k in range(RING):
                    sp.wait_ge(unit_split, RING * i + (k + 1 - RING))
                    sp.dma_start(raw[:, k, :], w_in[bass.ds((RING * i + k) * P, P), :]).then_inc(unit_in[k], 16)
            for n in range(UNITS // RING * RING, UNITS):
                sp.wait_ge(unit_split, n + 1 - RING)
                sp.dma_start(raw[:, n % RING, :], w_in[n * P:(n + 1) * P, :]).then_inc(unit_in[n % RING], 16)

        @block.gpsimd
        def _(pool):
            def split(k, landed, done, high):
                pool.wait_ge(unit_in[k], landed)
                if done is not None:
                    pool.wait_ge(unit_done, done)
                pool.tensor_tensor(wh[:, k % 2, :], raw[:, k, :], unity[:, 0:1].broadcast_to([P, KT * P]),
                                   ALU.mult).then_inc(high_split, 1)
                pool.wait_ge(high_split, high)
                pool.tensor_tensor(wl[:, k % 2, :], raw[:, k, :], wh[:, k % 2, :].bitcast(F32),
                                   ALU.subtract).then_inc(unit_split, 1)

            pool.memset(unity[:, :], 1.0).then_inc(unity_set, 1)
            pool.wait_ge(unity_set, 1)
            for n in range(RING):
                split(n, 16, None if n < 2 else n - 1, n + 1)
            with pool.Fori(1, UNITS // RING) as i:
                for k in range(RING):
                    split(k, 16 * i + 16, RING * i + k - 1, RING * i + k + 1)
            for n in range(UNITS // RING * RING, UNITS):
                split(n % RING, 16 * (n // RING + 1), n - 1, n + 1)

        @block.tensor
        def _(pe):
            take, taken = counter(pe)
            meetings, blocks_split = [0], [0]

            def meet():
                meetings[0] += 1
                pe.drain().then_inc(at_pe, 1)
                pe.wait_ge(at_act, meetings[0])
                pe.wait_ge(at_dve, meetings[0])

            def products(n, nkt, h, l, width, fresh=None, summing=False):
                o = gemm_ps[:, n % 2, 0:width]
                for kt in range(nkt):
                    if fresh is not None:
                        pe.wait_ge(rhs_ready, fresh + kt + 1)
                    w = slice(kt * P, (kt + 1) * P)
                    pe.matmul(o, wh[:, n % 2, w], h[:, kt, 0:width], start=(kt == 0), stop=False)
                    pe.matmul(o, wh[:, n % 2, w], l[:, kt, 0:width], start=False, stop=False)
                    last = pe.matmul(o, wl[:, n % 2, w], h[:, kt, 0:width], start=False, stop=(kt == nkt - 1))
                    if summing and kt < KT - 1:
                        column_sum(kt)
                last.then_inc(unit_done, 1)
                if summing:
                    column_sum(KT - 1)

            def unit(n, h, l, nkt=KT, width=N):
                pe.wait_ge(unit_split, n + 1)
                if n >= 2:
                    pe.wait_ge(emptied, n - 1)
                products(n, nkt, h, l, width)

            def units(n0, count, h, l, nkt=KT, width=N, fresh=False, summing=False):
                if fresh:
                    pe.wait_ge(unit_split, n0 + 1)
                    if n0 >= 2:
                        pe.wait_ge(emptied, n0 - 1)
                    products(n0, nkt, h, l, width, blocks_split[0], summing)
                    blocks_split[0] += nkt
                    n0, count = n0 + 1, count - 1
                first, pairs = n0, count // 2
                if first < 2:
                    unit(first, h, l, nkt, width)
                    first, pairs = first + 1, (count - 1) // 2
                if pairs:
                    with pe.Fori(0, pairs) as i:
                        for n in (first, first + 1):
                            pe.wait_ge(unit_split, 2 * i + (n + 1))
                            pe.wait_ge(emptied, 2 * i + (n - 1))
                            products(n, nkt, h, l, width)
                for n in range(first + 2 * pairs, n0 + count):
                    unit(n, h, l, nkt, width)

            def column_sum(b, width=N, bank=0):
                take(square_ready)
                pe.matmul(turn_ps[:, bank, 0:width], ones, sq[:, b % 2, 0:width], start=(b == 0),
                          stop=(b == KT - 1)).then_inc(square_used, 1)

            def units_summed(n0, h, l, nkt=KT, fresh=False):
                for b in range(KT):
                    if fresh and b == 0:
                        units(n0, 1, h, l, nkt, fresh=True)
                    else:
                        unit(n0 + b, h, l, nkt)
                    if b >= 2:
                        column_sum(b - 2)
                column_sum(KT - 2)
                column_sum(KT - 1)

            def head_norm(nb):
                heads = 2 * nb
                for b in range(nb):
                    take(square_ready)
                    w = CCOL["stat"] + NSTAT - 2 * b
                    pe.matmul(turn_ps[0:heads, 0, :], con[:, w:w + heads], sq[:, b % 2, :], start=(b == 0),
                              stop=(b == nb - 1)).then_inc(square_used, 1)
                spread(nb, roots[0:heads, :])

            def spread(nb, rows):
                take(rows_ready)
                for b in range(nb):
                    if b >= 2:
                        take(spread_used)
                    w = CCOL["pair"] + b * P
                    pe.matmul(score_ps[:, b % 2, :], con[0:rows.shape[0], w:w + P], rows, start=True,
                              stop=True).then_inc(spread_ready, 1)
                take(spread_used, min(2, nb))

            def turn_values(blocks):
                for i, a in enumerate(blocks):
                    if i >= 2:
                        take(copied_v)
                    for t in range(a.shape[1] // P):
                        m = pe.transpose(turn_ps[:, i % 2, t * P:(t + 1) * P], a[:, t * P:(t + 1) * P], ident)
                    m.then_inc(turned_v, 1)
                take(copied_v, min(2, len(blocks)))

            def attention(items, between=lambda i: None):
                groups0 = taken.get(group_used, 0)

                def scores(i, it):
                    if i >= 2:
                        take(exp_ready if it["bias"] is None else scores_used)
                    pe.matmul(score_ps[:, i % 2, 0:it["nk"]], it["q"], it["k"], start=True,
                              stop=True).then_inc(scores_ready, 1)

                def turned(i, it):
                    take(probs_ready)
                    for c in range(it["nk"] // P):
                        m = pe.transpose(turn_ps[:, i % 2, c * P:(c + 1) * P], y[:, i % 3, c * P:(c + 1) * P],
                                         ident)
                    m.then_inc(probs_turned, 1)

                def values(i, it):
                    take(probs_copied)
                    if it["first"] and it["group"] >= 2:
                        pe.wait_ge(group_used, groups0 + it["group"] - 1)
                    o = out_ps[it["rows"], it["group"] % 2, it["tile"] * P:(it["tile"] + 1) * P]
                    chunks = it["nk"] // P
                    for c in range(chunks):
                        m = pe.matmul(o, it["v"][c], y[:, 3 + i % 2, c * P:(c + 1) * P], start=(c == 0),
                                      stop=(c == chunks - 1))
                    m.then_inc(item_done, 1)

                n = len(items)
                for i in range(n + 3):
                    if i < n:
                        scores(i, items[i])
                    if 2 <= i < n + 2:
                        turned(i - 2, items[i - 2])
                    if i >= 3:
                        values(i - 3, items[i - 3])
                    between(i)
                take(exp_ready if items[0]["bias"] is None else scores_used, 2)
                if items[0]["bias"] is not None:
                    taken[exp_ready] = taken.get(exp_ready, 0) + n
                taken[group_used] = groups0 + items[-1]["group"] + 1

            def weighted(h, w, j, **flags):
                return pe.matmul(out_ps[(h % 2) * HD:(h % 2 + 1) * HD, h // 2, j * P:N],
                                 values1[:, j, h * HD:(h + 1) * HD], w[:, j * N + j * P:(j + 1) * N], **flags)

            filled = [0]

            def fill(count=1):
                for _ in range(count):
                    unit(later_unit(filled[0]), xh, xl)
                    filled[0] += 1

            def mlstm():
                turn_values([proj1[:, M_V, :], proj1[:, M_V + 1, :]])
                fill()
                take(gate_rows)
                for t in range(T):
                    m = pe.transpose(turn_ps[:, 0, 4 * t:4 * t + 4], gate_b[0:4, t * P:(t + 1) * P], ident[0:4, 0:4])
                m.then_inc(cols_turned, 1)
                take(cols_ready)
                take(gate_rows)
                take(keys_ready, 2)
                for h in range(4):
                    w = weights[h % 2]
                    kb = (M_K if h % 2 else M_V) + h // 2
                    if h >= 1:
                        take(bound_used)
                    pe.matmul(turn_ps[:, 0, :], con[0:4, CCOL["row"] + h * P:CCOL["row"] + (h + 1) * P],
                              gate_a[0:4, :], start=True, stop=True).then_inc(bound_ready, 1)
                    if h < FILL_MLSTM - 1:
                        fill()
                    for j in range(T + 2):
                        if j < T:
                            if h > 0 or j >= 2:
                                take(scores_used)
                            pe.matmul(score_ps[:, j % 2, j * P:N], proj1[:, kb, j * P:(j + 1) * P],
                                      proj1[:, M_Q + h // 2, j * P:N], start=True, stop=True).then_inc(scores_ready, 1)
                        if j >= 2:
                            k = j - 2
                            take(weights_ready)
                            weighted(h, w, k, start=(k == 0), stop=(k == T - 1))
                            m = pe.matmul(turn_ps[0:4, 1, k * P:N], con[:, CCOL["col"] + 4 - h:CCOL["col"] + 8 - h],
                                          w[:, k * N + k * P:(k + 1) * N], start=(h == 0 and k == 0),
                                          stop=(h == 3 and k == T - 1), skip_group_check=True)
                    m.then_inc(weights_used, 1)
                take(scores_used, 2)
                take(bound_used)
                spread(2, gate_b[0:4, :])

            def hgrn():
                turn_values([proj1[:, H_I, :], proj1[:, H_I + 1, :]])
                fill(FILL_START)
                for b in range(2):
                    take(level_ready)
                    q1, q2, q3 = level_kq[1][2], edge[:, 0, :], edge[:, 1, :]
                    for s in range(2):
                        for j, i, q in ((0, 1, q1), (1, 2, q1), (2, 3, q1), (0, 2, q2), (1, 3, q2), (0, 3, q3)):
                            bank, col = (0, i * P) if j == 0 else (1, (i if j == 1 else 0) * P)
                            m = pe.matmul(turn_ps[:, bank, col:col + P], level_kq[1][s][:, j * P:(j + 1) * P],
                                          q[:, i * P:(i + 1) * P], start=True, stop=True)
                        m.then_inc(far_ready, 1)
                        take(far_copied)
                    for lev in range(len(LEVELS) + 1):
                        take(level_ready)
                        for s in range(2):
                            kk, qq = level_kq[lev % 2][s], level_kq[lev % 2][2]
                            if lev:
                                take(scores_used)
                            for j in range(T):
                                t = slice(j * P, (j + 1) * P)
                                m = pe.matmul(score_ps[:, s, t], kk[:, t], qq[:, t], start=True, stop=True)
                            m.then_inc(scores_ready, 1)
                        if lev in FILL_LEVELS:
                            fill()
                    take(scores_used, 2)
                    for s in range(2):
                        for j in range(T):
                            m = weighted(2 * b + s, weights[s], j, start=(j == 0), stop=(j == T - 1))
                    m.then_inc(weights_used, 1)

            def retention(h, s):
                q, k, v0, v1 = (head_in[h % 2][:, b, :] for b in range(4))

                def scores(j):
                    pe.matmul(score_ps[:, j % 2, :], k[:, j * P:(j + 1) * P], q, start=True,
                              stop=True).then_inc(scores_ready, 1)

                def values(j):
                    for c in range(2):
                        m = pe.matmul(out_ps[:, c, :], values_r[:, j, c * P:(c + 1) * P], ret_w[:, j, :],
                                      start=(j == 0), stop=(j == T - 1))
                    if j == T - 1:
                        m.then_inc(weights_used, 1)

                if s == 0:
                    pe.wait_ge(emptied, ret_unit(h) + 4)
                    if h:
                        take(ret_std)
                    for i, a in enumerate((v0, v1)):
                        for t in range(T):
                            m = pe.transpose(turn_ps[:, i, t * P:(t + 1) * P], a[:, t * P:(t + 1) * P], ident)
                    m.then_inc(head_turned, 1)
                    scores(0)
                    scores(1)
                elif s < 3:
                    take(scores_used)
                    scores(s + 1)
                    if s == 1:
                        take(copied_v)
                        if h:
                            take(head_done)
                    values(s - 1)
                elif s == 3:
                    take(scores_used, 2)
                    values(2)
                    values(3)
                elif s == 4:
                    for c in range(2):
                        take(square_ready)
                        pe.matmul(turn_ps[:, 0, :], ones, sq[:, c, :], start=(c == 0),
                                  stop=(c == 1)).then_inc(square_used, 1)

            def mlp(name, parts, up, h, l):
                for p in range(len(parts)):
                    units(FIRST[f"{name}up{p}"], up * parts[p], h, l)
                    if p:
                        units(FIRST[f"{name}down{p - 1}"], KT, *hidden[(p - 1) % 2], nkt=parts[p - 1], fresh=True)

            pe.wait_ge(inputs_in, 32)
            meet()
            units(FIRST["in"], 1 + len(FIRST_BLOCKS), xh, xl, fresh=True, summing=True)
            meet()
            hgrn()
            meet()
            fill(FILL_NORM)
            head_norm(2)
            meet()
            mlstm()
            meet()
            fill(FILL_NORM)
            head_norm(2)
            meet()
            turn_values([proj1[:, A_V, :], proj1[:, A_V + 1, :]])
            take(keys_ready, 2)
            attention(attention_items("moba"))
            meet()
            unit(FIRST["mix"], xh, xl)
            unit(FIRST["mix"] + 1, xh, xl)
            for kt in range(KT):
                column_sum(kt, M, 1)
            for b in range(2, KT):
                unit(FIRST["mix"] + b, xh, xl)
                column_sum(b - 2)
            column_sum(KT - 2)
            column_sum(KT - 1)
            for u in range(8):
                unit(FIRST["cross_kv"] + u, mem_h, mem_l, width=M)
                for b in KV_BLOCKS[u]:
                    column_sum(b)
            units(FIRST["cross_q"], 4, xh, xl, fresh=True)
            meet()
            turn_values([cross_vf[:, b, :] for b in range(4)])
            attention(attention_items("cross"))
            meet()
            units_summed(FIRST["co"], xh, xl, nkt=4)
            units(FIRST["fup0"], 1, xh, xl, fresh=True, summing=True)
            FIRST_LEFT = 2 * FF1_PARTS[0] - 1
            units(FIRST["fup0"] + 1, FIRST_LEFT, xh, xl)
            for p in (1, 2):
                units(FIRST[f"fup{p}"], 2 * FF1_PARTS[p], xh, xl)
                units(FIRST[f"fdown{p - 1}"], KT, *hidden[(p - 1) % 2], nkt=FF1_PARTS[p - 1], fresh=True)
            units_summed(FIRST["fdown2"], *hidden[0], nkt=FF1_PARTS[2], fresh=True)
            units(FIRST["even_in"], 6, xh, xl, fresh=True, summing=True)
            pe.wait_ge(emptied, FIRST["even_in"] + 6)
            turn_values([proj2[:, E_AV, :]])
            head_norm(5)
            take(keys_ready)

            def neighbour_unit(i):
                if i % 3 == 1 and i // 3 < 12:
                    unit(FIRST["even_in"] + 6 + i // 3, xh, xl)
            attention(attention_items("window"), neighbour_unit)
            meet()
            turn_values([proj2[:, E_BV + b, :] for b in range(4)])
            head_norm(8)
            take(keys_ready, 4)
            meet()
            attention(attention_items("neighbour"))
            meet()
            units_summed(FIRST["even_out"], xh, xl)
            units(FIRST["mup0"], 1, mh, ml, fresh=True)
            units(FIRST["mup0"] + 1, 7, mh, ml)
            for p in (1, 2, 3):
                units(FIRST[f"mup{p}"], 8, mh, ml)
                units(FIRST[f"mdown{p - 1}"], KT, *hidden[(p - 1) % 2], fresh=True)
            units_summed(FIRST["mdown3"], *hidden[1], fresh=True)
            for half in range(2):
                for h in range(4 * half, 4 * half + 4):
                    for u in range(U_HEAD):
                        if h == 0 and u == 0:
                            units(ret_unit(0), 1, xh, xl, fresh=True)
                        else:
                            unit(ret_unit(h) + u, xh, xl)
                        if h % 4:
                            retention(h - 1, u)
                for s in range(U_HEAD):
                    retention(4 * half + 3, s)
                if half:
                    units_summed(FIRST["odd_out1"], ret_h, ret_l, fresh=True)
                else:
                    units(FIRST["odd_out0"], KT, ret_h, ret_l, fresh=True)
            take(ret_std)
            take(head_done)
            units(FIRST["nup0"], 8, xh, xl, fresh=True)
            for p in (1, 2, 3):
                units(FIRST[f"nup{p}"], 8, xh, xl)
                units(FIRST[f"ndown{p - 1}"], KT, *hidden[(p - 1) % 2], fresh=True)
            units(FIRST["ndown3"], KT, *hidden[1], fresh=True)
            meet()

        @block.scalar
        def _(act):
            take, taken = counter(act)
            meetings, steps = [0], [0]

            def meet():
                meetings[0] += 1
                act.drain().then_inc(at_act, 1)
                act.wait_ge(at_pe, meetings[0])
                act.wait_ge(at_dve, meetings[0])

            def step(ins):
                steps[0] += 1
                ins.then_inc(act_step, 1)
                act.wait_ge(act_step, steps[0])

            def squares(src, nb, width=N):
                for b in range(nb):
                    if b >= 2:
                        take(square_used)
                    act.activation(sq[:, b % 2, 0:width], src[b], ACT.Square).then_inc(square_ready, 1)
                take(square_used, min(2, nb))

            def prepare(src, gain, h, ready=None, width=N, dst=None, n=KT):
                dst = rstd[:, 0:width] if dst is None else dst
                for b in range(n):
                    high_and_square(src, gain, h, b, ready, width)
                finish_norm(dst, width)

            def high_and_square(src, gain, h, b, ready=None, width=N):
                if ready is not None:
                    ready(b)
                if h is not None:
                    act.activation(h[:, b, 0:width], src[:, b, 0:width], ACT.Copy,
                                   scale=p_(gain, b)).then_inc(high_made, 1)
                if b >= 2:
                    take(square_used)
                act.activation(sq[:, b % 2, 0:width], src[:, b, 0:width], ACT.Square).then_inc(square_ready, 1)

            def finish_norm(dst, width=N, bank=0):
                take(square_used, 2)
                act.activation(dst, turn_ps[:, bank, 0:width], ACT.Sqrt, bias=eps[:, 0:1],
                               scale=1.0 / D).then_inc(std_ready, 1)

            def stored(n0):
                return lambda b: act.wait_ge(emptied, n0 + b + 1)

            def head_norm(src):
                squares(src, len(src))
                r = slice(0, 2 * len(src))
                act.activation(roots[r, :], turn_ps[r, 0, :], ACT.Sqrt, bias=eps[r, 0:1],
                               scale=1.0 / HD).then_inc(std_ready, 1)

            def copy_values(dst):
                for i, o in enumerate(dst):
                    take(turned_v)
                    w = o.shape[1] * P
                    act.activation(o, turn_ps[:, i % 2, 0:w].rearrange("p (t c) -> p t c", c=P),
                                   ACT.Identity).then_inc(copied_v, 1)

            def attention(items, whole=False):
                items0 = taken.get(item_done, 0)

                def exps(i, it):
                    take(logits_ready)
                    s, a = 8 * (i % 3), y[:, i % 3, 0:it["nk"]]
                    if it["sink"] is not None:
                        act.activation(small[:, s + 2:s + 3], it["sink"], ACT.Exp, bias=small[:, s:s + 1], scale=-1.0)
                    act.activation(a, score_ps[:, i % 2, 0:it["nk"]] if it["bias"] is None else a, ACT.Exp,
                                   bias=small[:, s:s + 1], accum_out=small[:, s + 1:s + 2]).then_inc(exp_ready, 1)

                def copies(i, it):
                    take(probs_turned)
                    if i >= 2:
                        act.wait_ge(item_done, items0 + i - 1)
                    act.activation(y[:, 3 + i % 2, 0:it["nk"]], turn_ps[:, i % 2, 0:it["nk"]],
                                   ACT.Identity).then_inc(probs_copied, 1)

                def outputs(i, it):
                    act.wait_ge(item_done, items0 + i + 1)
                    if whole:
                        act.activation(y[:, 5 + it["group"], :], out_ps[:, it["group"] % 2, :],
                                       ACT.Identity).then_inc(high_ready, 1)
                        return
                    o, a = xh[:, it["to"], :], out_ps[:, it["group"] % 2, :]
                    if it["turned"]:
                        o = o.rearrange("p (r c) -> p c r", r=8)
                        a = a.rearrange("p (c r) -> p c r", r=8)
                    act.activation(o, a, ACT.Identity).then_inc(high_ready, 1)

                n = len(items)
                for i in range(n + 4):
                    if i < n:
                        exps(i, items[i])
                    if 2 <= i < n + 2:
                        copies(i - 2, items[i - 2])
                    if i >= 4 and items[i - 4]["last"]:
                        outputs(i - 4, items[i - 4])
                taken[item_done] = items0 + n

            filled = [0]

            def add_bias(n, b):
                act.wait_ge(emptied, n + 1)
                act.activation(proj1[:, b, :], proj1[:, b, :], ACT.Identity,
                               bias=p_("b_in", b)).then_inc(bias_added, 1)

            def fill(count=1):
                for _ in range(count):
                    add_bias(later_unit(filled[0]), LATER_BLOCKS[filled[0]])
                    filled[0] += 1

            def mlstm():
                f = slice(32, 36)
                step(act.activation(gate_a[f, :], gates[f, :], ACT.Abs))
                step(act.activation(gate_a[f, :], gate_a[f, :], ACT.Exp, scale=-1.0))
                act.activation(gate_b[f, :], gate_a[f, :], ACT.Ln, bias=1.0).then_inc(gate_fun, 1)
                copy_values([values1[:, :, b * P:(b + 1) * P] for b in range(2)])
                act.drain().then_inc(values_free, 1)
                fill()
                take(cols_turned)
                act.activation(small[:, 32:48], turn_ps[:, 0, 0:16], ACT.Identity).then_inc(cols_ready, 1)
                take(gate_arg)
                step(act.activation(gates[0:4, :], gates[0:4, :], ACT.Exp, scale=-1.0))
                for h in range(4):
                    take(bound_used)
                    for j in range(T):
                        m = act.activation(edge[:, j, j * P:N], edge[:, j, j * P:N], ACT.Exp)
                    m.then_inc(gate_fun, 1)
                    if h < FILL_MLSTM - 1:
                        fill()
                take(weights_used, 4)
                act.activation(gate_g[0:4, :], turn_ps[0:4, 1, :], ACT.Abs).then_inc(gate_fun, 1)
                for b in range(2):
                    step(act.activation(proj1[:, M_O + b, :], proj1[:, M_O + b, :], ACT.Sigmoid))

            def hgrn():
                take(gate_arg)
                act.activation(small[:, 18:20], small[:, 16:18], ACT.Exp).then_inc(gate_fun, 1)
                for b in range(2):
                    act.activation(proj1[:, H_F + b, :], proj1[:, H_F + b, :], ACT.Sigmoid)
                    act.activation(proj1[:, H_Q + b, :], proj1[:, H_Q + b, :], ACT.Silu)
                    m = act.activation(proj1[:, H_G + b, :], proj1[:, H_G + b, :], ACT.Silu)
                m.then_inc(gate_fun, 1)
                copy_values([values1[:, :, b * P:(b + 1) * P] for b in range(2)])
                act.drain().then_inc(values_free, 1)
                take(gate_arg)
                for b in range(2):
                    m = act.activation(log_decay[:, b, :], proj1[:, H_F + b, :], ACT.Ln)
                m.then_inc(gate_fun, 1)
                fill(FILL_START)
                take(gate_arg)
                for b in range(2):
                    g = log_decay[:, b, :]
                    if b:
                        take(weights_used)
                    for j in range(T):
                        t = slice(j * P, (j + 1) * P)
                        act.activation(edge[:, 0, t], g[:, t], ACT.Exp, bias=g[:, (j + 1) * P - 1:(j + 1) * P],
                                       scale=-1.0)
                    act.activation(edge[:, 1, :], g, ACT.Exp)
                    act.activation(small[:, 24:28], g[:, P - 1:N:P], ACT.Exp).then_inc(gate_fun, 1)
                    for s in range(2):
                        take(far_ready)
                        w = weights[s]
                        act.activation(w[:, P:N], turn_ps[:, 0, P:N], ACT.Identity)
                        act.activation(w[:, N + 2 * P:2 * N], turn_ps[:, 1, 2 * P:N], ACT.Identity)
                        act.activation(w[:, 2 * N + 3 * P:3 * N], turn_ps[:, 1, 0:P],
                                       ACT.Identity).then_inc(far_copied, 1)
                    for lev in range(len(LEVELS)):
                        take(gate_arg)
                        act.activation(edge[:, 2, :], edge[:, 3, :], ACT.Exp).then_inc(gate_fun, 1)
                        if lev - 2 in FILL_LEVELS:
                            fill()
                    fill(sum(lev in FILL_LEVELS for lev in (5, 6)))
                take(weights_used)
                for b in range(2):
                    step(act.activation(mixed[:, b, :], out_ps[:, b, :], ACT.Identity))

            def retention(h, s):
                if s == 0:
                    take(head_turned)
                    take(mean_ready)
                    a = turn_ps[:, :, :].rearrange("p b (t c) -> p t b c", c=P)
                    for t in range(T):
                        m = act.activation(values_r[:, t, :].rearrange("p (b c) -> p b c", c=P), a[:, t],
                                           ACT.Identity, bias=small[:, 8 + t:9 + t])
                    m.then_inc(copied_v, 1)
                    take(gate_arg)
                    act.activation(decay, decay, ACT.Exp).then_inc(gate_fun, 1)
                elif s == 3:
                    take(weights_used)
                    for c in range(2):
                        act.activation(sq[:, c, :], out_ps[:, c, :], ACT.Square).then_inc(square_ready, 1)
                elif s == 4:
                    take(square_used, 2)
                    act.activation(rstd_r[:, :], turn_ps[:, 0, :], ACT.Sqrt, bias=eps[:, 1:2],
                                   scale=1.0 / G).then_inc(ret_std, 1)

            def mlp(name, p):
                for b in range(FF2_PARTS[p]):
                    n = FIRST[f"{name}up{p}"] + b
                    act.wait_ge(emptied, n + 1)
                    step(act.activation(sq[:, b % 2, :], tmp[:, b % 2, :], ACT.Square))
                    act.activation(hidden[p % 2][0][:, b, :], sq[:, b % 2, :], ACT.Copy).then_inc(hidden_raw, 1)

            def gated():
                for b in range(sum(FF1_PARTS)):
                    take(conv_ready)
                    act.activation(sq[:, b % 2, :], tmp[:, b % 2, :], ACT.Silu,
                                   bias=p_("ffn_conv_b", b)).then_inc(hidden_raw, 1)

            act.wait_ge(inputs_in, 32)
            meet()
            prepare(x, "norm_mix_pre", xh, lambda b: act.wait_ge(x_in_sem[b], 16))
            act.wait_ge(emptied, FIRST["in"] + 1)
            act.activation(gates[0:HD, :], gates[0:HD, :], ACT.Identity, bias=p_("b_gates", 0, 0, HD))
            for i, b in enumerate(FIRST_BLOCKS):
                add_bias(FIRST["in"] + 1 + i, b)
            meet()
            hgrn()
            meet()
            fill(FILL_NORM)
            head_norm([mixed[:, b, :] for b in range(2)])
            meet()
            mlstm()
            meet()
            act.dma_start(arena[:, 0:4 * N], mem_in).then_inc(memory_in, 16)
            fill(FILL_NORM)
            head_norm([mixed[:, b, :] for b in range(2)])
            take(conv_done)
            act.dma_start(arena[:, 8 * N:12 * N], moba_in).then_inc(moba_table_in, 16)
            meet()
            copy_values([values1[:, :, b * P:(b + 1) * P] for b in range(2)])
            act.drain().then_inc(values_free, 1)
            attention(attention_items("moba"))
            meet()
            act.wait_ge(memory_in, 16)
            for b in range(KT):
                high_and_square(mem_raw, "mem_norm", mem_h, b, width=M)
            finish_norm(mem_rstd, M, 1)
            prepare(y, None, None, stored(FIRST["mix"]))
            for u in range(8):
                for b in KV_BLOCKS[u]:
                    high_and_square(x, "norm_cross_pre", xh, b, lambda b: take(block_ready))
            finish_norm(rstd[:, :])
            meet()
            copy_values([cross_v[:, :, b * P:(b + 1) * P] for b in range(4)])
            attention(attention_items("cross"))
            meet()
            prepare(y, None, None, stored(FIRST["co"]))
            prepare(x, "norm_ffn_pre", xh, lambda b: take(block_ready))
            gated()
            act.wait_ge(emptied, FIRST["fdown1"] + KT)
            act.dma_start(arena[:, 23 * N:29 * N], alibi_in).then_inc(layer_tables_in, 16)
            act.dma_start(na_all, na_in).then_inc(layer_tables_in, 16)
            prepare(y, None, None, stored(FIRST["fdown2"]))
            prepare(x, "attn_norm_e_2", xh, lambda b: take(block_ready))
            copy_values([values_a])
            act.drain().then_inc(values_free, 1)
            take(proj_raw)
            head_norm([proj2[:, E_AQ + b, :] for b in range(5)])
            attention(attention_items("window"), whole=True)
            meet()
            copy_values([values_b[:, :, b * P:(b + 1) * P] for b in range(4)])
            head_norm([proj2[:, E_BQ + b, :] for b in range(8)])
            meet()
            attention(attention_items("neighbour"))
            meet()
            prepare(x, "mlp0", mh, stored(FIRST["even_out"]))
            for p in range(4):
                mlp("m", p)
            act.wait_ge(emptied, FIRST["mdown2"] + KT)
            prepare(x, "ret_norm_o_2", xh, stored(FIRST["mdown3"]))
            act.dma_start(dist, dist_in).then_inc(distances_in, 16)
            step(act.activation(small[:, 16:32], par[:, PCOL["dec_f"]:PCOL["dec_f"] + 16], ACT.Abs))
            step(act.activation(small[:, 16:32], small[:, 16:32], ACT.Exp, scale=-1.0))
            act.activation(small[:, 32:48], small[:, 16:32], ACT.Ln, bias=1.0).then_inc(gate_fun, 1)
            for half in range(2):
                for h in range(4 * half, 4 * half + 4):
                    for u in range(U_HEAD):
                        if u >= 4:
                            act.wait_ge(emptied, ret_unit(h) + u + 1)
                            a = head_in[h % 2][:, u, :]
                            act.activation(a, a, ACT.Silu).then_inc(proj_ready, 1)
                        if h % 4:
                            retention(h - 1, u)
                for s in range(U_HEAD):
                    retention(4 * half + 3, s)
            prepare(x, "mlp1", xh, stored(FIRST["odd_out1"]))
            for p in range(4):
                mlp("n", p)
            meet()
            act.dma_start(out, x[:]).then_inc(out_done, 16)
            act.wait_ge(out_done, 16)

        @block.vector
        def _(dve):
            take, taken = counter(dve)
            meetings = [0]

            def meet():
                meetings[0] += 1
                dve.drain().then_inc(at_dve, 1)
                dve.wait_ge(at_pe, meetings[0])
                dve.wait_ge(at_act, meetings[0])

            def done(ins, s=dve_step):
                ins.then_inc(s, 1)
                take(s)

            def stt(o, a, scalar, b, op0, op1, s=dve_step):
                done(dve.scalar_tensor_tensor(out=o, in0=a, scalar=scalar, in1=b, op0=op0, op1=op1), s)

            def split(a, h, l, s=dve_step):
                done(dve.tensor_copy(h, a))
                done(dve.tensor_tensor(l, a, h.bitcast(F32), ALU.subtract), s)

            def low(src, gain, h, l, b, s=rhs_ready, width=N):
                take(high_made)
                stt(l[:, b, 0:width], src[:, b, 0:width], p_(gain, b), h[:, b, 0:width].bitcast(F32), ALU.mult,
                    ALU.subtract, s)

            def inverse(a=None):
                a = rstd[:, :] if a is None else a
                take(std_ready)
                done(dve.reciprocal(a, a))

            def add_normed(post, pre, b):
                stt(tmp[:, b % 2, :], y[:, b, :], p_(post, b), rstd[:, :], ALU.mult, ALU.mult)
                done(dve.tensor_tensor(x[:, b, :], x[:, b, :], tmp[:, b % 2, :], ALU.add), block_ready)
                if b:
                    low(x, pre, xh, xl, b - 1)

            def scaled(n, dst, s=None, rows=P, width=N, rs=None, factor=1.0, src=None):
                dve.wait_ge(unit_done, n + 1)
                a = gemm_ps[0:rows, n % 2, 0:width]
                r = (rstd if rs is None else rs)[0:rows, 0:width]
                if src is not None:
                    a, r = src(a), src(r)
                stt(dst, a, factor, r, ALU.mult, ALU.mult, emptied)

            def head_rows(nb):
                take(std_ready)
                done(dve.reciprocal(roots[0:2 * nb, :], roots[0:2 * nb, :]), rows_ready)

            def head_norm(blocks, gains):
                head_rows(len(blocks))
                for b, a in enumerate(blocks):
                    take(spread_ready)
                    stt(a, a, gains[b], score_ps[:, b % 2, :], ALU.mult, ALU.mult, spread_used)

            filled = [0]

            def fill(count=1):
                for _ in range(count):
                    scaled(later_unit(filled[0]), proj1[:, LATER_BLOCKS[filled[0]], :])
                    filled[0] += 1

            def mixer_out(gain, gate):
                head_rows(2)
                for b in range(2):
                    take(spread_ready)
                    stt(tmp[:, b, :], mixed[:, b, :], p_(gain, b), score_ps[:, b, :], ALU.mult, ALU.mult,
                        spread_used)
                    done(dve.tensor_tensor(proj1[:, gate + b, :], tmp[:, b, :], proj1[:, gate + b, :], ALU.mult))

            def store(n0, first):
                for b in range(KT):
                    store_one(n0, b, first)

            def store_one(n0, b, first):
                dve.wait_ge(unit_done, n0 + b + 1)
                ps = gemm_ps[:, (n0 + b) % 2, :]
                if first:
                    done(dve.tensor_copy(y[:, b, :], ps), emptied)
                else:
                    done(dve.tensor_tensor(y[:, b, :], y[:, b, :], ps, ALU.add), emptied)

            def add(n0, gain=None, h=None, l=None):
                for b in range(KT):
                    dve.wait_ge(unit_done, n0 + b + 1)
                    done(dve.tensor_tensor(x[:, b, :], x[:, b, :], gemm_ps[:, (n0 + b) % 2, :], ALU.add), emptied)
                    if gain and b:
                        low(x, gain, h, l, b - 1)
                if gain:
                    low(x, gain, h, l, KT - 1)

            def part_heads(k, other):
                done(dve.tensor_scalar(other, k, c_("half", 2)[:, 0:1], None, ALU.mult))
                done(dve.tensor_scalar(k, k, c_("half", 2)[:, 1:2], None, ALU.mult), keys_ready)

            def attention(items, between=lambda i: None, whole=False):
                def logits(i, it):
                    take(scores_ready)
                    s = 8 * (i % 3)
                    ps, top = score_ps[:, i % 2, 0:it["nk"]], small[:, s:s + 1]
                    if i >= 3:
                        take(probs_turned)
                    if it["bias"] is None:
                        done(dve.tensor_reduce(top, ps, AX_X, ALU.max, negate=True), logits_ready)
                        return
                    done(dve.tensor_tensor_reduce(y[:, i % 3, 0:it["nk"]], ps, it["bias"], 1.0, LEAST, ALU.add,
                                                  ALU.max, small[:, s + 4:s + 5]), scores_used)
                    if it["sink"] is None:
                        done(dve.tensor_scalar(top, small[:, s + 4:s + 5], -1.0, None, ALU.mult), logits_ready)
                    else:
                        stt(top, small[:, s + 4:s + 5], -1.0, it["sink"], ALU.mult, ALU.min, logits_ready)

                def divide(i, it):
                    take(exp_ready)
                    s = 8 * (i % 3)
                    total, a = small[:, s + 1:s + 2], y[:, i % 3, 0:it["nk"]]
                    if it["sink"] is not None:
                        done(dve.tensor_tensor(total, total, small[:, s + 2:s + 3], ALU.add))
                    done(dve.reciprocal(small[:, s + 3:s + 4], total))
                    done(dve.tensor_scalar(a, a, small[:, s + 3:s + 4], None, ALU.mult), probs_ready)

                def outputs(it):
                    take(high_ready)
                    if whole:
                        done(dve.memset(eps[:, 2:3], 0.0), group_used)
                        return
                    h, l, a = xh[:, it["to"], :], xl[:, it["to"], :], out_ps[:, it["group"] % 2, :]
                    if it["turned"]:
                        h, l = (v.rearrange("p (r c) -> p c r", r=8) for v in (h, l))
                        a = a.rearrange("p (c r) -> p c r", r=8)
                    done(dve.tensor_tensor(l, a, h.bitcast(F32), ALU.subtract), group_used)

                n = len(items)
                for i in range(n + 4):
                    if i < n:
                        logits(i, items[i])
                    if 1 <= i <= n:
                        divide(i - 1, items[i - 1])
                    if i >= 4 and items[i - 4]["last"]:
                        outputs(items[i - 4])
                    between(i)
                take(probs_turned, 3)

            def mlstm():
                f, r = slice(32, 36), slice(0, 4)
                one = edge[:, 0, :]
                done(dve.memset(one, 1.0))
                done(dve.tensor_scalar(gate_g[f, :], gates[f, :], 0.0, None, ALU.min))
                take(gate_fun)
                done(dve.tensor_tensor(gate_g[f, :], gate_g[f, :], gate_b[f, :], ALU.subtract))
                done(dve.tensor_tensor_scan(gate_a[f, :], one[f, :], gate_g[f, :], 0.0,
                                            ALU.mult, ALU.add))
                done(dve.tensor_copy(gate_g[r, :], gate_a[f, :]))
                done(dve.tensor_tensor(gate_b[r, :], gates[r, :], gate_g[r, :], ALU.subtract), gate_rows)
                done(dve.tensor_tensor_scan(gate_a[r, :], one[r, :], gate_b[r, :], 0.0,
                                            ALU.mult, ALU.max))
                done(dve.tensor_tensor(gates[r, :], gate_g[r, :], gate_a[r, :], ALU.add), gate_arg)
                done(dve.tensor_scalar(gate_a[r, :], gate_a[r, :], -1.0, None, ALU.mult), gate_rows)
                take(values_free)
                for b in range(2):
                    part_heads(proj1[:, M_K + b, :], proj1[:, M_V + b, :])
                fill()
                take(cols_ready)
                for h in range(4):
                    take(bound_ready)
                    for j in range(T):
                        m = dve.tensor_scalar(edge[:, j, j * P:N], turn_ps[:, 0, j * P:N],
                                              small[:, 32 + 4 * j + h:33 + 4 * j + h], 0.0, ALU.add, ALU.min)
                    done(m, bound_used)
                    if h < FILL_MLSTM - 1:
                        fill()
                    take(gate_fun)
                    if h >= 2:
                        take(weights_used)
                    w = weights[h % 2]
                    for j in range(T):
                        take(scores_ready)
                        done(dve.tensor_tensor(w[:, j * N + j * P:(j + 1) * N], score_ps[:, j % 2, j * P:N],
                                               edge[:, j, j * P:N], ALU.mult), scores_used)
                        d = w[:, j * N + j * P:j * N + (j + 1) * P]
                        done(dve.tensor_tensor(d, d, c_("tri", P), ALU.mult), weights_ready)
                take(weights_used, 2)
                take(gate_fun)
                done(dve.tensor_tensor(gate_g[r, :], gate_g[r, :], gates[r, :], ALU.max))
                done(dve.reciprocal(gate_b[r, :], gate_g[r, :]), rows_ready)
                for b in range(2):
                    take(spread_ready)
                    done(dve.tensor_copy(tmp[:, b, :], score_ps[:, b, :]), spread_used)
                    done(dve.tensor_tensor(mixed[:, b, :], out_ps[:, b, :], tmp[:, b, :], ALU.mult))

            def short_conv():
                for b in range(2):
                    u = edge_all[:, b * (N + 4):(b + 1) * (N + 4)]
                    t = tmp[:, b, :]
                    done(dve.memset(u[:, 0:2], 0.0))
                    done(dve.tensor_tensor(u[:, 2:N + 2], proj1[:, C_C + b, :], proj1[:, C_H + b, :], ALU.mult))
                    convolve(t, u, [p_("sconv_w", 2 * k + b) for k in range(3)])
                    done(dve.tensor_tensor(proj1[:, C_H + b, :], t, proj1[:, C_B + b, :], ALU.mult),
                         conv_done if b else dve_step)

            def convolve(o, u, w, s=dve_step):
                done(dve.tensor_scalar(o, u[:, 0:N], w[0], None, ALU.mult))
                stt(o, u[:, 1:N + 1], w[1], o, ALU.mult, ALU.add)
                stt(o, u[:, 2:N + 2], w[2], o, ALU.mult, ALU.add, s)

            def hgrn():
                lb = par[:, PCOL["hgrn_lb"]:PCOL["hgrn_lb"] + 2]
                a, e, r = small[:, 16:18], small[:, 18:20], small[:, 20:22]
                done(dve.tensor_tensor(a, lb, lb, ALU.subtract), gate_arg)
                take(gate_fun)
                done(dve.reciprocal(r, e))
                done(dve.tensor_tensor(a, e, r, ALU.mult))
                done(dve.tensor_tensor(e, a, a, ALU.subtract))
                done(dve.tensor_scalar(r, e, -1.0, 1.0, ALU.mult, ALU.add))
                take(gate_fun)
                for b in range(2):
                    f = proj1[:, H_F + b, :]
                    done(dve.tensor_scalar(f, f, r[:, b:b + 1], e[:, b:b + 1], ALU.mult, ALU.add),
                         gate_arg if b else dve_step)
                for w in weights:
                    done(dve.memset(w, 0.0))
                reset = edge[:, 3, :]
                done(dve.memset(reset, 1.0))
                done(dve.memset(reset.rearrange("p (t c) -> p t c", c=P)[:, :, 0:1], 0.0))
                take(gate_fun)
                for b in range(2):
                    g = log_decay[:, b, :]
                    done(dve.tensor_tensor_scan(g, reset, g, 0.0, ALU.mult, ALU.add), gate_arg if b else dve_step)
                take(values_free)
                for b in range(2):
                    k, k0 = proj1[:, H_F + b, :], proj1[:, H_I + b, :]
                    done(dve.tensor_scalar(k, k, -1.0, 1.0, ALU.mult, ALU.add))
                    w = CCOL["stat"] + NSTAT
                    done(dve.tensor_scalar(k0, k, con[:, w:w + 1], None, ALU.mult))
                    done(dve.tensor_scalar(k, k, con[:, w + 1:w + 2], None, ALU.mult))
                fill(FILL_START)
                for b in range(2):
                    q, g = proj1[:, H_Q + b, :], log_decay[:, b, :]
                    keys = (proj1[:, H_I + b, :], proj1[:, H_F + b, :])
                    q1, q2, q3 = level_kq[1][2], edge[:, 0, :], edge[:, 1, :]
                    take(gate_fun)
                    for s in range(2):
                        done(dve.tensor_tensor(level_kq[1][s], edge[:, 0, :], keys[s], ALU.mult))
                    done(dve.tensor_tensor(q1, edge[:, 1, :], q, ALU.mult))
                    for o, src, i, over in ((q2, q1, 2, 1), (q2, q1, 3, 2), (q3, q2, 3, 1)):
                        t = slice(i * P, (i + 1) * P)
                        done(dve.tensor_scalar(o[:, t], src[:, t], small[:, 24 + over:25 + over], None, ALU.mult),
                             level_ready if o is q3 else dve_step)
                    if b:
                        take(weights_used)

                    def scores(lev):
                        mask = con[:, CCOL["level"] + lev * P:CCOL["level"] + (lev + 1) * P].bitcast(U32)
                        for s in range(2):
                            take(scores_ready)
                            done(dve.copy_predicated(
                                diagonal(s), mask.unsqueeze(1).broadcast_to([P, T, P]),
                                score_ps[:, s, :].rearrange("p (j c) -> p j c", c=P)), scores_used)

                    for lev, half in enumerate(LEVELS):
                        gs = g.rearrange("p (s c) -> p s c", c=2 * half)
                        ds = edge[:, 3, :].rearrange("p (s c) -> p s c", c=2 * half)
                        ref = gs[:, :, half - 1:half].broadcast_to([P, N // (2 * half), half])
                        done(dve.tensor_tensor(ds[:, :, 0:half], ref, gs[:, :, 0:half], ALU.subtract))
                        done(dve.tensor_tensor(ds[:, :, half:], gs[:, :, half:], ref, ALU.subtract), gate_arg)
                        if lev:
                            scores(lev - 1)
                        take(gate_fun)
                        for o, a in zip(level_kq[lev % 2], (*keys, q)):
                            done(dve.tensor_tensor(o, a, edge[:, 2, :], ALU.mult),
                                 level_ready if a is q else dve_step)
                        if lev - 1 in FILL_LEVELS:
                            fill()
                    for o, a in zip(level_kq[1], (*keys, q)):
                        done(dve.tensor_copy(o, a), level_ready if a is q else dve_step)
                    if 6 in FILL_LEVELS:
                        fill()
                    scores(6)
                    scores(7)
                take(weights_used)

            def retention(h, s):
                if s == 0:
                    take(head_turned)
                    done(dve.tensor_reduce(small[:, 8:12],
                                           turn_ps[:, :, :].rearrange("p b (t c) -> p t b c", c=P),
                                           AX_XY, ALU.add))
                    done(dve.tensor_scalar(small[:, 8:12], small[:, 8:12], -1.0 / G, None, ALU.mult), mean_ready)
                    done(dve.tensor_scalar(decay, dist[:, 0:7 * P], small[:, 48 + h:49 + h], None, ALU.mult))
                    stt(decay, dist[:, 7 * P:14 * P], small[:, 56 + h:57 + h], decay, ALU.mult, ALU.add, gate_arg)
                    take(gate_fun)
                    weigh(0)
                    weigh(1)
                elif s < 3:
                    weigh(s + 1)
                elif s == 3:
                    take(weights_used)
                elif s == 5:
                    take(ret_std)
                    done(dve.reciprocal(rstd_r[:, :], rstd_r[:, :]))
                    for c in range(2):
                        stt(tmp[:, c, :], out_ps[:, c, :], p_("gn", 2 * h + c), rstd_r[:, :], ALU.mult, ALU.mult,
                            head_done if c else dve_step)
                    take(proj_ready, 2)
                    for c in range(2):
                        t, b = tmp[:, c, :], 2 * (h % 4) + c
                        done(dve.tensor_tensor(t, t, head_in[h % 2][:, 4 + c, :], ALU.mult))
                        split(t, ret_h[:, b, :], ret_l[:, b, :], rhs_ready)

            def weigh(j):
                take(scores_ready)
                stt(ret_w[:, j, :], score_ps[:, j % 2, :], P ** -0.5, decay[:, (3 - j) * P:(7 - j) * P],
                    ALU.mult, ALU.mult, scores_used)

            def mlp(name, p):
                h, l = hidden[p % 2]

                def low_part(b):
                    take(hidden_raw)
                    done(dve.tensor_tensor(l[:, b, :], sq[:, b % 2, :], h[:, b, :].bitcast(F32), ALU.subtract),
                         rhs_ready)

                for b in range(FF2_PARTS[p]):
                    n = FIRST[f"{name}up{p}"] + b
                    dve.wait_ge(unit_done, n + 1)
                    stt(tmp[:, b % 2, :], gemm_ps[:, n % 2, :], 0.0, rstd[:, :], ALU.max, ALU.mult, emptied)
                    if b:
                        low_part(b - 1)
                low_part(FF2_PARTS[p] - 1)

            def gated():
                for u in padded:
                    done(dve.memset(u[:, 0:2], 0.0))
                b = 0
                for p in range(len(FF1_PARTS)):
                    for i in range(FF1_PARTS[p]):
                        n, t, u = FIRST[f"fup{p}"] + 2 * i, tmp[:, b % 2, :], padded[b % 2]
                        scaled(n, u[:, 2:N + 2])
                        convolve(t, u, [p_("ffn_conv_w", 22 * k + b) for k in range(3)], conv_ready)
                        take(hidden_raw)
                        dve.wait_ge(unit_done, n + 2)
                        done(dve.tensor_tensor(t, sq[:, b % 2, :], gemm_ps[:, (n + 1) % 2, :], ALU.mult), emptied)
                        done(dve.tensor_tensor(t, t, rstd[:, :], ALU.mult))
                        split(t, hidden[p % 2][0][:, i, :], hidden[p % 2][1][:, i, :], rhs_ready)
                        b += 1
                    if p:
                        store(FIRST[f"fdown{p - 1}"], p == 1)
                store(FIRST["fdown2"], False)

            dve.memset(eps[:, 0:1], RMS_EPS)
            dve.memset(eps[:, 1:2], GN_EPS)
            dve.wait_ge(inputs_in, 32)
            meet()
            for b in range(KT):
                low(x, "norm_mix_pre", xh, xl, b)
            inverse()
            scaled(FIRST["in"], gates[0:HD, :], rows=HD)
            for i, b in enumerate(FIRST_BLOCKS):
                scaled(FIRST["in"] + 1 + i, proj1[:, b, :])
            meet()
            hgrn()
            meet()
            fill(FILL_NORM)
            mixer_out("hgrn_norm", H_G)
            meet()
            mlstm()
            meet()
            fill(FILL_NORM)
            short_conv()
            mixer_out("mlstm_norm", M_O)
            meet()
            dve.wait_ge(moba_table_in, 16)
            take(values_free)
            for b in range(2):
                part_heads(proj1[:, A_K + b, :], proj1[:, A_V + b, :])

            def split_mixer(i):
                if i % 3 == 2 and i // 3 < 6:
                    b = i // 3
                    to, src = ((0, M_O), (1, M_O + 1), (2, C_H), (3, C_H + 1), (6, H_G), (7, H_G + 1))[b]
                    split(proj1[:, src, :], xh[:, to, :], xl[:, to, :])
            attention(attention_items("moba"), split_mixer)
            meet()
            dve.wait_ge(memory_in, 16)
            for b in range(KT):
                low(mem_raw, "mem_norm", mem_h, mem_l, b, dve_step, M)
            store_one(FIRST["mix"], 0, True)
            store_one(FIRST["mix"], 1, True)
            inverse(mem_rstd)
            for b in range(2, KT):
                store_one(FIRST["mix"], b, True)
            inverse()
            for u in range(8):
                o = cross_k if u < 4 else cross_vf
                scaled(FIRST["cross_kv"] + u, o[:, u % 4, :], width=M, rs=mem_rstd)
                for b in KV_BLOCKS[u]:
                    add_normed("norm_mix_post", "norm_cross_pre", b)
            low(x, "norm_cross_pre", xh, xl, KT - 1)
            inverse()
            for b in range(4):
                scaled(FIRST["cross_q"] + b, cross_q[:, b, :], factor=P ** -0.5)
            meet()
            attention(attention_items("cross"))
            meet()
            store(FIRST["co"], True)
            inverse()
            for b in range(KT):
                add_normed("norm_cross_post", "norm_ffn_pre", b)
            low(x, "norm_ffn_pre", xh, xl, KT - 1)
            inverse()
            gated()
            inverse()
            for b in range(KT):
                add_normed("norm_ffn_post", "attn_norm_e_2", b)
            low(x, "attn_norm_e_2", xh, xl, KT - 1)
            inverse()
            for b in range(6):
                scaled(FIRST["even_in"] + b, proj2[:, b, :])
            done(dve.memset(eps[:, 2:3], 0.0), proj_raw)
            sinks = par[:, PCOL["sink"]:PCOL["sink"] + 8]
            done(dve.tensor_scalar(sinks, sinks, -1.0, None, ALU.mult))
            head_norm([proj2[:, E_AQ + b, :] for b in range(5)], [p_("qa", 0)] * 4 + [p_("ka", 0)])
            take(values_free)
            part_heads(proj2[:, E_AK, :], proj2[:, E_AV, :])
            dve.wait_ge(layer_tables_in, 32)

            def neighbour_unit(i):
                if i % 3 == 1 and i // 3 < 12:
                    b = 6 + i // 3
                    scaled(FIRST["even_in"] + b, proj2[:, b, :].rearrange("p (c r) -> p r c", r=8),
                           src=lambda a: a.rearrange("p (r c) -> p r c", r=8))
            attention(attention_items("window"), neighbour_unit, whole=True)
            meet()
            for b in range(4):
                split(y[:, 5 + b, :], xh[:, b, :], xl[:, b, :])
            head_norm([proj2[:, E_BQ + b, :] for b in range(8)], [p_("qb", 0)] * 4 + [p_("kb", 0)] * 4)
            for b in range(4):
                part_heads(proj2[:, E_BK + b, :], proj2[:, E_BV + b, :])
            meet()
            attention(attention_items("neighbour"))
            meet()
            add(FIRST["even_out"], "mlp0", mh, ml)
            inverse()
            mlp("m", 0)
            for p in (1, 2, 3):
                mlp("m", p)
                add(FIRST[f"mdown{p - 1}"])
            add(FIRST["mdown3"], "ret_norm_o_2", xh, xl)
            inverse()
            take(gate_fun)
            dec = par[:, PCOL["dec_f"]:PCOL["dec_f"] + 16]
            done(dve.tensor_scalar(small[:, 16:32], dec, 0.0, None, ALU.min))
            done(dve.tensor_tensor(small[:, 48:64], small[:, 16:32], small[:, 32:48], ALU.subtract))
            dve.wait_ge(distances_in, 16)
            for half in range(2):
                for h in range(4 * half, 4 * half + 4):
                    for u in range(U_HEAD):
                        scaled(ret_unit(h) + u, head_in[h % 2][:, u, :])
                        if h % 4:
                            retention(h - 1, u)
                for s in range(U_HEAD):
                    retention(4 * half + 3, s)
                if half:
                    add(FIRST["odd_out1"], "mlp1", xh, xl)
                else:
                    add(FIRST["odd_out0"])
            inverse()
            mlp("n", 0)
            for p in (1, 2, 3):
                mlp("n", p)
                add(FIRST[f"ndown{p - 1}"])
            add(FIRST["ndown3"])
            meet()


def _blocks(w, nkt=KT, start=0):
    k, m = w.shape
    a = w[start * P:(start + nkt) * P].reshape(nkt, P, m // P, P).transpose(2, 1, 0, 3).reshape(m // P, P, nkt * P)
    return np.pad(a, ((0, 0), (0, 0), (0, KT * P - nkt * P)))


def _stream(inp):
    units = []
    w = inp["w_in"][0]
    cuts = np.cumsum([G] * 4 + [4, 4] + [G] * 10)
    cols = np.split(w, cuts[:-1], axis=1)
    gates = np.zeros((D, P), w.dtype)
    gates[:, 0:4], gates[:, 32:36] = cols[4], cols[5]
    units.append(_blocks(gates))
    units.append(_blocks(np.concatenate(cols[12:16] + cols[0:4] + cols[6:12], axis=1)))
    units.append(_blocks(inp["w_mix_out"][0]))
    for name in ("w_ck", "w_cv", "w_cq"):
        units.append(_blocks(inp[name][0]))
    units.append(_blocks(inp["w_co"][0], 4))

    def parts(sizes, ups, down):
        at = np.concatenate([[0], np.cumsum(sizes)])

        def up(p):
            u = [_blocks(a[:, at[p] * P:at[p + 1] * P]) for a in ups]
            units.append(np.stack(u, 1).reshape(-1, P, KT * P))

        up(0)
        for p in range(len(sizes)):
            if p + 1 < len(sizes):
                up(p + 1)
            units.append(_blocks(down, sizes[p], at[p]))

    f = inp["w_ffn_in"][0]
    parts(FF1_PARTS, [f[:, :FF1], f[:, FF1:]], inp["w_ffn_out"][0])
    pair = np.array([0, 4, 1, 5, 2, 6, 3, 7])
    e = inp["w_in_e_2"][0]
    units.append(_blocks(np.concatenate([e[:, :512].reshape(D, 8, HD)[:, pair].reshape(D, 512), e[:, 512:]], 1)))
    e = inp["w_out_e_2"][0]
    units.append(_blocks(np.concatenate([e[:512].reshape(8, HD, D)[pair].reshape(512, D), e[512:]], 0)))
    parts(FF2_PARTS, [inp["w_mlp_in_2"][0]], inp["w_mlp_out_2"][0])
    o = inp["w_in_o_2"][0]
    q, k, v, g = np.split(o, [D, 2 * D, 4 * D], axis=1)
    for half in range(2):
        heads = []
        for h in range(4 * half, 4 * half + 4):
            heads += [q[:, h * P:(h + 1) * P], k[:, h * P:(h + 1) * P], v[:, h * G:(h + 1) * G],
                      g[:, h * G:(h + 1) * G]]
        units.append(_blocks(np.concatenate(heads, 1)))
        units.append(_blocks(inp["w_out_o_2"][0], KT, half * KT))
    parts(FF2_PARTS, [inp["w_mlp_in_2"][1]], inp["w_mlp_out_2"][1])
    out = np.concatenate(units)
    assert out.shape == (UNITS, P, KT * P), out.shape
    return out.reshape(UNITS * P, KT * P)


def _parameters(inp):
    par = np.zeros((P, PARAMS), np.float32)

    def put(name, a):
        par[:, PCOL[name]:PCOL[name] + a.shape[0]] = a.T

    for name in ("norm_mix_pre", "norm_mix_post", "mem_norm", "norm_cross_pre", "norm_cross_post", "norm_ffn_pre",
                 "norm_ffn_post", "attn_norm_e_2", "ret_norm_o_2", "mlstm_norm", "hgrn_norm"):
        put(name, inp[name][0].reshape(-1, P))
    put("mlp0", inp["mlp_norm_2"][0].reshape(-1, P))
    put("mlp1", inp["mlp_norm_2"][1].reshape(-1, P))
    b = inp["b_in"][0]
    put("b_in", np.concatenate([b[:4 * G], b[4 * G + 8:]]).reshape(-1, P))
    par[0:4, PCOL["b_gates"]] = b[4 * G:4 * G + 4]
    par[32:36, PCOL["b_gates"]] = b[4 * G + 4:4 * G + 8]
    put("hgrn_lb", inp["hgrn_lb_logits"][0].reshape(-1, P))
    put("sconv_w", inp["sconv_w"][0].reshape(-1, P))
    put("ffn_conv_w", inp["ffn_conv_w"][0].reshape(-1, P))
    put("ffn_conv_b", inp["ffn_conv_b"][0].reshape(-1, P))
    for name, src in (("qa", "q_norm_a_2"), ("ka", "k_norm_a_2"), ("qb", "q_norm_b_2"), ("kb", "k_norm_b_2")):
        put(name, np.tile(inp[src][0], 2).reshape(1, P))
    sink = inp["sink_a_2"][0][[0, 4, 1, 5, 2, 6, 3, 7]]
    put("sink", np.broadcast_to(sink[:, None], (8, P)))
    put("dec_f", np.broadcast_to(inp["decay_fwd_o_2"][0][:, None], (8, P)))
    put("dec_b", np.broadcast_to(inp["decay_bwd_o_2"][0][:, None], (8, P)))
    put("gn", inp["ret_gn_o_2"][0].reshape(-1, P))
    return par


def _moba_bias(rel_bias):
    dist = np.arange(P)[:, None] + 3 * P - np.arange(N)[None, :]
    n = np.maximum(dist, 0)
    large = 16 + (np.log(np.maximum(n, 1).astype(np.float32) / np.float32(16)) / np.float32(np.log(8.0))
                  * np.float32(16)).astype(np.int32)
    bucket = np.where(n < 16, n, np.minimum(large, 31))
    out = np.where((dist >= 0)[:, :, None], rel_bias[bucket], np.float32(NEG))
    return np.ascontiguousarray(out.transpose(0, 2, 1)).reshape(P, 4 * N)


def _na_bias(rpb):
    q = np.arange(P)
    out = []
    for t, lo, hi in ((0, 0, 2), (1, 0, 3), (3, 2, 4)):
        k = np.arange(lo * P, hi * P)
        qc, qr, kc, kr = 16 * t + q // 8, q % 8, k // 8, k % 8
        start = np.clip(qc - 8, 0, 48)
        valid = (kc[None] >= start[:, None]) & (kc[None] < start[:, None] + 16)
        col = np.clip(kc[None] - qc[:, None] + 15, 0, 30)
        row = kr[None] - qr[:, None] + 7
        out.append(np.where(valid[None], rpb[:, row, col], np.float32(NEG)).transpose(1, 0, 2).reshape(P, -1))
    return np.concatenate(out, 1)


def _feature_major(a):
    return np.ascontiguousarray(a.T.reshape(KT, P, -1).transpose(1, 0, 2)).reshape(P, -1)


def kernel(**inputs):
    import concourse.bacc as bacc
    from concourse.bass_utils import run_bass_kernel_spmd

    inp = {k: np.asarray(v) for k, v in inputs.items()}
    arrays = {
        "x_in": _feature_major(inp["x"][0]),
        "mem_in": _feature_major(inp["mem"][0]),
        "w_in": _stream(inp),
        "par_in": _parameters(inp),
        "con_in": _constants(),
        "moba_in": _moba_bias(inp["rel_bias"]),
        "alibi_in": _alibi(),
        "na_in": _na_bias(inp["rpb_b_2"][0]),
        "dist_in": _distances(),
    }
    nc = bacc.Bacc("TRN2", target_bir_lowering=False, num_devices=1)
    args = [nc.dram_tensor(k, a.shape, F32, kind="ExternalInput").ap() for k, a in arrays.items()]
    out = nc.dram_tensor("out", (P, KT * N), F32, kind="ExternalOutput").ap()
    args[0] = args[0].rearrange("p (b n) -> p b n", n=N)
    build(nc, *args, out.rearrange("p (b n) -> p b n", n=N))
    got = run_bass_kernel_spmd(nc, [arrays], core_ids=[0]).results[0]["out"]
    return np.ascontiguousarray(got.reshape(P, KT, N).transpose(2, 1, 0)).reshape(1, N, D)
```

```python
from contextlib import ExitStack

import numpy as np
import concourse.bass as bass
from concourse import mybir

F32 = mybir.dt.float32
F32R = mybir.dt.float32r
U32 = mybir.dt.uint32
ALU = mybir.AluOpType
ACT = mybir.ActivationFunctionType
AX_X = mybir.AxisListType.X
AX_XY = mybir.AxisListType.XY

P = 128
D = 1024
KT = D // P
N = 512
T = N // P
M = 256
HD = 64
G = 256
FF1 = 2816
NEG = -1.0e30
LEAST = -3.0e38
RMS_EPS = 1e-6
GN_EPS = 1e-5

U_IN = 1 + 14 * 2
U_MIX = KT
U_CO = KT // 2
FF1_PARTS = (8, 8, 6)
FF2_PARTS = (8, 8, 8, 8)
U_EVEN_IN = 18
U_EVEN_OUT = KT
U_HEAD = 6
RH = 8

KV_EARLY = 6

ORDER = []
ORDER.append(("in", U_IN))
ORDER.append(("memory0", KV_EARLY))
ORDER.append(("mix", U_MIX))
ORDER.append(("memory1", 8 - KV_EARLY))
ORDER.append(("cross_q", 4))
ORDER.append(("co", U_CO))


def _parts(name, parts, up):
    out = [(f"{name}up0", up * parts[0])]
    for p in range(len(parts)):
        if p + 1 < len(parts):
            out.append((f"{name}up{p + 1}", up * parts[p + 1]))
        out.append((f"{name}down{p}", KT))
    return out


ORDER += _parts("f", FF1_PARTS, 2)
ORDER += [("even_in", U_EVEN_IN), ("even_out", U_EVEN_OUT)]
ORDER += _parts("m", FF2_PARTS, 1)
ODD_HEADS = (range(0, RH // 2 + 1), range(RH // 2 + 1, RH))
ORDER += [("odd_in0", len(ODD_HEADS[0]) * U_HEAD), ("odd_out0", KT),
          ("odd_in1", len(ODD_HEADS[1]) * U_HEAD), ("odd_out1", KT)]
ORDER += _parts("n", FF2_PARTS, 1)
FIRST = {}
_n = 0
for _name, _count in ORDER:
    FIRST[_name] = _n
    _n += _count
UNITS = _n

RING = 4
FILL_START, FILL_LEVELS, FILL_MLSTM = 3, (0, 1, 2, 3, 4, 5), 5
W_IN_P = 28
FIRST_BLOCKS = (22, 23, 24, 25, 20, 21, 26, 27)
LATER_BLOCKS = tuple(range(0, 20))
assert FILL_START + 2 * len(FILL_LEVELS) + FILL_MLSTM == len(LATER_BLOCKS)

PCOL = {}
_c = 0
for _name, _w in (("norm_mix_pre", 8), ("norm_mix_post", 8), ("mem_norm", 8), ("norm_cross_pre", 8),
                  ("norm_cross_post", 8), ("norm_ffn_pre", 8), ("norm_ffn_post", 8), ("attn_norm_e_2", 8),
                  ("mlp0", 8), ("ret_norm_o_2", 8), ("mlp1", 8), ("b_in", 28), ("b_gates", 1),
                  ("mlstm_norm", 2), ("hgrn_norm", 2), ("hgrn_lb", 2), ("sconv_w", 6),
                  ("ffn_conv_w", 66), ("ffn_conv_b", 22), ("qa", 1), ("ka", 1), ("qb", 1), ("kb", 1),
                  ("sink", 8), ("dec_f", 8), ("dec_b", 8), ("gn", 16)):
    PCOL[_name] = _c
    _c += _w
PARAMS = _c

NSTAT = 16
LEVELS = (64, 32, 16, 8, 4, 2, 1)
CCOL = {}
_c = 0
for _name, _w in (("ident", P), ("ones", P), ("stat", NSTAT + P), ("pair", 8 * P), ("row", 4 * P),
                  ("col", 8), ("tri", P), ("level", 8 * P), ("half", 2)):
    CCOL[_name] = _c
    _c += _w
CONSTS = _c


def _constants():
    c = np.zeros((P, CONSTS), np.float32)
    i = np.arange(P)

    def at(name, w):
        return c[:, CCOL[name]:CCOL[name] + w]

    at("ident", P)[:] = np.eye(P)
    at("ones", P)[:] = 1.0
    at("stat", NSTAT + P)[:HD, NSTAT] = 1.0
    at("stat", NSTAT + P)[HD:, NSTAT + 1] = 1.0
    for b in range(8):
        at("pair", 8 * P)[2 * b, b * P:b * P + HD] = 1.0
        at("pair", 8 * P)[2 * b + 1, b * P + HD:(b + 1) * P] = 1.0
    for h in range(4):
        at("row", 4 * P)[h, h * P:(h + 1) * P] = 1.0
    at("col", 8)[:, 4] = 1.0
    at("tri", P)[:] = i[None, :] >= i[:, None]
    for n, half in enumerate(LEVELS):
        seg = i // (2 * half)
        right = (i % (2 * half)) >= half
        at("level", 8 * P)[:, n * P:(n + 1) * P] = (
            (seg[:, None] == seg[None, :]) & ~right[:, None] & right[None, :])
    at("level", 8 * P)[:, 7 * P:] = np.eye(P)
    at("half", 2)[:HD, 0] = at("half", 2)[HD:, 1] = HD ** -0.5
    return c


def _alibi():
    q, k = np.arange(P)[:, None], np.arange(3 * P)[None, :]
    rel = k - P - q
    out = np.zeros((P, 8, 3 * P), np.float32)
    for b in range(4):
        for s in range(2):
            slope = 2.0 ** -(4 * s + b + 1.0)
            out[:, 2 * b + s] = np.where(np.abs(rel) <= P, -slope * np.abs(rel), NEG)
    return out.reshape(P, -1)


def _distances():
    d = np.arange(7 * P)[None, :] - 3 * P - np.arange(P)[:, None]
    return np.concatenate([np.maximum(d, 0), np.maximum(-d, 0)], 1).astype(np.float32)


def build(nc, x_in, mem_in, w_in, par_in, con_in, moba_in, alibi_in, na_in, dist_in, out):
    with ExitStack() as ctx:
        def sb(name, shape, dt=F32):
            return ctx.enter_context(nc.sbuf_tensor(name, shape, dt))

        def sem(name):
            return ctx.enter_context(nc.semaphore(name))

        gemm_ps = ctx.enter_context(nc.psum_tensor("gemm_ps", [P, 2, N], F32))
        score_ps = ctx.enter_context(nc.psum_tensor("score_ps", [P, 2, N], F32))
        turn_ps = ctx.enter_context(nc.psum_tensor("turn_ps", [P, 2, N], F32))
        out_ps = ctx.enter_context(nc.psum_tensor("out_ps", [P, 2, N], F32))

        x = sb("x", [P, KT, N])
        xh = sb("xh", [P, KT, N], F32R)
        xl = sb("xl", [P, KT, N], F32R)
        raw = sb("raw", [P, RING, KT * P])
        wh = sb("wh", [P, 2, KT * P], F32R)
        wl = sb("wl", [P, 2, KT * P], F32R)
        y_at = nc.sbuf_base
        y_all = sb("y_all", [P, (KT + 1) * N])
        y = y_all[:, :].rearrange("p (b n) -> p b n", n=N)
        y_r = nc.alloc_sbuf_tensor_at("y_r", [P, KT * N], F32R, offset=y_at)
        par = sb("par", [P, PARAMS])
        con = sb("con", [P, CONSTS])
        eps = sb("eps", [P, 4])
        unity = sb("unity", [P, 2])
        small = sb("small", [P, 64])
        sq = sb("sq", [P, 2, N])
        rstd = sb("rstd", [P, N])
        tmp = sb("tmp", [P, 2, N])
        ARENA = 43 * N
        arena_at = nc.sbuf_base
        arena = sb("arena", [P, ARENA])
        arena_r = nc.alloc_sbuf_tensor_at("arena_r", [P, ARENA], F32R, offset=arena_at)

        def region(first, blocks, dt=F32):
            a = (arena if dt is F32 else arena_r)[:, first * N:(first + blocks) * N]
            return a.rearrange("p (b n) -> p b n", n=N)

        def c_(name, w, p0=0, p1=P):
            return con[p0:p1, CCOL[name]:CCOL[name] + w]

        ident = c_("ident", P)
        ones = c_("ones", P)

        def p_(name, i, p0=0, p1=P):
            return par[p0:p1, PCOL[name] + i:PCOL[name] + i + 1]

        proj1 = region(0, W_IN_P)
        M_Q, M_K, M_V, M_O, C_B, C_C, C_H, A_Q, A_K, A_V, H_Q, H_F, H_I, H_G = range(0, W_IN_P, 2)
        edge = region(28, 4)
        conv_padded = arena[:, 24 * N:25 * N + 4]
        values1 = arena[:, 32 * N:34 * N].rearrange("p (t c) -> p t c", c=G)
        mixed = region(34, 2)
        mixed_m = region(41, 2)
        gates = arena[:, 36 * N:37 * N]
        gate_a, gate_b, gate_g = (arena[:, (37 + k) * N:(38 + k) * N] for k in range(3))
        moba_bias = region(8, 4)
        level_kq = ((tmp[:, 0, :], tmp[:, 1, :], y[:, 8, :]), (sq[:, 0, :], sq[:, 1, :], arena[:, 42 * N:43 * N]))
        log_decay = region(40, 2)
        weights = (y_all[:, 0:4 * N], y_all[:, 4 * N:8 * N])

        def diagonal(w):
            return y_all[:, w * 4 * N:w * 4 * N + 5 * N].rearrange("p (j c) -> p j c", c=N + P)[:, :, 0:P]

        E_AQ, E_AK, E_AV, E_BQ, E_BK, E_BV = 0, 4, 5, 6, 10, 14
        proj2 = region(0, U_EVEN_IN)
        values_a = arena[:, 18 * N:19 * N].rearrange("p (t c) -> p t c", c=P)
        values_b = arena[:, 19 * N:23 * N].rearrange("p (t c) -> p t c", c=4 * P)
        alibi = arena[:, 23 * N:29 * N].rearrange("p (h k) -> p h k", h=8)
        na_all = arena[:, 29 * N:43 * N]
        na_bias = [na_all[:, 0:8 * 256].rearrange("p (h k) -> p h k", h=8),
                   na_all[:, 8 * 256:8 * 640].rearrange("p (h k) -> p h k", h=8),
                   na_all[:, 8 * 640:8 * 896].rearrange("p (h k) -> p h k", h=8)]
        na_bias = [na_bias[0], na_bias[1], na_bias[1], na_bias[2]]

        head_in = [region(6 * s, 6) for s in range(2)]
        values_hl = [arena_r[:, a * N:(a + 2) * N].rearrange("p (t c) -> p t c", c=G) for a in (12, 14)]
        decay = arena[:, 16 * N:16 * N + 7 * P]
        ret_qk = (region(18, 2, F32R), region(20, 2, F32R))
        ret_w = [y_r[:, a * N:(a + T) * N].rearrange("p (b n) -> p b n", n=N) for a in (0, T)]
        dist = arena[:, 22 * N:22 * N + 14 * P]
        rstd_r = arena[:, 42 * N:43 * N]
        ret_h, ret_l = region(26, 8, F32R), region(34, 8, F32R)
        mh, ml = y_r[:, :].rearrange("p (b n) -> p b n", n=N), region(32, 8, F32R)

        hidden = [(region(16 * s, 8, F32R), region(16 * s + 8, 8, F32R)) for s in range(2)]
        padded = [arena[:, 32 * N + s * (N + 4):32 * N + (s + 1) * (N + 4)] for s in range(2)]

        def memory_unit(u):
            return FIRST["memory0"] + u if u < KV_EARLY else FIRST["memory1"] + u - KV_EARLY

        def later_unit(i):
            return FIRST["in"] + 1 + len(FIRST_BLOCKS) + i

        def ret_unit(h):
            half = 0 if h in ODD_HEADS[0] else 1
            return FIRST[f"odd_in{half}"] + U_HEAD * (h - ODD_HEADS[half][0])

        def attention_items(kind):
            items = []
            if kind == "moba":
                for b in range(2):
                    for t in range(T):
                        for s in range(2):
                            nk = (t + 1) * P
                            r = slice(s * HD, (s + 1) * HD)
                            items.append(dict(
                                q=proj1[:, A_Q + b, t * P:(t + 1) * P], k=proj1[:, (A_V if s == 0 else A_K) + b, 0:nk], nk=nk,
                                bias=moba_bias[:, 2 * b + s, (3 - t) * P:4 * P], sink=None,
                                v=[values1[:, c, (2 * b + s) * HD:(2 * b + s + 1) * HD] for c in range(t + 1)],
                                rows=r, tile=t, group=b, last=t == T - 1 and s == 1, first=t == 0 and s == 0,
                                to=4 + b, turned=False))
            elif kind == "cross":
                for b in range(4):
                    for t in range(T):
                        items.append(dict(
                            q=cross_q[:, b, t * P:(t + 1) * P], k=cross_k[:, b, :], nk=M, bias=None,
                            sink=None, v=[cross_v[:, c, b * P:(b + 1) * P] for c in range(2)],
                            rows=slice(0, P), tile=t, group=b, last=t == T - 1, first=t == 0, to=b, turned=False))
            elif kind == "window":
                for b in range(4):
                    for t in range(T):
                        lo, hi = max(t - 1, 0), min(t + 2, T)
                        for s in range(2):
                            r = slice(s * HD, (s + 1) * HD)
                            items.append(dict(
                                q=proj2[:, E_AQ + b, t * P:(t + 1) * P], k=proj2[:, E_AV if s == 0 else E_AK, lo * P:hi * P],
                                nk=(hi - lo) * P, bias=alibi[:, 2 * b + s, (lo - t + 1) * P:(hi - t + 1) * P],
                                sink=p_("sink", 2 * b + s),
                                v=[values_a[:, c, s * HD:(s + 1) * HD] for c in range(lo, hi)],
                                rows=r, tile=t, group=b, last=t == T - 1 and s == 1, first=t == 0 and s == 0,
                                to=b, turned=False))
            else:
                for b in range(4):
                    for t in range(T):
                        lo, hi = max(t - 1, 0), min(t + 2, T)
                        for s in range(2):
                            r = slice(s * HD, (s + 1) * HD)
                            items.append(dict(
                                q=proj2[:, E_BQ + b, t * P:(t + 1) * P],
                                k=proj2[:, (E_BV if s == 0 else E_BK) + b, lo * P:hi * P],
                                nk=(hi - lo) * P, bias=na_bias[t][:, 2 * b + s, :],
                                sink=None,
                                v=[values_b[:, c, (2 * b + s) * HD:(2 * b + s + 1) * HD] for c in range(lo, hi)],
                                rows=r, tile=t, group=b, last=t == T - 1 and s == 1, first=t == 0 and s == 0,
                                to=4 + b, turned=True))
            return items

        cross_q = region(4, 4)
        cross_k = arena[:, 28 * N:30 * N].rearrange("p (b m) -> p b m", m=M)
        cross_vf = arena[:, 30 * N:32 * N].rearrange("p (b m) -> p b m", m=M)
        cross_v = arena[:, 13 * N:15 * N].rearrange("p (t c) -> p t c", c=N)
        mem_raw = arena[:, 20 * N:24 * N].rearrange("p (b m) -> p b m", m=M)
        mem_h = arena_r[:, 36 * N:40 * N].rearrange("p (b m) -> p b m", m=M)
        mem_l = arena_r[:, 0:4 * N].rearrange("p (b m) -> p b m", m=M)
        mem_rstd = arena[:, 40 * N:40 * N + M]

        square_sum = tmp[:, 0, :]
        roots = y[:, 4, :]

        inputs_in = sem("inputs_in")
        constants_in = sem("constants_in")
        x_in_sem = [sem(f"x_in_{b}") for b in range(KT)]
        moba_table_in = sem("moba_table_in")
        memory_in = sem("memory_in")
        layer_tables_in = sem("layer_tables_in")
        distances_in = sem("distances_in")
        unit_in = [sem(f"unit_in{k}") for k in range(RING)]
        unity_set = sem("unity_set")
        high_split = sem("high_split")
        unit_split = sem("unit_split")
        unit_done = sem("unit_done")
        emptied = sem("emptied")
        block_ready = sem("block_ready")
        high_made = sem("high_made")
        proj_raw = sem("proj_raw")
        proj_ready = sem("proj_ready")
        act_step = sem("act_step")
        dve_step = sem("dve_step")
        at_pe, at_act, at_dve = sem("at_pe"), sem("at_act"), sem("at_dve")
        rhs_ready = sem("rhs_ready")
        square_ready = sem("square_ready")
        square_made = sem("square_made")
        square_added = sem("square_added")
        square_used = sem("square_used")
        std_ready = sem("std_ready")
        rows_ready = sem("rows_ready")
        spread_ready = sem("spread_ready")
        spread_used = sem("spread_used")
        turned_v = sem("turned_v")
        bias_added = sem("bias_added")
        conv_done = sem("conv_done")
        copied_v = sem("copied_v")
        values_free = sem("values_free")
        scores_ready = sem("scores_ready")
        scores_used = sem("scores_used")
        logits_ready = sem("logits_ready")
        exp_ready = sem("exp_ready")
        probs_ready = sem("probs_ready")
        probs_turned = sem("probs_turned")
        probs_copied = sem("probs_copied")
        keys_ready = sem("keys_ready")
        item_done = sem("item_done")
        high_ready = sem("high_ready")
        group_used = sem("group_used")
        gate_arg = sem("gate_arg")
        gate_fun = sem("gate_fun")
        gate_rows = sem("gate_rows")
        bound_ready = sem("bound_ready")
        bound_used = sem("bound_used")
        weights_ready = sem("weights_ready")
        weights_used = sem("weights_used")
        cols_turned = sem("cols_turned")
        cols_ready = sem("cols_ready")
        level_ready = sem("level_ready")
        far_ready = sem("far_ready")
        far_copied = sem("far_copied")
        tile_weighted = sem("tile_weighted")
        weights_high = sem("weights_high")
        keys_high = sem("keys_high")
        keys_low = sem("keys_low")
        values_high = sem("values_high")
        values_low = sem("values_low")
        ret_std = sem("ret_std")
        head_turned = sem("head_turned")
        mean_ready = sem("mean_ready")
        hidden_raw = sem("hidden_raw")
        head_done = sem("head_done")
        conv_ready = sem("conv_ready")
        out_done = sem("out_done")

        block = ctx.enter_context(nc.Block())

        def counter(eng):
            taken = {}

            def take(s, by=1):
                taken[s] = taken.get(s, 0) + by
                eng.wait_ge(s, taken[s])
            return take, taken

        @block.sync
        def _(sp):
            sp.dma_start(par[:], par_in).then_inc(inputs_in, 16)
            sp.dma_start(x[:, 0, :], x_in[:, 0, :]).then_inc(x_in_sem[0], 16)
            sp.dma_start(x[:, 1, :], x_in[:, 1, :]).then_inc(x_in_sem[1], 16)
            sp.dma_start(con[:, 0:2 * P], con_in[:, 0:2 * P]).then_inc(inputs_in, 16)
            sp.dma_start(raw[:, 0, :], w_in[0:P, :]).then_inc(unit_in[0], 16)
            for b in range(2, KT):
                sp.dma_start(x[:, b, :], x_in[:, b, :]).then_inc(x_in_sem[b], 16)
            for k in range(1, RING):
                sp.dma_start(raw[:, k, :], w_in[k * P:(k + 1) * P, :]).then_inc(unit_in[k], 16)
            sp.dma_start(con[:, 2 * P:], con_in[:, 2 * P:]).then_inc(constants_in, 16)
            with sp.Fori(1, UNITS // RING) as i:
                for k in range(RING):
                    sp.wait_ge(unit_split, RING * i + (k + 1 - RING))
                    sp.dma_start(raw[:, k, :], w_in[bass.ds((RING * i + k) * P, P), :]).then_inc(unit_in[k], 16)
            for n in range(UNITS // RING * RING, UNITS):
                sp.wait_ge(unit_split, n + 1 - RING)
                sp.dma_start(raw[:, n % RING, :], w_in[n * P:(n + 1) * P, :]).then_inc(unit_in[n % RING], 16)

        @block.gpsimd
        def _(pool):
            def split(k, landed, done, high):
                pool.wait_ge(unit_in[k], landed)
                if done is not None:
                    pool.wait_ge(unit_done, done)
                pool.tensor_tensor(wh[:, k % 2, :], raw[:, k, :], unity[:, 0:1].broadcast_to([P, KT * P]),
                                   ALU.mult).then_inc(high_split, 1)
                pool.wait_ge(high_split, high)
                pool.tensor_tensor(wl[:, k % 2, :], raw[:, k, :], wh[:, k % 2, :].bitcast(F32),
                                   ALU.subtract).then_inc(unit_split, 1)

            pool.memset(unity[:, :], 1.0).then_inc(unity_set, 1)
            pool.wait_ge(unity_set, 1)
            for n in range(RING):
                split(n, 16, None if n < 2 else n - 1, n + 1)
            with pool.Fori(1, UNITS // RING) as i:
                for k in range(RING):
                    split(k, 16 * i + 16, RING * i + k - 1, RING * i + k + 1)
            for n in range(UNITS // RING * RING, UNITS):
                split(n % RING, 16 * (n // RING + 1), n - 1, n + 1)

        @block.tensor
        def _(pe):
            take, taken = counter(pe)
            meetings, blocks_split = [0], [0]

            def meet():
                meetings[0] += 1
                pe.drain().then_inc(at_pe, 1)
                pe.wait_ge(at_act, meetings[0])
                pe.wait_ge(at_dve, meetings[0])

            def products(n, nkt, h, l, width, fresh=None, summing=False, start=0):
                o = gemm_ps[:, n % 2, 0:width]
                for kt in range(start, nkt):
                    if fresh is not None:
                        pe.wait_ge(rhs_ready, fresh + kt + 1)
                    w = slice(kt * P, (kt + 1) * P)
                    pe.matmul(o, wh[:, n % 2, w], h[:, kt, 0:width], start=(kt == 0), stop=False)
                    pe.matmul(o, wh[:, n % 2, w], l[:, kt, 0:width], start=False, stop=False)
                    last = pe.matmul(o, wl[:, n % 2, w], h[:, kt, 0:width], start=False, stop=(kt == nkt - 1))
                    if summing and kt < KT - 1:
                        column_sum(kt)
                last.then_inc(unit_done, 1)
                if summing:
                    column_sum(KT - 1)

            def unit(n, h, l, nkt=KT, width=N):
                pe.wait_ge(unit_split, n + 1)
                if n >= 2:
                    pe.wait_ge(emptied, n - 1)
                products(n, nkt, h, l, width)

            def begun(n, first, end, h, l, fresh=True):
                pe.wait_ge(unit_split, n + 1)
                pe.wait_ge(emptied, n - 1)
                o = gemm_ps[:, n % 2, :]
                for kt in range(first, end):
                    if fresh:
                        pe.wait_ge(rhs_ready, blocks_split[0] + kt + 1)
                    w = slice(kt * P, (kt + 1) * P)
                    pe.matmul(o, wh[:, n % 2, w], h[:, kt, :], start=(kt == 0), stop=False)
                    pe.matmul(o, wh[:, n % 2, w], l[:, kt, :], start=False, stop=False)
                    pe.matmul(o, wl[:, n % 2, w], h[:, kt, :], start=False, stop=False)

            def units(n0, count, h, l, nkt=KT, width=N, fresh=False, summing=False):
                if fresh:
                    pe.wait_ge(unit_split, n0 + 1)
                    if n0 >= 2:
                        pe.wait_ge(emptied, n0 - 1)
                    products(n0, nkt, h, l, width, blocks_split[0], summing)
                    blocks_split[0] += nkt
                    n0, count = n0 + 1, count - 1
                first, pairs = n0, count // 2
                if first < 2:
                    unit(first, h, l, nkt, width)
                    first, pairs = first + 1, (count - 1) // 2
                if pairs:
                    with pe.Fori(0, pairs) as i:
                        for n in (first, first + 1):
                            pe.wait_ge(unit_split, 2 * i + (n + 1))
                            pe.wait_ge(emptied, 2 * i + (n - 1))
                            products(n, nkt, h, l, width)
                for n in range(first + 2 * pairs, n0 + count):
                    unit(n, h, l, nkt, width)

            def column_sum(b, width=N, bank=0):
                take(square_ready)
                pe.matmul(turn_ps[:, bank, 0:width], ones, sq[:, b % 2, 0:width], start=(b == 0),
                          stop=(b == KT - 1)).then_inc(square_used, 1)

            def units_summed(n0, h, l, nkt=KT, fresh=False):
                units(n0, KT, h, l, nkt, fresh=fresh)
                added_sum()

            def added_sum():
                take(square_added, KT - 2)
                pe.matmul(turn_ps[:, 0, :], ones, square_sum, start=True, stop=False)
                take(square_made, KT)
                pe.matmul(turn_ps[:, 0, :], ones, sq[:, (KT - 1) % 2, :], start=False,
                          stop=True).then_inc(square_used, 2)

            def head_norm(nb):
                for b in range(nb):
                    take(square_ready)
                    w = CCOL["stat"] + NSTAT - 2 * b
                    pe.matmul(turn_ps[:, 0, :], con[:, w:w + P], sq[:, b % 2, :], start=(b == 0),
                              stop=(b == nb - 1)).then_inc(square_used, 1)
                spread(nb, roots)

            def spread(nb, rows):
                take(rows_ready)
                for b in range(nb):
                    if b >= 2:
                        take(spread_used)
                    w = CCOL["pair"] + b * P
                    pe.matmul(score_ps[:, b % 2, :], con[:, w:w + P], rows, start=True,
                              stop=True).then_inc(spread_ready, 1)
                take(spread_used, min(2, nb))

            def turn_values(blocks):
                for i, a in enumerate(blocks):
                    if i >= 2:
                        take(copied_v)
                    for t in range(a.shape[1] // P):
                        m = pe.transpose(turn_ps[:, i % 2, t * P:(t + 1) * P], a[:, t * P:(t + 1) * P], ident)
                    m.then_inc(turned_v, 1)
                take(copied_v, min(2, len(blocks)))

            def attention(items, between=lambda i: None):
                groups0 = taken.get(group_used, 0)

                def scores(i, it):
                    if i >= 2:
                        take(exp_ready if it["bias"] is None else scores_used)
                    pe.matmul(score_ps[:, i % 2, 0:it["nk"]], it["q"], it["k"], start=True,
                              stop=True).then_inc(scores_ready, 1)

                def turned(i, it):
                    take(probs_ready)
                    for c in range(it["nk"] // P):
                        m = pe.transpose(turn_ps[:, i % 2, c * P:(c + 1) * P], y[:, i % 3, c * P:(c + 1) * P],
                                         ident)
                    m.then_inc(probs_turned, 1)

                def values(i, it):
                    take(probs_copied)
                    if it["first"] and it["group"] >= 2:
                        pe.wait_ge(group_used, groups0 + it["group"] - 1)
                    o = out_ps[it["rows"], it["group"] % 2, it["tile"] * P:(it["tile"] + 1) * P]
                    chunks = it["nk"] // P
                    for c in range(chunks):
                        m = pe.matmul(o, it["v"][c], y[:, 3 + i % 2, c * P:(c + 1) * P], start=(c == 0),
                                      stop=(c == chunks - 1))
                    m.then_inc(item_done, 1)

                n = len(items)
                for i in range(n + 3):
                    if i < n:
                        scores(i, items[i])
                    if 2 <= i < n + 2:
                        turned(i - 2, items[i - 2])
                    if i >= 3:
                        values(i - 3, items[i - 3])
                    between(i)
                take(exp_ready if items[0]["bias"] is None else scores_used, 2)
                if items[0]["bias"] is not None:
                    taken[exp_ready] = taken.get(exp_ready, 0) + n
                taken[group_used] = groups0 + items[-1]["group"] + 1

            def weighted(h, w, j, **flags):
                return pe.matmul(out_ps[(h % 2) * HD:(h % 2 + 1) * HD, h // 2, j * P:N],
                                 values1[:, j, h * HD:(h + 1) * HD], w[:, j * N + j * P:(j + 1) * N], **flags)

            filled = [0]

            def fill(count=1):
                for _ in range(count):
                    unit(later_unit(filled[0]), xh, xl)
                    filled[0] += 1

            def mlstm():
                turn_values([proj1[:, M_V, :], proj1[:, M_V + 1, :]])
                fill()
                take(gate_rows)
                for t in range(T):
                    m = pe.transpose(turn_ps[:, 0, 4 * t:4 * t + 4], gate_b[0:4, t * P:(t + 1) * P], ident[0:4, 0:4])
                m.then_inc(cols_turned, 1)
                take(cols_ready)
                take(gate_rows)
                take(keys_ready, 2)
                for h in range(4):
                    w = weights[h % 2]
                    kb = (M_K if h % 2 else M_V) + h // 2
                    if h >= 1:
                        take(bound_used)
                    pe.matmul(turn_ps[:, 0, :], con[:, CCOL["row"] + h * P:CCOL["row"] + (h + 1) * P],
                              gate_a, start=True, stop=True).then_inc(bound_ready, 1)
                    if h < FILL_MLSTM - 1:
                        fill()
                    for j in range(T + 2):
                        if j < T:
                            if h > 0 or j >= 2:
                                take(scores_used)
                            pe.matmul(score_ps[:, j % 2, j * P:N], proj1[:, kb, j * P:(j + 1) * P],
                                      proj1[:, M_Q + h // 2, j * P:N], start=True, stop=True).then_inc(scores_ready, 1)
                        if j >= 2:
                            k = j - 2
                            take(weights_ready)
                            weighted(h, w, k, start=(k == 0), stop=(k == T - 1))
                            m = pe.matmul(turn_ps[0:4, 1, k * P:N], con[:, CCOL["col"] + 4 - h:CCOL["col"] + 8 - h],
                                          w[:, k * N + k * P:(k + 1) * N], start=(h == 0 and k == 0),
                                          stop=(h == 3 and k == T - 1), skip_group_check=True)
                    m.then_inc(weights_used, 1)
                take(scores_used, 2)
                take(bound_used)
                spread(2, gate_b)

            def hgrn():
                fill(1)
                pe.wait_ge(bias_added, 4)
                turn_values([proj1[:, H_I, :], proj1[:, H_I + 1, :]])
                fill(FILL_START - 1)
                for b in range(2):
                    take(level_ready)
                    q1, q2, q3 = level_kq[1][2], edge[:, 0, :], edge[:, 1, :]
                    for s in range(2):
                        for j, i, q in ((0, 1, q1), (1, 2, q1), (2, 3, q1), (0, 2, q2), (1, 3, q2), (0, 3, q3)):
                            bank, col = (0, i * P) if j == 0 else (1, (i if j == 1 else 0) * P)
                            m = pe.matmul(turn_ps[:, bank, col:col + P], level_kq[1][s][:, j * P:(j + 1) * P],
                                          q[:, i * P:(i + 1) * P], start=True, stop=True)
                        m.then_inc(far_ready, 1)
                        take(far_copied)
                    for lev in range(len(LEVELS) + 1):
                        take(level_ready)
                        for s in range(2):
                            kk, qq = level_kq[lev % 2][s], level_kq[lev % 2][2]
                            if lev:
                                take(scores_used)
                            for j in range(T):
                                t = slice(j * P, (j + 1) * P)
                                m = pe.matmul(score_ps[:, s, t], kk[:, t], qq[:, t], start=True, stop=True)
                            m.then_inc(scores_ready, 1)
                        if lev in FILL_LEVELS:
                            fill()
                    take(scores_used, 2)
                    for s in range(2):
                        for j in range(T):
                            m = weighted(2 * b + s, weights[s], j, start=(j == 0), stop=(j == T - 1))
                    m.then_inc(weights_used, 1)

            def retention(h, s):
                v0, v1 = (head_in[h % 2][:, b, :] for b in (2, 3))

                def scores(j):
                    for i, (kp, qp) in enumerate(((0, 0), (0, 1), (1, 0))):
                        m = pe.matmul(score_ps[:, j % 2, :], ret_qk[kp][:, 1, j * P:(j + 1) * P], ret_qk[qp][:, 0, :],
                                      start=(i == 0), stop=(i == 2))
                    m.then_inc(scores_ready, 1)

                def values(j):
                    take(weights_ready)
                    for c in range(2):
                        for i, (vp, wp) in enumerate(((0, 0), (0, 1), (1, 0))):
                            m = pe.matmul(out_ps[:, c, :], values_hl[vp][:, j, c * P:(c + 1) * P], ret_w[wp][:, j, :],
                                          start=(j == 0 and i == 0), stop=(j == T - 1 and i == 2))
                    if j == T - 1:
                        m.then_inc(weights_used, 1)

                if s == 0:
                    pe.wait_ge(emptied, ret_unit(h) + 4)
                    if h:
                        take(ret_std)
                    for i, a in enumerate((v0, v1)):
                        for t in range(T):
                            m = pe.transpose(turn_ps[:, i, t * P:(t + 1) * P], a[:, t * P:(t + 1) * P], ident)
                    m.then_inc(head_turned, 1)
                    take(keys_low)
                    scores(0)
                    scores(1)
                elif s < 3:
                    take(tile_weighted)
                    scores(s + 1)
                    if s == 2:
                        take(values_low)
                        if h:
                            take(head_done)
                        values(0)
                elif s == 3:
                    take(tile_weighted, 2)
                    for j in (1, 2, 3):
                        values(j)
                elif s == 4:
                    take(square_added)
                    pe.matmul(turn_ps[:, 0, :], ones, sq[:, 0, :], start=True, stop=True).then_inc(square_used, 1)
                    take(square_made, 2)

            pe.wait_ge(inputs_in, 32)
            meet()
            units(FIRST["in"], 1 + len(FIRST_BLOCKS), xh, xl, fresh=True, summing=True)
            hgrn()
            meet()
            mlstm()
            meet()
            for kt in range(KT):
                column_sum(kt, M, 1)
            head_norm(4)
            meet()
            turn_values([proj1[:, A_V, :], proj1[:, A_V + 1, :]])
            take(keys_ready, 2)

            def early_memory(i):
                if i % 3 == 1 and i // 3 < KV_EARLY:
                    unit(memory_unit(i // 3), mem_h, mem_l, width=M)
            attention(attention_items("moba"), early_memory)
            meet()
            units(FIRST["mix"], KT, xh, xl)
            added_sum()
            for u in range(KV_EARLY, 8):
                unit(memory_unit(u), mem_h, mem_l, width=M)
            units(FIRST["cross_q"], 4, xh, xl, fresh=True, summing=True)
            meet()
            turn_values([cross_vf[:, b, :] for b in range(4)])
            attention(attention_items("cross"))
            meet()
            for n in range(FIRST["co"], FIRST["co"] + U_CO):
                pe.wait_ge(unit_split, n + 1)
                pe.wait_ge(emptied, n - 1)
                for i, o in enumerate((score_ps[:, n % 2, :], gemm_ps[:, n % 2, :])):
                    for kt in range(4):
                        w = slice((4 * i + kt) * P, (4 * i + kt + 1) * P)
                        pe.matmul(o, wh[:, n % 2, w], xh[:, kt, :], start=(kt == 0), stop=False)
                        pe.matmul(o, wh[:, n % 2, w], xl[:, kt, :], start=False, stop=False)
                        last = pe.matmul(o, wl[:, n % 2, w], xh[:, kt, :], start=False, stop=(kt == 3))
                last.then_inc(unit_done, 1)
            added_sum()
            units(FIRST["fup0"], 1, xh, xl, fresh=True, summing=True)
            units(FIRST["fup0"] + 1, 2 * FF1_PARTS[0] - 1, xh, xl)
            for p in (1, 2):
                units(FIRST[f"fup{p}"], 2 * FF1_PARTS[p], xh, xl)
                units(FIRST[f"fdown{p - 1}"], KT, *hidden[(p - 1) % 2], nkt=FF1_PARTS[p - 1], fresh=True)
            units_summed(FIRST["fdown2"], *hidden[0], nkt=FF1_PARTS[2], fresh=True)
            units(FIRST["even_in"], 6, xh, xl, fresh=True, summing=True)
            pe.wait_ge(emptied, FIRST["even_in"] + 6)
            turn_values([proj2[:, E_AV, :]])
            head_norm(5)
            take(keys_ready)

            def neighbour_unit(i):
                if i % 3 == 1 and i // 3 < 12:
                    unit(FIRST["even_in"] + 6 + i // 3, xh, xl)
            attention(attention_items("window"), neighbour_unit)
            meet()
            turn_values([proj2[:, E_BV + b, :] for b in range(4)])
            head_norm(8)
            take(keys_ready, 4)
            meet()
            out = FIRST["even_out"]

            def window_part(i):
                if i in (8, 14, 20, 26):
                    k = (i - 8) // 6
                    begun(out + k // 2, 2 * (k % 2), 2 * (k % 2) + 2, xh, xl, fresh=False)
            attention(attention_items("neighbour"), window_part)
            meet()
            for n in (out, out + 1):
                products(n, KT, xh, xl, N, start=4)
            units(out + 2, KT - 2, xh, xl)
            added_sum()
            units(FIRST["mup0"], 1, mh, ml, fresh=True)
            units(FIRST["mup0"] + 1, 7, mh, ml)
            for p in (1, 2, 3):
                units(FIRST[f"mup{p}"], 8, mh, ml)
                units(FIRST[f"mdown{p - 1}"], KT, *hidden[(p - 1) % 2], fresh=True)
            units_summed(FIRST["mdown3"], *hidden[1], fresh=True)
            for h in range(RH):
                for u in range(U_HEAD):
                    if h == 0 and u == 0:
                        units(ret_unit(0), 1, xh, xl, fresh=True)
                    else:
                        unit(ret_unit(h) + u, xh, xl)
                    if h:
                        retention(h - 1, u)
                if h == RH // 2:
                    units(FIRST["odd_out0"], KT, ret_h, ret_l, fresh=True)
            out1 = FIRST["odd_out1"]
            for s in range(U_HEAD):
                retention(RH - 1, s)
                for n, at, first, end in ((out1, 0, 0, 6), (out1 + 1, 3, 0, 2), (out1 + 1, 4, 2, 6)):
                    if s == at:
                        begun(n, first, end, ret_h, ret_l)
            for n in (out1, out1 + 1):
                products(n, KT, ret_h, ret_l, N, blocks_split[0], start=KT - 2)
            blocks_split[0] += KT
            units(out1 + 2, KT - 2, ret_h, ret_l)
            added_sum()
            take(ret_std)
            take(head_done)
            units(FIRST["nup0"], 8, xh, xl, fresh=True)
            for p in (1, 2, 3):
                units(FIRST[f"nup{p}"], 8, xh, xl)
                units(FIRST[f"ndown{p - 1}"], KT, *hidden[(p - 1) % 2], fresh=True)
            units(FIRST["ndown3"], KT, *hidden[1], fresh=True)
            meet()

        @block.scalar
        def _(act):
            take, taken = counter(act)
            meetings, steps = [0], [0]

            def meet():
                meetings[0] += 1
                act.drain().then_inc(at_act, 1)
                act.wait_ge(at_pe, meetings[0])
                act.wait_ge(at_dve, meetings[0])

            def step(ins):
                steps[0] += 1
                ins.then_inc(act_step, 1)
                act.wait_ge(act_step, steps[0])

            def squares(src, nb, width=N):
                for b in range(nb):
                    if b >= 2:
                        take(square_used)
                    act.activation(sq[:, b % 2, 0:width], src[b], ACT.Square).then_inc(square_ready, 1)
                take(square_used, min(2, nb))

            def prepare(src, gain, h, ready=None, added=False):
                base = taken.get(square_added, 0)
                act.activation(eps[:, 3:4], eps[:, 0:1], ACT.Sqrt)
                for b in range(KT):
                    high_and_square(src, gain, h, b, ready, base=base if added else None)
                if added:
                    taken[square_added] = base + KT - 2
                finish_norm(rstd[:, :])

            def high_and_square(src, gain, h, b, ready=None, width=N, base=None):
                if ready is not None:
                    ready(b)
                if h is not None:
                    act.activation(h[:, b, 0:width], src[:, b, 0:width], ACT.Copy,
                                   scale=p_(gain, b)).then_inc(high_made, 1)
                if b >= 2:
                    if base is None:
                        take(square_used)
                    else:
                        act.wait_ge(square_added, base + max(1, b - 2))
                act.activation(sq[:, b % 2, 0:width], src[:, b, 0:width],
                               ACT.Square).then_inc(square_ready if base is None else square_made, 1)

            def finish_norm(dst, width=N, bank=0):
                take(square_used, 2)
                act.activation(dst, turn_ps[:, bank, 0:width], ACT.Sqrt, bias=eps[:, 0:1],
                               scale=1.0 / D).then_inc(std_ready, 1)

            def stored(n0):
                return lambda b: act.wait_ge(emptied, n0 + b + 1)

            def head_norm(src):
                squares(src, len(src))
                act.activation(roots, turn_ps[:, 0, :], ACT.Sqrt, bias=eps[:, 0:1],
                               scale=1.0 / HD).then_inc(std_ready, 1)

            def copy_values(dst):
                for i, o in enumerate(dst):
                    take(turned_v)
                    w = o.shape[1] * P
                    act.activation(o, turn_ps[:, i % 2, 0:w].rearrange("p (t c) -> p t c", c=P),
                                   ACT.Identity).then_inc(copied_v, 1)

            def attention(items, whole=False):
                items0 = taken.get(item_done, 0)

                def exps(i, it):
                    take(logits_ready)
                    s, a = 8 * (i % 3), y[:, i % 3, 0:it["nk"]]
                    if it["sink"] is not None:
                        act.activation(small[:, s + 2:s + 3], it["sink"], ACT.Exp, bias=small[:, s:s + 1], scale=-1.0)
                    act.activation(a, score_ps[:, i % 2, 0:it["nk"]] if it["bias"] is None else a, ACT.Exp,
                                   bias=small[:, s:s + 1], accum_out=small[:, s + 1:s + 2]).then_inc(exp_ready, 1)

                def copies(i, it):
                    take(probs_turned)
                    if i >= 2:
                        act.wait_ge(item_done, items0 + i - 1)
                    act.activation(y[:, 3 + i % 2, 0:it["nk"]], turn_ps[:, i % 2, 0:it["nk"]],
                                   ACT.Identity).then_inc(probs_copied, 1)

                def outputs(i, it):
                    act.wait_ge(item_done, items0 + i + 1)
                    if whole:
                        act.activation(y[:, 5 + it["group"], :], out_ps[:, it["group"] % 2, :],
                                       ACT.Identity).then_inc(high_ready, 1)
                        return
                    o, a = xh[:, it["to"], :], out_ps[:, it["group"] % 2, :]
                    if it["turned"]:
                        o = o.rearrange("p (r c) -> p c r", r=8)
                        a = a.rearrange("p (c r) -> p c r", r=8)
                    act.activation(o, a, ACT.Identity).then_inc(high_ready, 1)

                n = len(items)
                for i in range(n + 4):
                    if i < n:
                        exps(i, items[i])
                    if 2 <= i < n + 2:
                        copies(i - 2, items[i - 2])
                    if i >= 4 and items[i - 4]["last"]:
                        outputs(i - 4, items[i - 4])
                taken[item_done] = items0 + n

            filled = [0]

            def add_bias(n, b):
                act.wait_ge(emptied, n + 1)
                act.activation(proj1[:, b, :], proj1[:, b, :], ACT.Identity,
                               bias=p_("b_in", b)).then_inc(bias_added, 1)

            def fill(count=1):
                for _ in range(count):
                    add_bias(later_unit(filled[0]), LATER_BLOCKS[filled[0]])
                    filled[0] += 1

            def mlstm():
                f = slice(32, 36)
                step(act.activation(gate_a[f, :], gates[f, :], ACT.Abs))
                step(act.activation(gate_a[f, :], gate_a[f, :], ACT.Exp, scale=-1.0))
                act.activation(gate_b[f, :], gate_a[f, :], ACT.Ln, bias=1.0).then_inc(gate_fun, 1)
                copy_values([values1[:, :, b * P:(b + 1) * P] for b in range(2)])
                act.drain().then_inc(values_free, 1)
                fill()
                take(cols_turned)
                act.activation(small[:, 32:48], turn_ps[:, 0, 0:16], ACT.Identity).then_inc(cols_ready, 1)
                take(gate_arg)
                step(act.activation(gates[0:4, :], gates[0:4, :], ACT.Exp, scale=-1.0))
                for h in range(4):
                    take(bound_used)
                    for j in range(T):
                        m = act.activation(edge[:, j, j * P:N], edge[:, j, j * P:N], ACT.Exp)
                    m.then_inc(gate_fun, 1)
                    if h < FILL_MLSTM - 1:
                        fill()
                take(weights_used, 4)
                act.activation(gate_g[0:4, :], turn_ps[0:4, 1, :], ACT.Abs).then_inc(gate_fun, 1)
                for b in range(2):
                    step(act.activation(proj1[:, M_O + b, :], proj1[:, M_O + b, :], ACT.Sigmoid))

            def hgrn():
                first = [(FIRST["in"] + 1 + i, b) for i, b in enumerate(FIRST_BLOCKS)]
                for n, b in first[0:2]:
                    add_bias(n, b)
                take(gate_arg)
                act.activation(small[:, 18:20], small[:, 16:18], ACT.Exp).then_inc(gate_fun, 1)
                act.wait_ge(bias_added, 2)
                for b in range(2):
                    m = act.activation(proj1[:, H_F + b, :], proj1[:, H_F + b, :], ACT.Sigmoid)
                m.then_inc(gate_fun, 1)
                take(gate_arg)
                for b in range(2):
                    m = act.activation(log_decay[:, b, :], proj1[:, H_F + b, :], ACT.Ln)
                m.then_inc(gate_fun, 1)
                for n, b in first[2:]:
                    add_bias(n, b)
                act.wait_ge(bias_added, len(first))
                for b in range(2):
                    act.activation(proj1[:, H_Q + b, :], proj1[:, H_Q + b, :], ACT.Silu)
                    m = act.activation(proj1[:, H_G + b, :], proj1[:, H_G + b, :], ACT.Silu)
                m.then_inc(gate_fun, 1)
                copy_values([values1[:, :, b * P:(b + 1) * P] for b in range(2)])
                act.drain().then_inc(values_free, 1)
                take(gate_arg)
                for b in range(2):
                    g = log_decay[:, b, :]
                    for j in range(T):
                        t = slice(j * P, (j + 1) * P)
                        act.activation(edge[:, 0, t], g[:, t], ACT.Exp, bias=g[:, (j + 1) * P - 1:(j + 1) * P],
                                       scale=-1.0)
                    act.activation(edge[:, 1, :], g, ACT.Exp)
                    act.activation(small[:, 24:28], g[:, P - 1:N:P], ACT.Exp).then_inc(gate_fun, 1)
                    if not b:
                        fill(FILL_START)
                    take(gate_arg)
                    act.activation(edge[:, 2, :], edge[:, 3, :], ACT.Exp).then_inc(gate_fun, 1)
                    if b:
                        take(weights_used)
                    for s in range(2):
                        take(far_ready)
                        w = weights[s]
                        act.activation(w[:, P:N], turn_ps[:, 0, P:N], ACT.Identity)
                        act.activation(w[:, N + 2 * P:2 * N], turn_ps[:, 1, 2 * P:N], ACT.Identity)
                        act.activation(w[:, 2 * N + 3 * P:3 * N], turn_ps[:, 1, 0:P],
                                       ACT.Identity).then_inc(far_copied, 1)
                    for lev in range(len(LEVELS)):
                        if lev:
                            take(gate_arg)
                            act.activation(edge[:, 2, :], edge[:, 3, :], ACT.Exp).then_inc(gate_fun, 1)
                        if lev - 2 in FILL_LEVELS:
                            fill()
                    fill(sum(lev in FILL_LEVELS for lev in (5, 6)))
                take(weights_used)
                for b in range(2):
                    step(act.activation(mixed[:, b, :], out_ps[:, b, :], ACT.Identity))

            def make_decay():
                take(gate_arg)
                act.activation(decay, decay, ACT.Exp).then_inc(gate_fun, 1)

            def high(j):
                take(tile_weighted)
                act.activation(ret_w[0][:, j, :], tmp[:, j % 2, :], ACT.Copy).then_inc(weights_high, 1)

            def retention(h, s):
                if s == 0:
                    take(head_turned)
                    take(mean_ready)
                    a = turn_ps[:, :, :].rearrange("p b (t c) -> p t b c", c=P)
                    for t in range(T):
                        m = act.activation(values_hl[0][:, t, :].rearrange("p (b c) -> p b c", c=P), a[:, t],
                                           ACT.Identity, bias=small[:, 8 + t:9 + t])
                    m.then_inc(values_high, 1)
                    high(0)
                elif s < 3:
                    high(s)
                elif s == 3:
                    if h + 1 == RH:
                        act.activation(eps[:, 3:4], eps[:, 0:1], ACT.Sqrt)
                    high(3)
                    take(weights_used)
                    for c in range(2):
                        act.activation(sq[:, c, :], out_ps[:, c, :], ACT.Square).then_inc(square_made, 1)
                elif s == 4:
                    take(square_used)
                    take(square_added)
                    act.activation(rstd_r[:, :], turn_ps[:, 0, :], ACT.Sqrt, bias=eps[:, 1:2],
                                   scale=1.0 / G).then_inc(ret_std, 1)
                    if h + 1 < RH:
                        make_decay()

            def mlp(name, p):
                for b in range(FF2_PARTS[p]):
                    n = FIRST[f"{name}up{p}"] + b
                    act.wait_ge(emptied, n + 1)
                    step(act.activation(sq[:, b % 2, :], tmp[:, b % 2, :], ACT.Square))
                    act.activation(hidden[p % 2][0][:, b, :], sq[:, b % 2, :], ACT.Copy).then_inc(hidden_raw, 1)

            def gated():
                for b in range(sum(FF1_PARTS)):
                    take(conv_ready)
                    act.activation(sq[:, b % 2, :], tmp[:, b % 2, :], ACT.Silu,
                                   bias=p_("ffn_conv_b", b)).then_inc(hidden_raw, 1)

            act.wait_ge(inputs_in, 32)
            meet()
            prepare(x, "norm_mix_pre", xh, lambda b: act.wait_ge(x_in_sem[b], 16))
            act.wait_ge(emptied, FIRST["in"] + 1)
            act.activation(gates[0:HD, :], gates[0:HD, :], ACT.Identity, bias=p_("b_gates", 0, 0, HD))
            hgrn()
            meet()
            act.dma_start(arena[:, 20 * N:24 * N], mem_in).then_inc(memory_in, 16)
            mlstm()
            meet()
            act.wait_ge(memory_in, 16)
            for b in range(KT):
                high_and_square(mem_raw, "mem_norm", mem_h, b, width=M)
            finish_norm(mem_rstd, M, 1)
            head_norm([m[:, b, :] for m in (mixed, mixed_m) for b in range(2)])
            take(conv_done)
            act.dma_start(arena[:, 8 * N:12 * N], moba_in).then_inc(moba_table_in, 16)
            meet()
            copy_values([values1[:, :, b * P:(b + 1) * P] for b in range(2)])
            act.drain().then_inc(values_free, 1)
            attention(attention_items("moba"))
            meet()
            prepare(y, None, None, stored(FIRST["mix"]), added=True)
            prepare(x, "norm_cross_pre", xh, lambda b: take(block_ready))
            meet()
            copy_values([cross_v[:, :, b * P:(b + 1) * P] for b in range(4)])
            attention(attention_items("cross"))
            meet()
            prepare(y, None, None, lambda b: act.wait_ge(emptied, FIRST["co"] + b // 2 + 1), added=True)
            prepare(x, "norm_ffn_pre", xh, lambda b: take(block_ready))
            gated()
            act.wait_ge(emptied, FIRST["fdown1"] + KT)
            act.dma_start(arena[:, 23 * N:29 * N], alibi_in).then_inc(layer_tables_in, 16)
            act.dma_start(na_all, na_in).then_inc(layer_tables_in, 16)
            prepare(y, None, None, stored(FIRST["fdown2"]), added=True)
            prepare(x, "attn_norm_e_2", xh, lambda b: take(block_ready))
            copy_values([values_a])
            act.drain().then_inc(values_free, 1)
            take(proj_raw)
            head_norm([proj2[:, E_AQ + b, :] for b in range(5)])
            attention(attention_items("window"), whole=True)
            meet()
            copy_values([values_b[:, :, b * P:(b + 1) * P] for b in range(4)])
            head_norm([proj2[:, E_BQ + b, :] for b in range(8)])
            meet()
            attention(attention_items("neighbour"))
            meet()
            prepare(x, "mlp0", mh, stored(FIRST["even_out"]), added=True)
            for p in range(4):
                mlp("m", p)
            act.wait_ge(emptied, FIRST["mdown2"] + KT)
            prepare(x, "ret_norm_o_2", xh, stored(FIRST["mdown3"]), added=True)
            act.dma_start(dist, dist_in).then_inc(distances_in, 16)
            step(act.activation(small[:, 16:32], par[:, PCOL["dec_f"]:PCOL["dec_f"] + 16], ACT.Abs))
            step(act.activation(small[:, 16:32], small[:, 16:32], ACT.Exp, scale=-1.0))
            act.activation(small[:, 32:48], small[:, 16:32], ACT.Ln, bias=1.0).then_inc(gate_fun, 1)
            make_decay()
            for h in range(RH):
                for u in range(U_HEAD):
                    if u == 4:
                        act.wait_ge(emptied, ret_unit(h) + 2)
                        act.activation(ret_qk[0], head_in[h % 2][:, 0:2, :], ACT.Copy).then_inc(keys_high, 1)
                    if u >= 4:
                        act.wait_ge(emptied, ret_unit(h) + u + 1)
                        a = head_in[h % 2][:, u, :]
                        act.activation(a, a, ACT.Silu).then_inc(proj_ready, 1)
                    if h:
                        retention(h - 1, u)
            for s in range(U_HEAD):
                retention(RH - 1, s)
            prepare(x, "mlp1", xh, stored(FIRST["odd_out1"]), added=True)
            for p in range(4):
                mlp("n", p)
            for b in range(KT):
                act.wait_ge(emptied, FIRST["ndown3"] + b + 1)
                act.dma_start(out[:, b, :], x[:, b, :]).then_inc(out_done, 16)
            meet()
            act.wait_ge(out_done, 16 * KT)

        @block.vector
        def _(dve):
            take, taken = counter(dve)
            meetings = [0]

            def meet():
                meetings[0] += 1
                dve.drain().then_inc(at_dve, 1)
                dve.wait_ge(at_pe, meetings[0])
                dve.wait_ge(at_act, meetings[0])

            def done(ins, s=dve_step):
                ins.then_inc(s, 1)
                take(s)

            def stt(o, a, scalar, b, op0, op1, s=dve_step):
                done(dve.scalar_tensor_tensor(out=o, in0=a, scalar=scalar, in1=b, op0=op0, op1=op1), s)

            def split(a, h, l, s=dve_step):
                done(dve.tensor_copy(h, a))
                done(dve.tensor_tensor(l, a, h.bitcast(F32), ALU.subtract), s)

            def low(src, gain, h, l, b, s=rhs_ready, width=N):
                take(high_made)
                stt(l[:, b, 0:width], src[:, b, 0:width], p_(gain, b), h[:, b, 0:width].bitcast(F32), ALU.mult,
                    ALU.subtract, s)

            def inverse(a=None):
                a = rstd[:, :] if a is None else a
                take(std_ready)
                done(dve.reciprocal(a, a))

            def add_normed(post, pre, b):
                stt(tmp[:, b % 2, :], y[:, b, :], p_(post, b), rstd[:, :], ALU.mult, ALU.mult)
                done(dve.tensor_tensor(x[:, b, :], x[:, b, :], tmp[:, b % 2, :], ALU.add), block_ready)
                if b:
                    low(x, pre, xh, xl, b - 1)

            def scaled(n, dst, s=None, rows=P, width=N, rs=None, factor=1.0, src=None):
                dve.wait_ge(unit_done, n + 1)
                a = gemm_ps[0:rows, n % 2, 0:width]
                r = (rstd if rs is None else rs)[0:rows, 0:width]
                if src is not None:
                    a, r = src(a), src(r)
                stt(dst, a, factor, r, ALU.mult, ALU.mult, emptied)

            def head_rows():
                take(std_ready)
                done(dve.reciprocal(roots, roots), rows_ready)

            def head_norm(blocks, gains):
                head_rows()
                for b, a in enumerate(blocks):
                    take(spread_ready)
                    stt(a, a, gains[b], score_ps[:, b % 2, :], ALU.mult, ALU.mult, spread_used)

            filled = [0]

            def fill(count=1):
                for _ in range(count):
                    scaled(later_unit(filled[0]), proj1[:, LATER_BLOCKS[filled[0]], :])
                    filled[0] += 1

            def mixers_out():
                head_rows()
                b = 0
                for out, gain, gate in ((mixed, "hgrn_norm", H_G), (mixed_m, "mlstm_norm", M_O)):
                    for i in range(2):
                        take(spread_ready)
                        stt(tmp[:, i, :], out[:, i, :], p_(gain, i), score_ps[:, b % 2, :], ALU.mult, ALU.mult,
                            spread_used)
                        done(dve.tensor_tensor(proj1[:, gate + i, :], tmp[:, i, :], proj1[:, gate + i, :], ALU.mult))
                        b += 1

            def add_square(b):
                take(square_made)
                if b == 1:
                    done(dve.tensor_tensor(square_sum, sq[:, 0, :], sq[:, 1, :], ALU.add), square_added)
                elif 1 < b < KT - 1:
                    done(dve.tensor_tensor(square_sum, square_sum, sq[:, b % 2, :], ALU.add), square_added)

            def store(n0, first, squared=False):
                for b in range(KT):
                    store_one(n0, b, first)
                    if squared:
                        add_square(b)

            def store_one(n0, b, first):
                dve.wait_ge(unit_done, n0 + b + 1)
                ps = gemm_ps[:, (n0 + b) % 2, :]
                if first:
                    done(dve.tensor_copy(y[:, b, :], ps), emptied)
                else:
                    done(dve.tensor_tensor(y[:, b, :], y[:, b, :], ps, ALU.add), emptied)

            def add(n0, gain=None, h=None, l=None):
                for b in range(KT):
                    dve.wait_ge(unit_done, n0 + b + 1)
                    done(dve.tensor_tensor(x[:, b, :], x[:, b, :], gemm_ps[:, (n0 + b) % 2, :], ALU.add), emptied)
                    if gain:
                        low(x, gain, h, l, b)
                        add_square(b)

            def part_heads(k, other):
                done(dve.tensor_scalar(other, k, c_("half", 2)[:, 0:1], None, ALU.mult))
                done(dve.tensor_scalar(k, k, c_("half", 2)[:, 1:2], None, ALU.mult), keys_ready)

            def attention(items, between=lambda i: None, whole=False):
                def logits(i, it):
                    take(scores_ready)
                    s = 8 * (i % 3)
                    ps, top = score_ps[:, i % 2, 0:it["nk"]], small[:, s:s + 1]
                    if i >= 3:
                        take(probs_turned)
                    if it["bias"] is None:
                        done(dve.tensor_reduce(top, ps, AX_X, ALU.max, negate=True), logits_ready)
                        return
                    done(dve.tensor_tensor_reduce(y[:, i % 3, 0:it["nk"]], ps, it["bias"], 1.0, LEAST, ALU.add,
                                                  ALU.max, small[:, s + 4:s + 5]), scores_used)
                    if it["sink"] is None:
                        done(dve.tensor_scalar(top, small[:, s + 4:s + 5], -1.0, None, ALU.mult), logits_ready)
                    else:
                        stt(top, small[:, s + 4:s + 5], -1.0, it["sink"], ALU.mult, ALU.min, logits_ready)

                def divide(i, it):
                    take(exp_ready)
                    s = 8 * (i % 3)
                    total, a = small[:, s + 1:s + 2], y[:, i % 3, 0:it["nk"]]
                    if it["sink"] is not None:
                        done(dve.tensor_tensor(total, total, small[:, s + 2:s + 3], ALU.add))
                    done(dve.reciprocal(small[:, s + 3:s + 4], total))
                    done(dve.tensor_scalar(a, a, small[:, s + 3:s + 4], None, ALU.mult), probs_ready)

                def outputs(it):
                    take(high_ready)
                    if whole:
                        done(dve.memset(eps[:, 2:3], 0.0), group_used)
                        return
                    h, l, a = xh[:, it["to"], :], xl[:, it["to"], :], out_ps[:, it["group"] % 2, :]
                    if it["turned"]:
                        h, l = (v.rearrange("p (r c) -> p c r", r=8) for v in (h, l))
                        a = a.rearrange("p (c r) -> p c r", r=8)
                    done(dve.tensor_tensor(l, a, h.bitcast(F32), ALU.subtract), group_used)

                n = len(items)
                for i in range(n + 4):
                    if i < n:
                        logits(i, items[i])
                    if 1 <= i <= n:
                        divide(i - 1, items[i - 1])
                    if i >= 4 and items[i - 4]["last"]:
                        outputs(items[i - 4])
                    between(i)
                take(probs_turned, 3)

            def mlstm():
                f, r = slice(32, 36), slice(0, 4)
                one = edge[:, 0, :]
                done(dve.memset(one, 1.0))
                done(dve.tensor_scalar(gate_g[f, :], gates[f, :], 0.0, None, ALU.min))
                short_conv(0)
                take(gate_fun)
                done(dve.tensor_tensor(gate_g[f, :], gate_g[f, :], gate_b[f, :], ALU.subtract))
                done(dve.tensor_tensor_scan(gate_a[f, :], one[f, :], gate_g[f, :], 0.0,
                                            ALU.mult, ALU.add))
                done(dve.tensor_copy(gate_g[r, :], gate_a[f, :]))
                done(dve.tensor_tensor(gate_b[r, :], gates[r, :], gate_g[r, :], ALU.subtract), gate_rows)
                done(dve.tensor_tensor_scan(gate_a[r, :], one[r, :], gate_b[r, :], 0.0,
                                            ALU.mult, ALU.max))
                done(dve.tensor_tensor(gates[r, :], gate_g[r, :], gate_a[r, :], ALU.add), gate_arg)
                done(dve.tensor_scalar(gate_a[r, :], gate_a[r, :], -1.0, None, ALU.mult), gate_rows)
                take(values_free)
                for b in range(2):
                    part_heads(proj1[:, M_K + b, :], proj1[:, M_V + b, :])
                short_conv(1)
                fill()
                take(cols_ready)
                for h in range(4):
                    take(bound_ready)
                    for j in range(T):
                        m = dve.tensor_scalar(edge[:, j, j * P:N], turn_ps[:, 0, j * P:N],
                                              small[:, 32 + 4 * j + h:33 + 4 * j + h], 0.0, ALU.add, ALU.min)
                    done(m, bound_used)
                    if h < FILL_MLSTM - 1:
                        fill()
                    take(gate_fun)
                    if h >= 2:
                        take(weights_used)
                    w = weights[h % 2]
                    for j in range(T):
                        take(scores_ready)
                        done(dve.tensor_tensor(w[:, j * N + j * P:(j + 1) * N], score_ps[:, j % 2, j * P:N],
                                               edge[:, j, j * P:N], ALU.mult), scores_used)
                        d = w[:, j * N + j * P:j * N + (j + 1) * P]
                        done(dve.tensor_tensor(d, d, c_("tri", P), ALU.mult), weights_ready)
                take(weights_used, 2)
                take(gate_fun)
                done(dve.tensor_tensor(gate_g[r, :], gate_g[r, :], gates[r, :], ALU.max))
                done(dve.reciprocal(gate_b[r, :], gate_g[r, :]), rows_ready)
                for b in range(2):
                    take(spread_ready)
                    done(dve.tensor_copy(tmp[:, b, :], score_ps[:, b, :]), spread_used)
                    done(dve.tensor_tensor(mixed_m[:, b, :], out_ps[:, b, :], tmp[:, b, :], ALU.mult))

            def short_conv(b):
                u, t = conv_padded, log_decay[:, 0, :]
                done(dve.memset(u[:, 0:2], 0.0))
                done(dve.tensor_tensor(u[:, 2:N + 2], proj1[:, C_C + b, :], proj1[:, C_H + b, :], ALU.mult))
                convolve(t, u, [p_("sconv_w", 2 * k + b) for k in range(3)])
                done(dve.tensor_tensor(proj1[:, C_H + b, :], t, proj1[:, C_B + b, :], ALU.mult),
                     conv_done if b else dve_step)

            def convolve(o, u, w, s=dve_step):
                done(dve.tensor_scalar(o, u[:, 0:N], w[0], None, ALU.mult))
                stt(o, u[:, 1:N + 1], w[1], o, ALU.mult, ALU.add)
                stt(o, u[:, 2:N + 2], w[2], o, ALU.mult, ALU.add, s)

            def hgrn():
                lb = par[:, PCOL["hgrn_lb"]:PCOL["hgrn_lb"] + 2]
                a, e, r = small[:, 16:18], small[:, 18:20], small[:, 20:22]
                first = [(FIRST["in"] + 1 + i, proj1[:, b, :]) for i, b in enumerate(FIRST_BLOCKS)]
                for n, o in first[0:2]:
                    scaled(n, o)
                done(dve.tensor_tensor(a, lb, lb, ALU.subtract), gate_arg)
                take(gate_fun)
                done(dve.reciprocal(r, e))
                done(dve.tensor_tensor(a, e, r, ALU.mult))
                done(dve.tensor_tensor(e, a, a, ALU.subtract))
                done(dve.tensor_scalar(r, e, -1.0, 1.0, ALU.mult, ALU.add))
                take(gate_fun)
                for b in range(2):
                    f = proj1[:, H_F + b, :]
                    done(dve.tensor_scalar(f, f, r[:, b:b + 1], e[:, b:b + 1], ALU.mult, ALU.add),
                         gate_arg if b else dve_step)
                for n, o in first[2:4]:
                    scaled(n, o)
                for w in (*weights, gate_a, gate_b):
                    done(dve.memset(w, 0.0))
                reset = edge[:, 3, :]
                done(dve.memset(reset, 1.0))
                done(dve.memset(reset.rearrange("p (t c) -> p t c", c=P)[:, :, 0:1], 0.0))
                take(gate_fun)
                for b in range(2):
                    g = log_decay[:, b, :]
                    done(dve.tensor_tensor_scan(g, reset, g, 0.0, ALU.mult, ALU.add), gate_arg if b else dve_step)
                for n, o in first[4:]:
                    scaled(n, o)
                take(gate_fun)
                take(values_free)
                dve.wait_ge(constants_in, 16)
                for b in range(2):
                    k, k0 = proj1[:, H_F + b, :], proj1[:, H_I + b, :]
                    done(dve.tensor_scalar(k, k, -1.0, 1.0, ALU.mult, ALU.add))
                    w = CCOL["stat"] + NSTAT
                    done(dve.tensor_scalar(k0, k, con[:, w:w + 1], None, ALU.mult))
                    done(dve.tensor_scalar(k, k, con[:, w + 1:w + 2], None, ALU.mult))
                for b in range(2):
                    q, g = proj1[:, H_Q + b, :], log_decay[:, b, :]
                    keys = (proj1[:, H_I + b, :], proj1[:, H_F + b, :])
                    q1, q2, q3 = level_kq[1][2], edge[:, 0, :], edge[:, 1, :]
                    take(gate_fun)
                    for s in range(2):
                        done(dve.tensor_tensor(level_kq[1][s], edge[:, 0, :], keys[s], ALU.mult))
                    done(dve.tensor_tensor(q1, edge[:, 1, :], q, ALU.mult))
                    for o, src, i, over in ((q2, q1, 2, 1), (q2, q1, 3, 2), (q3, q2, 3, 1)):
                        t = slice(i * P, (i + 1) * P)
                        done(dve.tensor_scalar(o[:, t], src[:, t], small[:, 24 + over:25 + over], None, ALU.mult),
                             level_ready if o is q3 else dve_step)
                    if not b:
                        fill(FILL_START)
                    if b:
                        take(weights_used)

                    def scores(lev):
                        mask = con[:, CCOL["level"] + lev * P:CCOL["level"] + (lev + 1) * P].bitcast(U32)
                        for s in range(2):
                            take(scores_ready)
                            done(dve.copy_predicated(
                                diagonal(s), mask.unsqueeze(1).broadcast_to([P, T, P]),
                                score_ps[:, s, :].rearrange("p (j c) -> p j c", c=P)), scores_used)

                    for lev, half in enumerate(LEVELS):
                        gs = g.rearrange("p (s c) -> p s c", c=2 * half)
                        ds = edge[:, 3, :].rearrange("p (s c) -> p s c", c=2 * half)
                        ref = gs[:, :, half - 1:half].broadcast_to([P, N // (2 * half), half])
                        done(dve.tensor_tensor(ds[:, :, 0:half], ref, gs[:, :, 0:half], ALU.subtract))
                        done(dve.tensor_tensor(ds[:, :, half:], gs[:, :, half:], ref, ALU.subtract), gate_arg)
                        if lev:
                            scores(lev - 1)
                        take(gate_fun)
                        for o, a in zip(level_kq[lev % 2], (*keys, q)):
                            done(dve.tensor_tensor(o, a, edge[:, 2, :], ALU.mult),
                                 level_ready if a is q else dve_step)
                        if lev - 1 in FILL_LEVELS:
                            fill()
                    for o, a in zip(level_kq[1], (*keys, q)):
                        done(dve.tensor_copy(o, a), level_ready if a is q else dve_step)
                    if 6 in FILL_LEVELS:
                        fill()
                    scores(6)
                    scores(7)
                take(weights_used)

            def decay_argument(h):
                done(dve.tensor_scalar(decay, dist[:, 0:7 * P], small[:, 48 + h:49 + h], None, ALU.mult))
                stt(decay, dist[:, 7 * P:14 * P], small[:, 56 + h:57 + h], decay, ALU.mult, ALU.add, gate_arg)

            def retention(h, s):
                if s == 0:
                    take(head_turned)
                    done(dve.tensor_reduce(small[:, 8:12],
                                           turn_ps[:, :, :].rearrange("p b (t c) -> p t b c", c=P),
                                           AX_XY, ALU.add))
                    done(dve.tensor_scalar(small[:, 8:12], small[:, 8:12], -1.0 / G, None, ALU.mult), mean_ready)
                    take(gate_fun)
                    weigh(0)
                    weigh(1)
                    low_weights(0)
                elif s < 3:
                    if s == 1:
                        low_values()
                    weigh(s + 1)
                    low_weights(s)
                elif s == 4:
                    if h + 1 < RH:
                        decay_argument(h + 1)
                elif s == 3:
                    low_weights(3)
                    take(weights_used)
                    take(square_made, 2)
                    done(dve.tensor_tensor(sq[:, 0, :], sq[:, 0, :], sq[:, 1, :], ALU.add), square_added)
                elif s == 5:
                    take(ret_std)
                    done(dve.reciprocal(rstd_r[:, :], rstd_r[:, :]))
                    for c in range(2):
                        stt(tmp[:, c, :], out_ps[:, c, :], p_("gn", 2 * h + c), rstd_r[:, :], ALU.mult, ALU.mult,
                            head_done if c else dve_step)
                    take(proj_ready, 2)
                    for c in range(2):
                        t, b = tmp[:, c, :], 2 * (h % 4) + c
                        done(dve.tensor_tensor(t, t, head_in[h % 2][:, 4 + c, :], ALU.mult))
                        split(t, ret_h[:, b, :], ret_l[:, b, :], rhs_ready)

            def weigh(j):
                take(scores_ready)
                stt(tmp[:, j % 2, :], score_ps[:, j % 2, :], P ** -0.5, decay[:, (3 - j) * P:(7 - j) * P],
                    ALU.mult, ALU.mult, tile_weighted)

            def low_values():
                take(values_high)
                a = turn_ps[:, :, :].rearrange("p b (t c) -> p t b c", c=P)
                for t in range(T):
                    vh, vl = (v[:, t, :].rearrange("p (b c) -> p b c", c=P) for v in values_hl)
                    stt(vl, a[:, t], small[:, 8 + t:9 + t], vh.bitcast(F32), ALU.add, ALU.subtract,
                        values_low if t == T - 1 else dve_step)

            def low_weights(j):
                take(weights_high)
                done(dve.tensor_tensor(ret_w[1][:, j, :], tmp[:, j % 2, :], ret_w[0][:, j, :].bitcast(F32),
                                       ALU.subtract), weights_ready)

            def mlp(name, p):
                h, l = hidden[p % 2]

                def low_part(b):
                    take(hidden_raw)
                    done(dve.tensor_tensor(l[:, b, :], sq[:, b % 2, :], h[:, b, :].bitcast(F32), ALU.subtract),
                         rhs_ready)

                for b in range(FF2_PARTS[p]):
                    n = FIRST[f"{name}up{p}"] + b
                    dve.wait_ge(unit_done, n + 1)
                    stt(tmp[:, b % 2, :], gemm_ps[:, n % 2, :], 0.0, rstd[:, :], ALU.max, ALU.mult, emptied)
                    if b:
                        low_part(b - 1)
                low_part(FF2_PARTS[p] - 1)

            def gated():
                for u in padded:
                    done(dve.memset(u[:, 0:2], 0.0))
                b = 0
                for p in range(len(FF1_PARTS)):
                    for i in range(FF1_PARTS[p]):
                        n, t, u = FIRST[f"fup{p}"] + 2 * i, tmp[:, b % 2, :], padded[b % 2]
                        scaled(n, u[:, 2:N + 2])
                        convolve(t, u, [p_("ffn_conv_w", 22 * k + b) for k in range(3)], conv_ready)
                        take(hidden_raw)
                        dve.wait_ge(unit_done, n + 2)
                        done(dve.tensor_tensor(t, sq[:, b % 2, :], gemm_ps[:, (n + 1) % 2, :], ALU.mult), emptied)
                        done(dve.tensor_tensor(t, t, rstd[:, :], ALU.mult))
                        split(t, hidden[p % 2][0][:, i, :], hidden[p % 2][1][:, i, :], rhs_ready)
                        b += 1
                    if p:
                        store(FIRST[f"fdown{p - 1}"], p == 1)
                store(FIRST["fdown2"], False, squared=True)

            dve.memset(eps[:, 0:1], RMS_EPS)
            dve.memset(eps[:, 1:2], GN_EPS)
            dve.wait_ge(inputs_in, 32)
            meet()
            for b in range(KT):
                low(x, "norm_mix_pre", xh, xl, b)
            inverse()
            scaled(FIRST["in"], gates[0:HD, :], rows=HD)
            hgrn()
            meet()
            mlstm()
            meet()
            dve.wait_ge(memory_in, 16)
            for b in range(KT):
                low(mem_raw, "mem_norm", mem_h, mem_l, b, dve_step, M)
            inverse(mem_rstd)
            mixers_out()
            meet()
            dve.wait_ge(moba_table_in, 16)
            take(values_free)
            for b in range(2):
                part_heads(proj1[:, A_K + b, :], proj1[:, A_V + b, :])

            def memory_scaled(u):
                o = cross_k if u < 4 else cross_vf
                scaled(memory_unit(u), o[:, u % 4, :], width=M, rs=mem_rstd)

            def split_mixer(i):
                if i % 3 == 2 and i // 3 < 6:
                    b = i // 3
                    to, src = ((0, M_O), (1, M_O + 1), (2, C_H), (3, C_H + 1), (6, H_G), (7, H_G + 1))[b]
                    split(proj1[:, src, :], xh[:, to, :], xl[:, to, :])

            def beside(i):
                split_mixer(i)
                if i % 3 == 1 and i // 3 < KV_EARLY:
                    memory_scaled(i // 3)
            attention(attention_items("moba"), beside)
            meet()
            store(FIRST["mix"], True, squared=True)
            inverse()
            for b in range(KT):
                if b < 8 - KV_EARLY:
                    memory_scaled(KV_EARLY + b)
                add_normed("norm_mix_post", "norm_cross_pre", b)
            low(x, "norm_cross_pre", xh, xl, KT - 1)
            inverse()
            for b in range(4):
                scaled(FIRST["cross_q"] + b, cross_q[:, b, :], factor=P ** -0.5)
            meet()
            attention(attention_items("cross"))
            meet()
            for i in range(U_CO):
                n = FIRST["co"] + i
                dve.wait_ge(unit_done, n + 1)
                done(dve.tensor_copy(y[:, 2 * i, :], score_ps[:, n % 2, :]))
                done(dve.tensor_copy(y[:, 2 * i + 1, :], gemm_ps[:, n % 2, :]), emptied)
                add_square(2 * i)
                add_square(2 * i + 1)
            inverse()
            for b in range(KT):
                add_normed("norm_cross_post", "norm_ffn_pre", b)
            low(x, "norm_ffn_pre", xh, xl, KT - 1)
            inverse()
            gated()
            inverse()
            for b in range(KT):
                add_normed("norm_ffn_post", "attn_norm_e_2", b)
            low(x, "attn_norm_e_2", xh, xl, KT - 1)
            inverse()
            for b in range(6):
                scaled(FIRST["even_in"] + b, proj2[:, b, :])
            done(dve.memset(eps[:, 2:3], 0.0), proj_raw)
            sinks = par[:, PCOL["sink"]:PCOL["sink"] + 8]
            done(dve.tensor_scalar(sinks, sinks, -1.0, None, ALU.mult))
            head_norm([proj2[:, E_AQ + b, :] for b in range(5)], [p_("qa", 0)] * 4 + [p_("ka", 0)])
            take(values_free)
            part_heads(proj2[:, E_AK, :], proj2[:, E_AV, :])
            dve.wait_ge(layer_tables_in, 32)

            def neighbour_unit(i):
                if i % 3 == 1 and i // 3 < 12:
                    b = 6 + i // 3
                    scaled(FIRST["even_in"] + b, proj2[:, b, :].rearrange("p (c r) -> p r c", r=8),
                           src=lambda a: a.rearrange("p (r c) -> p r c", r=8))
            attention(attention_items("window"), neighbour_unit, whole=True)
            meet()
            for b in range(4):
                split(y[:, 5 + b, :], xh[:, b, :], xl[:, b, :])
            head_norm([proj2[:, E_BQ + b, :] for b in range(8)], [p_("qb", 0)] * 4 + [p_("kb", 0)] * 4)
            for b in range(4):
                part_heads(proj2[:, E_BK + b, :], proj2[:, E_BV + b, :])
            meet()
            attention(attention_items("neighbour"))
            meet()
            add(FIRST["even_out"], "mlp0", mh, ml)
            inverse()
            mlp("m", 0)
            for p in (1, 2, 3):
                mlp("m", p)
                add(FIRST[f"mdown{p - 1}"])
            add(FIRST["mdown3"], "ret_norm_o_2", xh, xl)
            inverse()
            take(gate_fun)
            dec = par[:, PCOL["dec_f"]:PCOL["dec_f"] + 16]
            done(dve.tensor_scalar(small[:, 16:32], dec, 0.0, None, ALU.min))
            done(dve.tensor_tensor(small[:, 48:64], small[:, 16:32], small[:, 32:48], ALU.subtract))
            dve.wait_ge(distances_in, 16)
            decay_argument(0)
            for h in range(RH):
                for u in range(U_HEAD):
                    scaled(ret_unit(h) + u, head_in[h % 2][:, u, :])
                    if u == 4:
                        take(keys_high)
                        done(dve.tensor_tensor(ret_qk[1], head_in[h % 2][:, 0:2, :], ret_qk[0].bitcast(F32),
                                               ALU.subtract), keys_low)
                    if h:
                        retention(h - 1, u)
                if h == RH // 2:
                    add(FIRST["odd_out0"])
            for s in range(U_HEAD):
                retention(RH - 1, s)
            add(FIRST["odd_out1"], "mlp1", xh, xl)
            inverse()
            mlp("n", 0)
            for p in (1, 2, 3):
                mlp("n", p)
                add(FIRST[f"ndown{p - 1}"])
            add(FIRST["ndown3"])
            meet()


def _blocks(w, nkt=KT, start=0):
    k, m = w.shape
    a = w[start * P:(start + nkt) * P].reshape(nkt, P, m // P, P).transpose(2, 1, 0, 3).reshape(m // P, P, nkt * P)
    return np.pad(a, ((0, 0), (0, 0), (0, KT * P - nkt * P)))


def _stream(inp):
    units = []
    w = inp["w_in"][0]
    cuts = np.cumsum([G] * 4 + [4, 4] + [G] * 10)
    cols = np.split(w, cuts[:-1], axis=1)
    gates = np.zeros((D, P), w.dtype)
    gates[:, 0:4], gates[:, 32:36] = cols[4], cols[5]
    units.append(_blocks(gates))
    units.append(_blocks(np.concatenate([cols[13], cols[14], cols[12], cols[15]] + cols[0:4] + cols[6:12], axis=1)))
    memory = _blocks(np.concatenate([inp["w_ck"][0], inp["w_cv"][0]], 1))
    units += [memory[:KV_EARLY], _blocks(inp["w_mix_out"][0]), memory[KV_EARLY:], _blocks(inp["w_cq"][0])]
    a = _blocks(inp["w_co"][0], 4)[:, :, 0:4 * P].reshape(U_CO, 2, P, 4 * P)
    units.append(a.transpose(0, 2, 1, 3).reshape(U_CO, P, KT * P))

    def parts(sizes, ups, down):
        at = np.concatenate([[0], np.cumsum(sizes)])

        def up(p):
            u = [_blocks(a[:, at[p] * P:at[p + 1] * P]) for a in ups]
            units.append(np.stack(u, 1).reshape(-1, P, KT * P))

        up(0)
        for p in range(len(sizes)):
            if p + 1 < len(sizes):
                up(p + 1)
            units.append(_blocks(down, sizes[p], at[p]))

    f = inp["w_ffn_in"][0]
    parts(FF1_PARTS, [f[:, :FF1], f[:, FF1:]], inp["w_ffn_out"][0])
    pair = np.array([0, 4, 1, 5, 2, 6, 3, 7])
    e = inp["w_in_e_2"][0]
    units.append(_blocks(np.concatenate([e[:, :512].reshape(D, 8, HD)[:, pair].reshape(D, 512), e[:, 512:]], 1)))
    e = inp["w_out_e_2"][0]
    units.append(_blocks(np.concatenate([e[:512].reshape(8, HD, D)[pair].reshape(512, D), e[512:]], 0)))
    parts(FF2_PARTS, [inp["w_mlp_in_2"][0]], inp["w_mlp_out_2"][0])
    o = inp["w_in_o_2"][0]
    q, k, v, g = np.split(o, [D, 2 * D, 4 * D], axis=1)
    for half in range(2):
        heads = []
        for h in ODD_HEADS[half]:
            heads += [q[:, h * P:(h + 1) * P], k[:, h * P:(h + 1) * P], v[:, h * G:(h + 1) * G],
                      g[:, h * G:(h + 1) * G]]
        units.append(_blocks(np.concatenate(heads, 1)))
        units.append(_blocks(inp["w_out_o_2"][0], KT, half * KT))
    parts(FF2_PARTS, [inp["w_mlp_in_2"][1]], inp["w_mlp_out_2"][1])
    out = np.concatenate(units)
    assert out.shape == (UNITS, P, KT * P), out.shape
    return out.reshape(UNITS * P, KT * P)


def _parameters(inp):
    par = np.zeros((P, PARAMS), np.float32)

    def put(name, a):
        par[:, PCOL[name]:PCOL[name] + a.shape[0]] = a.T

    for name in ("norm_mix_pre", "norm_mix_post", "mem_norm", "norm_cross_pre", "norm_cross_post", "norm_ffn_pre",
                 "norm_ffn_post", "attn_norm_e_2", "ret_norm_o_2", "mlstm_norm", "hgrn_norm"):
        put(name, inp[name][0].reshape(-1, P))
    put("mlp0", inp["mlp_norm_2"][0].reshape(-1, P))
    put("mlp1", inp["mlp_norm_2"][1].reshape(-1, P))
    b = inp["b_in"][0]
    put("b_in", np.concatenate([b[:4 * G], b[4 * G + 8:]]).reshape(-1, P))
    par[0:4, PCOL["b_gates"]] = b[4 * G:4 * G + 4]
    par[32:36, PCOL["b_gates"]] = b[4 * G + 4:4 * G + 8]
    put("hgrn_lb", inp["hgrn_lb_logits"][0].reshape(-1, P))
    put("sconv_w", inp["sconv_w"][0].reshape(-1, P))
    put("ffn_conv_w", inp["ffn_conv_w"][0].reshape(-1, P))
    put("ffn_conv_b", inp["ffn_conv_b"][0].reshape(-1, P))
    for name, src in (("qa", "q_norm_a_2"), ("ka", "k_norm_a_2"), ("qb", "q_norm_b_2"), ("kb", "k_norm_b_2")):
        put(name, np.tile(inp[src][0], 2).reshape(1, P))
    sink = inp["sink_a_2"][0][[0, 4, 1, 5, 2, 6, 3, 7]]
    put("sink", np.broadcast_to(sink[:, None], (8, P)))
    put("dec_f", np.broadcast_to(inp["decay_fwd_o_2"][0][:, None], (8, P)))
    put("dec_b", np.broadcast_to(inp["decay_bwd_o_2"][0][:, None], (8, P)))
    put("gn", inp["ret_gn_o_2"][0].reshape(-1, P))
    return par


def _moba_bias(rel_bias):
    dist = np.arange(P)[:, None] + 3 * P - np.arange(N)[None, :]
    n = np.maximum(dist, 0)
    large = 16 + (np.log(np.maximum(n, 1).astype(np.float32) / np.float32(16)) / np.float32(np.log(8.0))
                  * np.float32(16)).astype(np.int32)
    bucket = np.where(n < 16, n, np.minimum(large, 31))
    out = np.where((dist >= 0)[:, :, None], rel_bias[bucket], np.float32(NEG))
    return np.ascontiguousarray(out.transpose(0, 2, 1)).reshape(P, 4 * N)


def _na_bias(rpb):
    q = np.arange(P)
    out = []
    for t, lo, hi in ((0, 0, 2), (1, 0, 3), (3, 2, 4)):
        k = np.arange(lo * P, hi * P)
        qc, qr, kc, kr = 16 * t + q // 8, q % 8, k // 8, k % 8
        start = np.clip(qc - 8, 0, 48)
        valid = (kc[None] >= start[:, None]) & (kc[None] < start[:, None] + 16)
        col = np.clip(kc[None] - qc[:, None] + 15, 0, 30)
        row = kr[None] - qr[:, None] + 7
        out.append(np.where(valid[None], rpb[:, row, col], np.float32(NEG)).transpose(1, 0, 2).reshape(P, -1))
    return np.concatenate(out, 1)


def _feature_major(a):
    return np.ascontiguousarray(a.T.reshape(KT, P, -1).transpose(1, 0, 2)).reshape(P, -1)


def kernel(**inputs):
    import concourse.bacc as bacc
    from concourse.bass_utils import run_bass_kernel_spmd

    inp = {k: np.asarray(v) for k, v in inputs.items()}
    arrays = {
        "x_in": _feature_major(inp["x"][0]),
        "mem_in": _feature_major(inp["mem"][0]),
        "w_in": _stream(inp),
        "par_in": _parameters(inp),
        "con_in": _constants(),
        "moba_in": _moba_bias(inp["rel_bias"]),
        "alibi_in": _alibi(),
        "na_in": _na_bias(inp["rpb_b_2"][0]),
        "dist_in": _distances(),
    }
    nc = bacc.Bacc("TRN2", target_bir_lowering=False, num_devices=1)
    args = [nc.dram_tensor(k, a.shape, F32, kind="ExternalInput").ap() for k, a in arrays.items()]
    out = nc.dram_tensor("out", (P, KT * N), F32, kind="ExternalOutput").ap()
    args[0] = args[0].rearrange("p (b n) -> p b n", n=N)
    build(nc, *args, out.rearrange("p (b n) -> p b n", n=N))
    got = run_bass_kernel_spmd(nc, [arrays], core_ids=[0]).results[0]["out"]
    return np.ascontiguousarray(got.reshape(P, KT, N).transpose(2, 1, 0)).reshape(1, N, D)
```
